# Optimizing a Trainium2 kernel written in Bass

```python
import math
import jax, jax.numpy as jnp
from jax import lax
import numpy as np

D_MODEL = 1024
BATCH = 1
SEQ = 1024
DEPTH = 1
DEC_BATCH = 8
DEC_SEQ = 1
PAST_LEN = 8192
PAGE_SIZE = 128

MIX_WIDTH = D_MODEL
ML_HEADS = 4
ML_WIDTH = MIX_WIDTH // 2
ML_DK = ML_WIDTH // ML_HEADS
ML_DV = ML_DK
ML_CHUNK = 128
CONV_WIDTH = 4
HG_HEADS = 4
HG_WIDTH = MIX_WIDTH - ML_WIDTH
HG_DK = HG_WIDTH // HG_HEADS
HG_DV = HG_DK
HG_CHUNK = 64
ML_COLS = 4 * ML_WIDTH + 2 * ML_HEADS
HG_COLS = 4 * HG_WIDTH
IN_COLS = ML_COLS + HG_COLS
N_GROUPS = 4
EXPERTS_PER_GROUP = 4
N_EXPERTS = N_GROUPS * EXPERTS_PER_GROUP
TOP_K_IN_GROUP = 2
EXPERT_FF = D_MODEL // 4
DEEPNORM_ALPHA = (2 * DEPTH) ** 0.25
DEEPNORM_BETA = (8 * DEPTH) ** -0.25
LN_EPS = 1e-5
RMS_EPS = 1e-6

kernel_name = "hymba_mlstm_hgrn2_hmoe_step"

F32 = jnp.float32

def _layer_norm(x, g, b):
    xf = x.astype(F32)
    mu = jnp.mean(xf, -1, keepdims=True)
    var = jnp.mean(jnp.square(xf - mu), -1, keepdims=True)
    return ((xf - mu) * lax.rsqrt(var + LN_EPS) * g.astype(F32) + b.astype(F32)).astype(x.dtype)

def _head_rms(h, g):
    H, Dh = h.shape[1], h.shape[3]
    h = h * lax.rsqrt(jnp.mean(jnp.square(h), -1, keepdims=True) + RMS_EPS)
    return h * g.astype(F32).reshape(1, H, 1, Dh)

def _to_heads(t, n_heads):
    B, T, _ = t.shape
    return t.reshape(B, T, n_heads, -1).transpose(0, 2, 1, 3)

def _from_heads(t):
    B, H, T, Dh = t.shape
    return t.transpose(0, 2, 1, 3).reshape(B, T, H * Dh)

def _to_chunks(t, L):
    B, H, T = t.shape[:3]
    return jnp.moveaxis(t.reshape(B, H, T // L, L, *t.shape[3:]), 2, 0)

def _from_chunks(t):
    t = jnp.moveaxis(t, 0, 2)
    return t.reshape(t.shape[0], t.shape[1], -1, *t.shape[4:])

def _mlstm_chunk_step(carry, xs):
    C, n, m = carry
    q, k, v, li, lf = xs
    L = q.shape[2]
    F = jnp.cumsum(lf, axis=2)
    a = li - F
    m_t = F + jnp.maximum(m[..., None], lax.cummax(a, axis=2))
    causal = jnp.tril(jnp.ones((L, L), dtype=bool))
    log_d = (F - m_t)[..., :, None] + a[..., None, :]
    dmat = jnp.exp(jnp.where(causal, log_d, -jnp.inf))
    s = jnp.einsum('bhtd,bhsd->bhts', q, k) * dmat
    dec = jnp.exp(F + m[..., None] - m_t)
    num = jnp.einsum('bhts,bhsv->bhtv', s, v) + dec[..., None] * jnp.einsum('bhtd,bhdv->bhtv', q, C)
    qn = jnp.sum(s, -1) + dec * jnp.einsum('bhtd,bhd->bht', q, n)
    h = num / jnp.maximum(jnp.abs(qn), jnp.exp(-m_t))[..., None]
    F_end = F[..., -1]
    m_end = m_t[..., -1]
    w_end = jnp.exp(F_end[..., None] + a - m_end[..., None])
    dec_end = jnp.exp(F_end + m - m_end)
    C_new = dec_end[..., None, None] * C + jnp.einsum('bhs,bhsd,bhsv->bhdv', w_end, k, v)
    n_new = dec_end[..., None] * n + jnp.einsum('bhs,bhsd->bhd', w_end, k)
    return (C_new, n_new, m_end), h

def _mlstm(q, k, v, li, lf, C0, n0, m0):
    L = min(ML_CHUNK, q.shape[2])
    xs = tuple(_to_chunks(t, L) for t in (q, k, v, li, lf))
    (C, n, m), h = lax.scan(_mlstm_chunk_step, (C0, n0, m0), xs)
    return _from_chunks(h), C, n, m

def _hgrn2_chunk_step(S, xs):
    q, k, i, lf = xs
    L = q.shape[2]
    G = jnp.cumsum(lf, axis=2)
    causal = jnp.tril(jnp.ones((L, L), dtype=bool))[:, :, None]
    gap = G[:, :, :, None, :] - G[:, :, None, :, :]
    decay = jnp.exp(jnp.where(causal, gap, -jnp.inf))
    A = jnp.einsum('bhtc,bhtsc,bhsc->bhts', q, decay, k)
    o = jnp.einsum('bhts,bhsv->bhtv', A, i) + jnp.einsum('bhtc,bhcv->bhtv', q * jnp.exp(G), S)
    G_end = G[:, :, -1:, :]
    S_new = jnp.exp(G_end[:, :, 0, :])[..., None] * S + jnp.einsum('bhsc,bhsv->bhcv', k * jnp.exp(G_end - G), i)
    return S_new, o

def _hgrn2(q, k, i, lf, S0):
    L = min(HG_CHUNK, q.shape[2])
    xs = tuple(_to_chunks(t, L) for t in (q, k, i, lf))
    S, o = lax.scan(_hgrn2_chunk_step, S0, xs)
    return _from_chunks(o), S

def _mixer(x, conv_buf, C0, n0, m0, S0, w_in, b_in, conv_w, conv_b, ml_g, lb, hg_g, w_out):
    B, T, _ = x.shape
    z = (jnp.einsum('btd,de->bte', x, w_in) + b_in).astype(F32)
    ml, hg = z[..., :ML_COLS], z[..., ML_COLS:]
    qk_raw = ml[..., :2 * ML_WIDTH]
    v_ml = ml[..., 2 * ML_WIDTH:3 * ML_WIDTH]
    o_ml = ml[..., 3 * ML_WIDTH:4 * ML_WIDTH]
    i_pre = ml[..., 4 * ML_WIDTH:4 * ML_WIDTH + ML_HEADS]
    f_pre = ml[..., 4 * ML_WIDTH + ML_HEADS:]
    xp = jnp.concatenate([conv_buf.astype(F32), qk_raw], axis=1)
    new_buf = xp[:, T:]
    cw = conv_w.astype(F32)
    qk = conv_b.astype(F32) + xp[:, 0:T] * cw[0]
    for j in range(1, CONV_WIDTH):
        qk = qk + xp[:, j:j + T] * cw[j]
    qk = jax.nn.silu(qk)
    q = _to_heads(qk[..., :ML_WIDTH], ML_HEADS)
    k = _to_heads(qk[..., ML_WIDTH:], ML_HEADS) * (ML_DK ** -0.5)
    v = _to_heads(v_ml, ML_HEADS)
    li = i_pre.transpose(0, 2, 1)
    lf = jax.nn.log_sigmoid(f_pre).transpose(0, 2, 1)
    h, C, n, m = _mlstm(q, k, v, li, lf, C0.astype(F32), n0.astype(F32), m0.astype(F32))
    h = _head_rms(jax.nn.sigmoid(_to_heads(o_ml, ML_HEADS)) * h, ml_g)
    hq, hf, hi, hgt = jnp.split(hg, 4, axis=-1)
    lb = lb.astype(F32)
    lf_h = jnp.logaddexp(jnp.log(lb), jnp.log1p(-lb) + jax.nn.log_sigmoid(hf))
    k_h = (1.0 - lb) * jax.nn.sigmoid(-hf)
    o_h, S = _hgrn2(_to_heads(jax.nn.silu(hq), HG_HEADS), _to_heads(k_h, HG_HEADS),
                    _to_heads(hi, HG_HEADS), _to_heads(lf_h, HG_HEADS), S0.astype(F32))
    o_h = _head_rms(o_h, hg_g) * jax.nn.silu(_to_heads(hgt, HG_HEADS))
    mixed = jnp.concatenate([_from_heads(h), _from_heads(o_h)], axis=-1).astype(x.dtype)
    out = jnp.einsum('bte,ed->btd', mixed, w_out)
    return out, new_buf, C, n, m, S

def _hmoe(x, w_rg, b_rg, w_re, b_re, w1, w3, w2):
    B, T, D = x.shape
    xt = x.reshape(B * T, D)
    lg = (xt @ w_rg + b_rg).astype(F32)
    pg = jax.nn.softmax(lg, axis=-1)
    g = jnp.argmax(lg, axis=-1)
    le = (xt @ w_re + b_re).astype(F32).reshape(-1, N_GROUPS, EXPERTS_PER_GROUP)
    le_g = jnp.take_along_axis(le, g[:, None, None], axis=1)[:, 0]
    top_v, top_i = lax.top_k(le_g, TOP_K_IN_GROUP)
    wts = jax.nn.softmax(top_v, axis=-1) * jnp.take_along_axis(pg, g[:, None], axis=1)
    eid = g[:, None] * EXPERTS_PER_GROUP + top_i
    gate = jnp.einsum('nk,nke->ne', wts, jax.nn.one_hot(eid, N_EXPERTS, dtype=F32))
    a = jnp.einsum('nd,edf->nef', xt, w1)
    u = jnp.einsum('nd,edf->nef', xt, w3)
    hdn = jax.nn.silu(a) * u * gate[..., None].astype(x.dtype)
    return jnp.einsum('nef,efd->nd', hdn, w2).reshape(B, T, D)

def _layer(x, conv_buf, C, n, m, S, w_in, b_in, conv_w, conv_b, ml_g, lb, hg_g, w_out,
           ln1_g, ln1_b, w_rg, b_rg, w_re, b_re, w1, w3, w2, ln2_g, ln2_b):
    mix, conv_buf, C, n, m, S = _mixer(x, conv_buf, C, n, m, S, w_in, b_in, conv_w, conv_b,
                                       ml_g, lb, hg_g, w_out)
    x = _layer_norm(DEEPNORM_ALPHA * x + mix, ln1_g, ln1_b)
    x = _layer_norm(DEEPNORM_ALPHA * x + _hmoe(x, w_rg, b_rg, w_re, b_re, w1, w3, w2), ln2_g, ln2_b)
    return x, conv_buf, C, n, m, S

def setup_inputs(seed: int = 0) -> dict:
    key = jax.random.key(seed)
    ks = iter(jax.random.split(key, 32))

    def nrm(shape, scale):
        return scale * jax.random.normal(next(ks), shape, F32)

    col_scale = np.ones((IN_COLS,), np.float32)
    col_scale[2 * ML_WIDTH:3 * ML_WIDTH] = DEEPNORM_BETA
    col_scale[ML_COLS + 2 * HG_WIDTH:ML_COLS + 3 * HG_WIDTH] = DEEPNORM_BETA
    f_bias = np.zeros((IN_COLS,), np.float32)
    f_bias[4 * ML_WIDTH + ML_HEADS:ML_COLS] = np.linspace(3.0, 6.0, ML_HEADS)
    return {
        "x_prompt": nrm((BATCH, SEQ, D_MODEL), 1.0),
        "x_sample": nrm((DEC_BATCH, DEC_SEQ, D_MODEL), 1.0),
        "state_conv": nrm((DEPTH, DEC_BATCH, CONV_WIDTH - 1, 2 * ML_WIDTH), 1.0),
        "state_ml_C": nrm((DEPTH, DEC_BATCH, ML_HEADS, ML_DK, ML_DV), 0.3),
        "state_ml_n": nrm((DEPTH, DEC_BATCH, ML_HEADS, ML_DK), 0.3),
        "state_ml_m": nrm((DEPTH, DEC_BATCH, ML_HEADS), 1.0),
        "state_hg_S": nrm((DEPTH, DEC_BATCH, HG_HEADS, HG_DK, HG_DV), 0.5),
        "w_in": nrm((DEPTH, D_MODEL, IN_COLS), D_MODEL ** -0.5) * jnp.asarray(col_scale),
        "b_in": nrm((DEPTH, IN_COLS), 0.02) + jnp.asarray(f_bias),
        "conv_w": nrm((DEPTH, CONV_WIDTH, 2 * ML_WIDTH), CONV_WIDTH ** -0.5),
        "conv_b": nrm((DEPTH, 2 * ML_WIDTH), 0.02),
        "ml_norm_g": 1.0 + nrm((DEPTH, ML_WIDTH), 0.02),
        "hg_lower_bounds": nrm((DEPTH, HG_WIDTH), 0.5),
        "hg_norm_g": 1.0 + nrm((DEPTH, HG_WIDTH), 0.02),
        "w_out": nrm((DEPTH, MIX_WIDTH, D_MODEL), MIX_WIDTH ** -0.5 * DEEPNORM_BETA),
        "ln1_g": 1.0 + nrm((DEPTH, D_MODEL), 0.02),
        "ln1_b": nrm((DEPTH, D_MODEL), 0.02),
        "w_router_group": nrm((DEPTH, D_MODEL, N_GROUPS), D_MODEL ** -0.5),
        "b_router_group": nrm((DEPTH, N_GROUPS), 0.01),
        "w_router_expert": nrm((DEPTH, D_MODEL, N_EXPERTS), D_MODEL ** -0.5),
        "b_router_expert": nrm((DEPTH, N_EXPERTS), 0.01),
        "w_gate": nrm((DEPTH, N_EXPERTS, D_MODEL, EXPERT_FF), D_MODEL ** -0.5),
        "w_up": nrm((DEPTH, N_EXPERTS, D_MODEL, EXPERT_FF), D_MODEL ** -0.5 * DEEPNORM_BETA),
        "w_down": nrm((DEPTH, N_EXPERTS, EXPERT_FF, D_MODEL), EXPERT_FF ** -0.5 * DEEPNORM_BETA),
        "ln2_g": 1.0 + nrm((DEPTH, D_MODEL), 0.02),
        "ln2_b": nrm((DEPTH, D_MODEL), 0.02),
    }

def reference(x_prompt, x_sample, state_conv, state_ml_C, state_ml_n, state_ml_m, state_hg_S,
              w_in, b_in, conv_w, conv_b, ml_norm_g, hg_lower_bounds, hg_norm_g, w_out, ln1_g, ln1_b,
              w_router_group, b_router_group, w_router_expert, b_router_expert,
              w_gate, w_up, w_down, ln2_g, ln2_b):
    sm = jax.nn.softmax(hg_lower_bounds.astype(F32), axis=0)
    lbs = jnp.concatenate([jnp.zeros_like(sm[:1]), jnp.cumsum(sm[1:], axis=0)], axis=0)
    B = x_prompt.shape[0]
    y_p, y_s = x_prompt, x_sample
    st_p, st_s = [], []
    for l in range(DEPTH):
        p = (w_in[l], b_in[l], conv_w[l], conv_b[l], ml_norm_g[l], lbs[l], hg_norm_g[l], w_out[l],
             ln1_g[l], ln1_b[l], w_router_group[l], b_router_group[l], w_router_expert[l],
             b_router_expert[l], w_gate[l], w_up[l], w_down[l], ln2_g[l], ln2_b[l])
        zc = jnp.zeros((B, CONV_WIDTH - 1, 2 * ML_WIDTH), F32)
        zC = jnp.zeros((B, ML_HEADS, ML_DK, ML_DV), F32)
        zn = jnp.zeros((B, ML_HEADS, ML_DK), F32)
        zm = jnp.zeros((B, ML_HEADS), F32)
        zS = jnp.zeros((B, HG_HEADS, HG_DK, HG_DV), F32)
        y_p, *sp = _layer(y_p, zc, zC, zn, zm, zS, *p)
        y_s, *ss = _layer(y_s, state_conv[l], state_ml_C[l], state_ml_n[l], state_ml_m[l], state_hg_S[l], *p)
        st_p.append(sp)
        st_s.append(ss)

    def stack(states, idx, dtype):
        return jnp.stack([s[idx] for s in states]).astype(dtype)

    conv_p = stack(st_p, 0, state_conv.dtype)
    C_p = stack(st_p, 1, state_ml_C.dtype)
    n_p = stack(st_p, 2, state_ml_n.dtype)
    m_p = stack(st_p, 3, state_ml_m.dtype)
    S_p = stack(st_p, 4, state_hg_S.dtype)
    conv_s = stack(st_s, 0, state_conv.dtype)
    C_s = stack(st_s, 1, state_ml_C.dtype)
    n_s = stack(st_s, 2, state_ml_n.dtype)
    m_s = stack(st_s, 3, state_ml_m.dtype)
    S_s = stack(st_s, 4, state_hg_S.dtype)
    return (y_p, y_s, conv_p, C_p, n_p, m_p, S_p, conv_s, C_s, n_s, m_s, S_s)


_drawn_inputs = setup_inputs


def setup_inputs(seed=0):
    import zlib

    import numpy as np

    out = dict(_drawn_inputs(seed))
    spreads = {}
    factors = {'ml_norm_g': 6.706,
     'hg_norm_g': 22.159,
     'ln1_g': 2.717,
     'ln1_b': 2.749,
     'b_router_group': 8.0,
     'b_router_expert': 27.713,
     'ln2_g': 7.9,
     'ln2_b': 7.906}
    for name, (base, spread) in spreads.items():
        noise = np.random.default_rng([zlib.crc32(name.encode()), seed]).standard_normal(out[name].shape)
        drawn = base * np.exp(spread * noise) if base else spread * noise
        out[name] = __import__('jax').numpy.asarray(drawn.astype(out[name].dtype))
    for name, factor in factors.items():
        out[name] = (out[name] * factor).astype(out[name].dtype)
    return out
```

```python
from contextlib import ExitStack

import numpy as np

import concourse.bass as bass
from concourse import mybir

F32 = mybir.dt.float32
I32 = mybir.dt.int32
U32 = mybir.dt.uint32
U8 = mybir.dt.uint8
ALU = mybir.AluOpType
ACT = mybir.ActivationFunctionType
X = mybir.AxisListType.X

P = 128
D = 1024
NP_, NS = 1024, 8
NT = NP_ + NS
KD = D // P
NCH = NP_ // P
H = 4
DV1 = P + 1
PIECE = NT // 3
HB = H * NS
LEVELS = [64, 32, 16, 8, 4, 2, 1]
NLEV = len(LEVELS)
NTT = NCH + 1
NG, NJ = 4, 4
NE = NG * NJ
FF = 256
TILES = (2 * NT + NE * (P - 1)) // P
ALPHA = 2 ** 0.25
LN_EPS, RMS_EPS = 1e-5, 1e-6
KSCALE = P ** -0.5
N_PARAMS = 8
BIG = 1e30
SMALL = 904

COL_Q, COL_K, COL_V, COL_O = 0, 512, 1024, 1536
COL_HG = 4 * 512 + 2 * H
COL_HQ, COL_HF, COL_HI, COL_GT = COL_HG, COL_HG + 512, COL_HG + 1024, COL_HG + 1536

CONST = {}


def constants():
    i = np.arange(P)
    c = {
        "ident": np.eye(P),
        "ones": np.ones((P, P)),
        "causal": (i[:, None] <= i[None, :]),
        "before": (i[:, None] < i[None, :]),
        "lane": np.broadcast_to(i[None, :], (P, P)),
        "token": np.where(i[:, None] + P * np.arange(NTT)[None] < NT, i[:, None] + P * np.arange(NTT)[None], 0),
        "valid": (i[:, None] + P * np.arange(NTT)[None] < NT),
        "first": np.broadcast_to(np.array([4, 3, 2, 1]), (P, 4)),
        "full": np.broadcast_to(P * np.arange(NTT), (P, NTT)),
        "eps": np.broadcast_to(np.array([1.0, RMS_EPS, LN_EPS, 0.0]), (P, 4)),
    }
    cols, at = [], 0
    for name, a in c.items():
        a = np.asarray(a, np.float32).reshape(P, -1)
        CONST[name] = (at, at + a.shape[1])
        at += a.shape[1]
        cols.append(a)
    masks = []
    for b in LEVELS:
        blk, first = i // (2 * b), (i // b) % 2 == 0
        masks.append((blk[:, None] == blk[None, :]) & first[:, None] & ~first[None, :])
    masks.append(np.eye(P, dtype=bool))
    masks = np.stack(masks, 1).astype(np.float32).reshape(P, -1)
    sel = ((i[:, None, None] == np.arange(H)[None, :, None]) * np.ones((P, H, P), np.float32)).reshape(P, -1)
    return np.ascontiguousarray(np.concatenate(cols, 1)), np.concatenate([masks, sel], 1)


CONST_F, CONST_M = constants()


def program(nc, t):
    with ExitStack() as ctx:
        _program(nc, t, ctx)


def _program(nc, t, ctx):
    def sb(name, shape, dt=F32):
        return ctx.enter_context(nc.sbuf_tensor(name, shape, dt))

    cst = sb("constants", [P, CONST_F.shape[1]])
    msk = sb("level_masks", [P, NLEV + 1, P], U8)
    xT = sb("x_cm", [P, KD, NT])
    W = sb("weight_slots", [P, 3, KD, 512])
    CC = sb("conv_qk", [P, 8, NP_])
    G = sb("hg_decay", [P, H, NT])
    Q = sb("hg_q", [P, H, NT])
    K = sb("hg_k", [P, H, NT])
    SC = sb("scratch", [P, 9728])
    R = sb("router", [P, 384])
    SM = sb("small", [P, SMALL])
    PS = ctx.enter_context(nc.psum_tensor("psum", [P, 8, 512], F32))

    def const(name):
        a, b = CONST[name]
        return cst[:, a:b]

    ident, ones = const("ident"), const("ones")
    one_col, rms_eps, ln_eps = (cst[:, CONST["eps"][0] + n:CONST["eps"][0] + n + 1] for n in range(3))

    at = [0]

    def small(n):
        at[0] += n
        assert at[0] <= SMALL
        return SM[:, at[0] - n:at[0]]

    cw = small(32).rearrange("p (c j) -> p c j", c=8)
    cb = small(8)
    b_cm = small(32)
    bg = small(1)
    g_mix = small(8)
    sconv = small(8 * 3 * NS).rearrange("p (c j b) -> p c j b", c=8, j=3)
    raw_s = small(8 * NS).rearrange("p (c b) -> p c b", c=8)
    raw_p3 = small(24).rearrange("p (c j) -> p c j", c=8)
    conv_ps = small(64)
    mend = small(NCH + 1)
    mprev = small(H * (NCH + 1)).rearrange("p (h c) -> p h c", h=H)
    m0 = small(NS)
    gs_rows = small(3 * NS)
    gs = small(H * 3 * NS).rearrange("p (h g b) -> p h g b", h=H, g=3)
    zs = small(16 * NS).rearrange("p (e b) -> p e b", e=16)
    den, rec, ssq, rstd, dend = (small(H) for _ in range(5))
    ms_row = small(NS)

    raw = [SC[:, 0:3 + NT], SC[:, 1036:1036 + 3 + NT]]
    cacc = SC[:, 2072:2072 + NP_]
    g3 = SC[:, 3100:3100 + NP_]
    CF = CC[:, :, :].rearrange("p a b -> p (a b)")
    grow = CF[:, 0:NT]
    fr, lnr = CF[0:H, NT:2 * NT], CF[0:H, 2 * NT:3 * NT]
    keep, drop, Frow, cmx = (CF[0:H, 3100 + n * NP_:3100 + (n + 1) * NP_] for n in range(4))
    buf = lambda n: SC[:, n * 512:(n + 1) * 512].rearrange("p (h t) -> p h t", h=H)
    dmat, qd, kw, hbuf, sq = (buf(n) for n in range(5))
    vext = [SC[:, 2560 + n * 516:2560 + (n + 1) * 516].rearrange("p (h v) -> p h v", h=H) for n in range(2)]
    ogate = SC[:, 3592:4104].rearrange("p (h t) -> p h t", h=H)
    Cst = SC[:, 4104:4620].rearrange("p (h v) -> p h v", h=H)
    negM = SC[0:H, 4620:5644]
    gcol = SC[:, 5644:6412].rearrange("p (c r) -> p c r", c=NCH)
    bias = SC[:, 6656:7680]

    xlev = [buf(0), buf(1)]
    amat, hmix, qdec, kend, ibuf, gtb = (buf(n) for n in (2, 3, 4, 5, 6, 7))
    Sst = buf(8)
    xrow = SC[:, 4608:5632]
    xTt = SC[:, 5632:6656].rearrange("p (k t) -> p k t", k=KD)
    ln_gb = SC[:, 7680:9728].rearrange("p (g n) -> p g n", g=2)
    w_out = W[:, 1:3].rearrange("p s a b -> p (s a b)").rearrange("p (e n) -> p e n", e=8)
    w_r = R[:, 0:160].rearrange("p (k e) -> p k e", k=KD)
    b_r = R[:, 160:180]
    LG = R[:, 180:360].rearrange("p (i e) -> p i e", i=NTT)
    stats = R[:, 360:372].rearrange("p (g n) -> p g n", g=2)
    mv = R[:, 372:374]
    lstd = R[:, 374:375]
    egend = R[:, 376:380]
    mixS = small(8 * NS).rearrange("p (e b) -> p e b", e=8)
    XF = xT[:, :, :].rearrange("p k t -> p (k t)")
    C0 = XF[:, 0:4096].rearrange("p (e v) -> p e v", e=HB)
    vdiag = XF[0:HB, 4096:8192].rearrange("p (e v) -> p e v", e=HB)
    S0 = W[:, 0].rearrange("p k n -> p (k n)").rearrange("p (e v) -> p e v", e=HB)
    n0 = small(HB)
    T = [SC[:, n * HB:(n + 1) * HB] for n in range(32)]
    by_hb = lambda ap: ap.rearrange("p (h b) -> p h b", h=H)
    x1_dram = nc.dram_tensor("x1_rows", (NT, D), F32).ap()
    flatf = lambda tile: tile[:, :, :].rearrange("p a b -> p (a b)")
    KF, GF, QF = flatf(K), flatf(G), flatf(Q)
    wslots = [flatf(CC), W[:, 1:3].rearrange("p s a b -> p (s a b)")]
    w_gu = [w[:, 0:4096].rearrange("p (k g f) -> p k g f", k=KD, g=2) for w in wslots]
    w_dn = [w[:, 4096:6144].rearrange("p (k n) -> p k n", k=2) for w in wslots]
    xg = [SC[:, n * D:(n + 1) * D] for n in range(2)]
    xgT = [SC[:, (2 + n) * D:(3 + n) * D].rearrange("p (k t) -> p k t", k=KD) for n in range(2)]
    ysb = [SC[:, (4 + n) * D:(5 + n) * D] for n in range(2)]
    silu, hid = SC[:, 6144:6400], SC[:, 6400:6656]
    hidT = SC[:, 6656:6912].rearrange("p (k t) -> p k t", k=2)
    gate_c = [SC[:, 6914 + n:6915 + n] for n in range(2)]
    y_slots = nc.dram_tensor("y_slots", (TILES * P, D), F32).ap()
    oh_lo = KF[:, 0:18 * P].rearrange("p (q n) -> p q n", q=18)
    oh_hi = QF[:, 0:18 * 64].rearrange("p (q w n) -> p q w n", q=18, w=2)
    kat = [18 * P]

    def route_tile(n):
        kat[0] += n
        assert kat[0] <= 4128
        return KF[:, kat[0] - n:kat[0]]

    slot_tok = route_tile(TILES).bitcast(I32)
    slot_gate = route_tile(TILES)
    tile_expert = route_tile(TILES)
    pos = route_tile(2 * NTT)
    pos_i = route_tile(2 * NTT).bitcast(I32)
    hi_i, lo_i = (route_tile(2 * NTT).bitcast(I32) for _ in range(2))
    hi_f, lo_f = (route_tile(2 * NTT) for _ in range(2))
    wts = route_tile(2 * NTT).rearrange("p (w i) -> p w i", w=2)
    gat = [0]

    def work(*shape):
        n = int(np.prod(shape))
        gat[0] += n
        assert gat[0] <= 4128
        ap = GF[:, gat[0] - n:gat[0]]
        if len(shape) == 2:
            return ap.rearrange("p (a b) -> p a b", b=shape[1])
        if len(shape) == 3:
            return ap.rearrange("p (a b c) -> p a b c", b=shape[1], c=shape[2])
        return ap

    gmax, gden, v1, v2, e2, s2 = (work(NTT) for _ in range(6))
    gexp, ghot, scr, leg, leg2 = (work(NTT, 4) for _ in range(5))
    hot = [work(NTT, 4) for _ in range(2)]
    ex = [work(NTT, NE) for _ in range(2)]
    esum, tot, slotp = (work(NTT, NE) for _ in range(3))
    le_m = work(NTT, 4, 4)
    cnt = work(NTT, NE)
    n_e, nt_e, end_e, base_e = (work(NE) for _ in range(4))
    cmp9 = work(NE, NTT)
    cmp32 = work(TILES, NE)
    x1_keep = [XF[:, c * D:(c + 1) * D] for c in range(8)] + [SC[:, 8 * D:9 * D]]
    ya = [GF[:, n * D:(n + 1) * D] for n in range(4)]
    yb = [QF[:, n * D:(n + 1) * D] for n in range(4)]
    ln2_gb = wslots[0][:, 6144:8192].rearrange("p (g n) -> p g n", g=2)
    fst, fmv, fsd = (small(n) for n in (12, 2, 1))
    class Semaphores:
        pass

    s = Semaphores()

    def sem(name):
        return ctx.enter_context(nc.semaphore(name))

    s.consts_in = sem("consts_in")
    s.params_in = sem("params_in")
    s.xT_in = sem("xT_in")
    s.xT_in2 = sem("xT_in2")
    s.bias_in = sem("bias_in")
    s.w_in0 = sem("w_in0")
    s.w_in1 = sem("w_in1")
    s.w_in2 = sem("w_in2")
    s.w_in3 = sem("w_in3")
    s.w_in4 = sem("w_in4")
    s.w_in5 = sem("w_in5")
    s.w_in6 = sem("w_in6")
    s.w_in7 = sem("w_in7")
    s.dve_step = sem("dve_step")
    s.act_step = sem("act_step")
    s.pool_step = sem("pool_step")
    s.projected = sem("projected")
    s.proj_read = sem("proj_read")
    s.gates_z = sem("gates_z")
    s.forget_ln = sem("forget_ln")
    s.gate_rows = sem("gate_rows")
    s.gates_spread = sem("gates_spread")
    s.gates_read = sem("gates_read")
    s.hf_ln = sem("hf_ln")
    s.k_arg = sem("k_arg")
    s.hg_k_ready = sem("hg_k_ready")
    s.conv_done = sem("conv_done")
    s.qk_silu = sem("qk_silu")
    s.hq_silu = sem("hq_silu")
    s.decay_b = sem("decay_b")
    s.scores = sem("scores")
    s.k_turned = sem("k_turned")
    s.num = sem("num")
    s.cupd = sem("cupd")
    s.h_turned = sem("h_turned")
    s.h_turned_read = sem("h_turned_read")
    s.d_arg = sem("d_arg")
    s.q_arg = sem("q_arg")
    s.d_exp = sem("d_exp")
    s.q_exp = sem("q_exp")
    s.d_masked = sem("d_masked")
    s.kw_ready = sem("kw_ready")
    s.s_ready = sem("s_ready")
    s.qd_ready = sem("qd_ready")
    s.v_proj = sem("v_proj")
    s.o_proj = sem("o_proj")
    s.v_ready = sem("v_ready")
    s.o_biased = sem("o_biased")
    s.o_exp = sem("o_exp")
    s.h_ready = sem("h_ready")
    s.h_sq = sem("h_sq")
    s.ssq_ready = sem("ssq_ready")
    s.rstd_ready = sem("rstd_ready")
    s.hn_ready = sem("hn_ready")
    s.c_ready = sem("c_ready")
    s.zs_proj = sem("zs_proj")
    s.zs_read = sem("zs_read")
    s.outputs = sem("outputs")
    s.masks_made = sem("masks_made")
    s.dots = sem("dots")
    s.dots_in = sem("dots_in")
    s.down_done = sem("down_done")
    s.esum_ready = sem("esum_ready")
    s.g_exp = sem("g_exp")
    s.gate_ready = sem("gate_ready")
    s.gt_biased = sem("gt_biased")
    s.gt_exp = sem("gt_exp")
    s.gt_proj = sem("gt_proj")
    s.hgs_ready = sem("hgs_ready")
    s.hidT_ready = sem("hidT_ready")
    s.hid_ready = sem("hid_ready")
    s.hid_turned = sem("hid_turned")
    s.i_proj = sem("i_proj")
    s.i_ready = sem("i_ready")
    s.kend_arg = sem("kend_arg")
    s.kend_exp = sem("kend_exp")
    s.kend_ready = sem("kend_ready")
    s.kend_tm = sem("kend_tm")
    s.kend_turned = sem("kend_turned")
    s.kv_in = sem("kv_in")
    s.kv_turned = sem("kv_turned")
    s.level_arg = sem("level_arg")
    s.level_exp = sem("level_exp")
    s.level_kept = sem("level_kept")
    s.level_scaled = sem("level_scaled")
    s.levels = sem("levels")
    s.ln2_in = sem("ln2_in")
    s.logits_read = sem("logits_read")
    s.lstd_ready = sem("lstd_ready")
    s.mixS_ready = sem("mixS_ready")
    s.mixed = sem("mixed")
    s.mixer_in = sem("mixer_in")
    s.moments = sem("moments")
    s.normed = sem("normed")
    s.o_copied = sem("o_copied")
    s.o_num = sem("o_num")
    s.o_sq = sem("o_sq")
    s.o_turned = sem("o_turned")
    s.o_turned_read = sem("o_turned_read")
    s.ogate_arg = sem("ogate_arg")
    s.ogate_exp = sem("ogate_exp")
    s.on_ready = sem("on_ready")
    s.onehots = sem("onehots")
    s.orstd_ready = sem("orstd_ready")
    s.ossq_ready = sem("ossq_ready")
    s.outer = sem("outer")
    s.qd_free = sem("qd_free")
    s.qg_ready = sem("qg_ready")
    s.ranked = sem("ranked")
    s.residual = sem("residual")
    s.route_arg = sem("route_arg")
    s.route_exp = sem("route_exp")
    s.routed = sem("routed")
    s.s_upd = sem("s_upd")
    s.sgates_arg = sem("sgates_arg")
    s.sgates_exp = sem("sgates_exp")
    s.silu_ready = sem("silu_ready")
    s.slots = sem("slots")
    s.sq_in = sem("sq_in")
    s.sq_sum = sem("sq_sum")
    s.srstd = sem("srstd")
    s.state_in = sem("state_in")
    s.state_read = sem("state_read")
    s.tiles_known = sem("tiles_known")
    s.up_done = sem("up_done")
    s.vdiag_ready = sem("vdiag_ready")
    s.w_dn_in0 = sem("w_dn_in0")
    s.w_dn_in1 = sem("w_dn_in1")
    s.w_gu_in0 = sem("w_gu_in0")
    s.w_gu_in1 = sem("w_gu_in1")
    s.wout_scaled = sem("wout_scaled")
    s.x1_back = sem("x1_back")
    s.x1_ready = sem("x1_ready")
    s.x1_turned = sem("x1_turned")
    s.x1_turned_read = sem("x1_turned_read")
    s.x1_written = sem("x1_written")
    s.x_in = sem("x_in")
    s.xgT_ready = sem("xgT_ready")
    s.xg_in0 = sem("xg_in0")
    s.xg_in1 = sem("xg_in1")
    s.xg_turned = sem("xg_turned")
    s.y_added = sem("y_added")
    s.y_out0 = sem("y_out0")
    s.y_out1 = sem("y_out1")
    s.y_read = sem("y_read")
    s.y_ready = sem("y_ready")
    s.yg_in0 = sem("yg_in0")
    s.yg_in1 = sem("yg_in1")
    s.yg_in2 = sem("yg_in2")
    s.yg_in3 = sem("yg_in3")
    s.zs2_proj = sem("zs2_proj")
    outs = [0]

    def out_dma(eng, dst, src):
        eng.dma_start(dst, src).then_inc(s.outputs, 16)
        outs[0] += 1

    def chain(eng, sem):
        n = [0]

        def link(ins):
            n[0] += 1
            ins.then_inc(sem, 1)
            eng.wait_ge(sem, n[0])
        return link

    def teller(eng):
        told = {}

        def tell(ins, sem):
            told[sem] = told.get(sem, 0) + 1
            ins.then_inc(sem, 1)
            eng.wait_ge(sem, told[sem])
        return tell

    w_cols = t["w_in"].rearrange("(p k) e -> p k e", k=KD)
    GROUPS = [(COL_HF, 0), (COL_HQ, 1), (COL_Q, 2), (COL_K, 0), (COL_V, 1), (COL_O, 2), (COL_GT, 0), (COL_HI, 3)]
    slot3 = CC[:, 4:8, :].rearrange("p a (b e) -> p (a b) e", b=2)
    w_slot = lambda g: slot3 if GROUPS[g][1] == 3 else W[:, GROUPS[g][1]]
    w_sem = [s.w_in0, s.w_in1, s.w_in2, s.w_in3, s.w_in4, s.w_in5, s.w_in6, s.w_in7]
    PIECES = 3 * 17
    last_piece = lambda unit: 3 * (unit + 2)
    mask_words = SC[:, 7680:7680 + (NLEV + 1) * P]
    sel = SC[:, 8704:8704 + H * P].rearrange("p (h m) -> p h m", h=H)
    wgt = SC[:, 4200:4200 + KD * 64].rearrange("p (k e) -> p k e", k=KD)

    def x_rows(c):
        return P if c < NCH else NS

    def sync_rest(sp):
        sp.wait_ge(s.qk_silu, 9)
        sp.wait_ge(s.cupd, NCH)
        sp.wait_ge(s.h_turned_read, NCH)
        sp.wait_ge(s.zs_proj, 1)
        sp.wait_ge(s.masks_made, 1)
        sp.dma_start(w_slot(7), w_cols[:, :, COL_HI:COL_HI + 512]).then_inc(s.w_in7, 16)
        sp.wait_ge(s.o_biased, NCH)
        sp.dma_start(bias, t["b_row"][:, 1024:2048].partition_broadcast(P).rearrange("p a n -> p (a n)")).then_inc(s.mixer_in, 16)
        sp.dma_start(w_out, t["w_out"].rearrange("(e p) n -> p e n", p=P)).then_inc(s.mixer_in, 16)
        sp.dma_start(ln_gb, t["ln1"].partition_broadcast(P)).then_inc(s.mixer_in, 16)
        sp.dma_start(w_r, t["w_r"]).then_inc(s.mixer_in, 16)
        sp.dma_start(b_r, t["b_r"].partition_broadcast(P).rearrange("p a n -> p (a n)")).then_inc(s.mixer_in, 16)
        sp.dma_start(by_hb(n0), t["n0"]).then_inc(s.mixer_in, 16)
        for c in range(NTT):
            if c == 0:
                sp.wait_ge(s.c_ready, NCH)
                sp.wait_ge(s.outputs, 16 * outs[0])
            else:
                sp.wait_ge(s.x1_turned, c)
                sp.wait_ge(s.x1_written, 16 * c)
            r = x_rows(c)
            sp.dma_start(xrow[0:r], t["x"][c * P:c * P + r]).then_inc(s.x_in, 16)
            if c == NCH - 1:
                sp.wait_ge(s.zs2_proj, 1)
                sp.dma_start(C0, t["C0"].rearrange("p h b v -> p (h b) v")).then_inc(s.state_in, 16)
                sp.dma_start(S0, t["S0"].rearrange("p h b v -> p (h b) v")).then_inc(s.state_in, 16)
                sp.wait_ge(s.hgs_ready, NCH)
                out_dma(sp, t["out_S_p"], Sst)
            if c == NCH:
                sp.wait_ge(s.state_read, 8)
                out_dma(sp, t["out_C_s"].rearrange("p h b v -> p (h b) v"), C0)
                out_dma(sp, t["out_n_s"].rearrange("p h b -> p (h b)"), T[20])
                out_dma(sp, t["out_m_s"].rearrange("h b -> (h b)").unsqueeze(0), T[21][0:1])
                sp.wait_ge(s.state_read, 16)
                out_dma(sp, t["out_S_s"].rearrange("p h b v -> p (h b) v"), S0)
            sp.wait_ge(s.x1_ready, c + 1)
            sp.dma_start(x1_dram[c * P:c * P + r], xrow[0:r]).then_inc(s.x1_written, 16)
        sync_moe(sp)

    def tensor_rest(pe, tokens_product):
        mm = nc.tensor.matmul
        hp = lambda bank, h: PS[:, bank, h * P:(h + 1) * P]
        pe.wait_ge(s.hg_k_ready, H)
        pe.wait_ge(s.hq_silu, H)

        def out_project(c, lhs_of):
            r = x_rows(c)
            for n in range(2):
                for e in range(8):
                    i = mm(PS[0:r, 6 + n, :], lhs_of(e), w_out[:, e, n * 512:(n + 1) * 512], start=(e == 0), stop=(e == 7))
            i.then_inc(s.mixed, 1)

        def turn_and_route(c):
            r = x_rows(c)
            pe.wait_ge(s.x1_ready, c + 1)
            for k in range(KD):
                i = nc.tensor.transpose(PS[:, k // 4, (k % 4) * P:(k % 4) * P + r], xrow[0:r, k * P:(k + 1) * P], ident[0:r, 0:r])
            i.then_inc(s.x1_turned, 1)
            pe.wait_ge(s.x1_turned_read, c + 1)
            pe.wait_ge(s.mixer_in, 16 * 6)
            if c >= 1:
                pe.wait_ge(s.logits_read, c)
            for k in range(KD):
                i = mm(PS[0:r, 3, 0:NG + NE], xTt[:, k, 0:r], w_r[:, k, :], start=(k == 0), stop=(k == KD - 1))
            i.then_inc(s.routed, 1)

        for c in range(NCH + 2):
            tok = slice(c * P, (c + 1) * P)
            if c < NCH:
                for l in range(NLEV + 1):
                    n = (NLEV + 1) * c + l
                    if n == 0:
                        pe.wait_ge(s.h_turned_read, NCH)
                    elif n == 1:
                        pe.wait_ge(s.s_ready, NCH)
                    else:
                        pe.wait_ge(s.level_kept, n - 1)
                    if l == 1 and c >= 3:
                        pe.wait_ge(s.logits_read, c - 2)
                    if l < NLEV:
                        xl = xlev[(NLEV * c + l) % 2]
                        pe.wait_ge(s.level_scaled, 2 * (NLEV * c + l + 1))
                    for h in range(H):
                        if l < NLEV:
                            i = mm(hp(2 + n % 2, h), xl[:, h], xl[:, h], start=True, stop=True)
                        else:
                            i = mm(hp(2 + n % 2, h), K[:, h, tok], Q[:, h, tok], start=True, stop=True)
                    i.then_inc(s.levels, 1)
                pe.wait_ge(s.kend_ready, c + 1)
                if c == 0:
                    pe.wait_ge(s.h_ready, NCH)
                else:
                    pe.wait_ge(s.hgs_ready, c)
                for h in range(H):
                    i = nc.tensor.transpose(hp(5, h), kend[:, h], ident)
                i.then_inc(s.kend_turned, 1)
                if c == 0:
                    pe.wait_ge(s.w_in7, 16)
                    pe.wait_ge(s.w_in6, 16)
                    pe.wait_ge(s.zs_read, 1)
                else:
                    pe.wait_ge(s.i_ready, c)
                    pe.wait_ge(s.gt_biased, c)
                    if c >= 3:
                        pe.wait_ge(s.x1_turned_read, c - 2)
                tokens_product(0, 7, c, s.i_proj)
                tokens_product(1, 6, c, s.gt_proj)
                if c == NCH - 1:
                    pe.wait_ge(s.residual, c - 1)
                    for e in range(8):
                        for k in range(KD):
                            i = mm(PS[:, 6, e * NS:(e + 1) * NS], w_slot(7 - e // 4)[:, k, (e % 4) * P:(e % 4 + 1) * P],
                                   xT[:, k, NP_:NT], start=(k == 0), stop=(k == KD - 1))
                    i.then_inc(s.zs2_proj, 1)
            if 1 <= c <= NCH:
                pe.wait_ge(s.on_ready, c)
                for h in range(H):
                    i = nc.tensor.transpose(hp(4, h), hmix[:, h], ident)
                i.then_inc(s.o_turned, 1)
            if c < NCH:
                pe.wait_ge(s.level_kept, (NLEV + 1) * (c + 1))
                pe.wait_ge(s.qg_ready, c + 1)
                pe.wait_ge(s.i_ready, c + 1)
                if c >= 1:
                    pe.wait_ge(s.o_turned_read, c)
                for h in range(H):
                    i = mm(hp(4, h), amat[:, h], ibuf[:, h], start=True, stop=(c == 0))
                    if c >= 1:
                        i = mm(hp(4, h), qdec[:, h], Sst[:, h], start=False, stop=True)
                i.then_inc(s.o_num, 1)
                pe.wait_ge(s.kend_tm, c + 1)
                for h in range(H):
                    i = mm(hp(5, h), kend[:, h], ibuf[:, h], start=True, stop=True)
                i.then_inc(s.s_upd, 1)
            if 1 <= c <= NCH:
                if c == 1:
                    pe.wait_ge(s.wout_scaled, 8)
                    pe.wait_ge(s.c_ready, NCH)
                else:
                    pe.wait_ge(s.residual, c - 1)
                if c == NCH - 1:
                    pe.wait_ge(s.zs_read, 2)
                pe.wait_ge(s.o_turned_read, c)
                last = slice((c - 1) * P, c * P)
                out_project(c - 1, lambda e: CC[:, e, last] if e < 4 else Q[:, e - 4, last])
            if c >= 2:
                if c < NCH:
                    pe.wait_ge(s.i_ready, c + 1)
                    pe.wait_ge(s.gt_biased, c + 1)
                    pe.wait_ge(s.level_kept, (NLEV + 1) * (c + 1))
                turn_and_route(c - 2)

        for kind in range(2):
            state = (C0, S0)[kind]
            if kind == 0:
                pe.wait_ge(s.x1_turned_read, NCH)
                pe.wait_ge(s.o_turned_read, NCH)
            else:
                pe.wait_ge(s.srstd, 1)
            pe.wait_ge(s.state_in, 32)
            pe.wait_ge(s.dots_in, kind + 1)
            n = 2 - kind
            mm(PS[:, 0, 0:n * HB], ones, SC[:, 0:n * HB], start=True, stop=True)
            for e in range(HB):
                q = conv_ps[:, e:e + 1] if kind == 0 else T[2][:, e:e + 1]
                i = mm(PS[:, 0, 2 * HB + e:2 * HB + e + 1], state[:, e, :], q, start=True, stop=True)
            i.then_inc(s.dots, 1)
            pe.wait_ge(s.kv_in, kind + 1)
            nc.tensor.transpose(PS[0:HB, 1, 0:P], T[3], ident)
            i = nc.tensor.transpose(PS[0:HB, 1, P:2 * P], T[4], ident)
            i.then_inc(s.kv_turned, 1)
            pe.wait_ge(s.sq_in, kind + 1)
            mm(PS[:, 0, 96:128], ones, T[5], start=True, stop=True).then_inc(s.sq_sum, 1)
            pe.wait_ge(s.vdiag_ready, kind + 1)
            for n in range(8):
                bank = 2 + n % 4
                if n >= 4:
                    pe.wait_ge(s.state_read, 8 * kind + n - 3)
                i = mm(PS[:, bank, :], SC[0:HB, 24 * HB:24 * HB + P], vdiag[:, 4 * n:4 * n + 4, :].rearrange("p a v -> p (a v)"),
                       start=True, stop=True)
                i.then_inc(s.outer, 1)
        pe.wait_ge(s.mixS_ready, 1)
        pe.wait_ge(s.residual, NCH)
        out_project(NCH, lambda e: mixS[:, e, :])
        turn_and_route(NCH)
        tensor_moe(pe)

    def scalar_rest(act, link, tell):
        A = nc.scalar.activation
        by_h = lambda ap: ap.rearrange("p (h t) -> p h t", h=H)

        def rms_scale(c, sem, done):
            act.wait_ge(sem, c)
            link(A(rstd, ssq, ACT.Ln, scale=1.0 / P, bias=rms_eps))
            tell(A(rstd, rstd, ACT.Exp, scale=-0.5), done)

        def ln_scale(c):
            r = x_rows(c)
            act.wait_ge(s.moments, c + 1)
            link(A(lstd[0:r], mv[0:r, 1:2], ACT.Ln, bias=ln_eps[0:r]))
            tell(A(lstd[0:r], lstd[0:r], ACT.Exp, scale=-0.5), s.lstd_ready)

        def x1_evacuate(c):
            r = x_rows(c)
            act.wait_ge(s.x1_turned, c + 1)
            if c >= 1:
                act.wait_ge(s.routed, c)
            for n in range(2):
                i = A(xTt[:, 4 * n:4 * n + 4, 0:r], by_h(PS[:, n, :])[:, :, 0:r], ACT.Copy)
                if n == 0:
                    link(i)
            tell(i, s.x1_turned_read)

        for c in range(NCH + 2):
            tok = slice(c * P, (c + 1) * P)
            if c < NCH:
                act.wait_ge(s.qd_free, c + 1)
                tell(A(qdec, G[:, :, tok], ACT.Exp), s.g_exp)
                act.wait_ge(s.kend_arg, c + 1)
                tell(A(kend, kend, ACT.Exp), s.kend_exp)
                for l in range(NLEV):
                    act.wait_ge(s.level_arg, NLEV * c + l + 1)
                    xl = xlev[(NLEV * c + l) % 2]
                    tell(A(xl, xl, ACT.Exp), s.level_exp)
            if 1 <= c <= NCH:
                act.wait_ge(s.o_turned, c)
                tell(A(Q[:, :, (c - 1) * P:c * P], by_h(PS[:, 4, :]), ACT.Copy), s.o_turned_read)
            if c < NCH:
                act.wait_ge(s.gt_biased, c + 1)
                tell(A(xlev[0], gtb, ACT.Exp, scale=-1.0), s.gt_exp)
                rms_scale(c + 1, s.ossq_ready, s.orstd_ready)
            if 1 <= c <= NCH:
                ln_scale(c - 1)
            if c >= 2:
                x1_evacuate(c - 2)
        act.wait_ge(s.sgates_arg, 1)
        tell(A(SC[:, 8 * HB:11 * HB], SC[:, 8 * HB:11 * HB], ACT.Exp), s.sgates_exp)
        for kind in range(2):
            act.wait_ge(s.ogate_arg, kind + 1)
            tell(A(T[11], T[12], ACT.Exp, scale=-1.0), s.ogate_exp)
            act.wait_ge(s.sq_sum, kind + 1)
            link(A(T[13], PS[:, 0, 96:128], ACT.Ln, scale=1.0 / P, bias=rms_eps))
            tell(A(T[13], T[13], ACT.Exp, scale=-0.5), s.srstd)
            if kind == 0:
                act.wait_ge(s.sgates_arg, 2)
                tell(A(T[14], T[14], ACT.Exp), s.sgates_exp)
        ln_scale(NCH)
        x1_evacuate(NCH)
        scalar_moe(act, link, tell)

    def pool_rest(pool, link, tell):
        g = nc.gpsimd
        pool.wait_ge(s.mixer_in, 16 * 6)
        pool.wait_ge(s.params_in, 16 * N_PARAMS)
        pool.wait_ge(s.mixer_in, 16 * 6)
        for e in range(8):
            tell(g.tensor_scalar(w_out[:, e, :], w_out[:, e, :], g_mix[:, e:e + 1], None, ALU.mult), s.wout_scaled)

        def ln_affine(c):
            r = x_rows(c)
            pool.wait_ge(s.normed, c + 1)
            link(g.tensor_tensor(xrow[0:r], xrow[0:r], ln_gb[0:r, 0], ALU.mult))
            tell(g.tensor_tensor(xrow[0:r], xrow[0:r], ln_gb[0:r, 1], ALU.add), s.x1_ready)

        for c in range(NCH + 1):
            if c < NCH:
                pool.wait_ge(s.kend_exp, c + 1)
                tell(g.tensor_tensor(kend, kend, K[:, :, c * P:(c + 1) * P], ALU.mult), s.kend_ready)
                for l, b in enumerate(LEVELS):
                    n = NLEV * c + l
                    pool.wait_ge(s.level_exp, n + 1)
                    for half, src in ((0, K), (1, Q)):
                        x = xlev[n % 2].rearrange("p h (n w b) -> p h n w b", w=2, b=b)[:, :, :, half]
                        y = src[:, :, c * P:(c + 1) * P].rearrange("p h (n w b) -> p h n w b", w=2, b=b)[:, :, :, half]
                        tell(g.tensor_tensor(x, x, y, ALU.mult), s.level_scaled)
                pool.wait_ge(s.o_copied, c + 1)
                tell(g.tensor_tensor(xlev[1], hmix, hmix, ALU.mult), s.o_sq)
            if c >= 1:
                ln_affine(c - 1)
        ln_affine(NCH)
        pool_moe(pool, link, tell)

    def vector_rest(dve, link, tell):
        v = nc.vector
        by_h = lambda ap: ap.rearrange("p (h t) -> p h t", h=H)
        link(v.memset(R[:, 180:360], 0.0))
        dve.wait_ge(s.h_turned, NCH)
        dve.wait_ge(s.masks_made, 1)

        def residual_norm(c):
            r = x_rows(c)
            dve.wait_ge(s.mixed, c + 1)
            dve.wait_ge(s.x_in, 16 * (c + 1))
            for n in range(2):
                half = xrow[0:r, n * 512:(n + 1) * 512]
                i = v.scalar_tensor_tensor(half, half, ALPHA, PS[0:r, 6 + n, :], ALU.mult, ALU.add)
            tell(i, s.residual)
            for n in range(2):
                i = v.bn_stats(stats[0:r, n], xrow[0:r, n * 512:(n + 1) * 512])
            link(i)
            tell(v.bn_aggr(mv[0:r], stats[0:r]), s.moments)
            dve.wait_ge(s.lstd_ready, c + 1)
            tell(v.tensor_scalar(xrow[0:r], xrow[0:r], mv[0:r, 0:1], lstd[0:r], ALU.subtract, ALU.mult), s.normed)

        def logits(c):
            r = x_rows(c)
            dve.wait_ge(s.routed, c + 1)
            dve.wait_ge(s.mixer_in, 16 * 6)
            tell(v.tensor_tensor(LG[0:r, c], PS[0:r, 3, 0:NG + NE], b_r[0:r], ALU.add), s.logits_read)

        def sample_state(kind, state, decay):
            link(v.tensor_tensor(state, state, decay.unsqueeze(2).to_broadcast([P, HB, P]), ALU.mult))
            for n in range(8):
                dve.wait_ge(s.outer, 8 * kind + n + 1)
                part = state[:, 4 * n:4 * n + 4, :]
                tell(v.tensor_tensor(part, part, by_h(PS[:, 2 + n % 4, :]), ALU.add), s.state_read)

        for c in range(NCH + 2):
            tok = slice(c * P, (c + 1) * P)
            if c < NCH:
                g_end = G[:, :, c * P + P - 1:(c + 1) * P]
                if c >= 1:
                    dve.wait_ge(s.o_num, c)
                    dve.wait_ge(s.s_upd, c)
                tell(v.memset(amat, 0.0), s.qd_free)
                tell(v.tensor_tensor(kend, g_end.to_broadcast([P, H, P]), G[:, :, tok], ALU.subtract), s.kend_arg)

                def keep_level(l):
                    n = (NLEV + 1) * c + l
                    dve.wait_ge(s.levels, n + 1)
                    tell(v.copy_predicated(amat, msk[:, l:l + 1, :].to_broadcast([P, H, P]), by_h(PS[:, 2 + n % 2, :])), s.level_kept)

                for l, b in enumerate(LEVELS):
                    n = NLEV * c + l
                    if n >= 2:
                        dve.wait_ge(s.levels, (NLEV + 1) * ((n - 2) // NLEV) + (n - 2) % NLEV + 1)
                    gv = G[:, :, tok].rearrange("p h (n w b) -> p h n w b", w=2, b=b)
                    xv = xlev[n % 2].rearrange("p h (n w b) -> p h n w b", w=2, b=b)
                    ref = gv[:, :, :, 0, b - 1:b].to_broadcast([P, H, P // (2 * b), b])
                    v.tensor_tensor(xv[:, :, :, 0], ref, gv[:, :, :, 0], ALU.subtract)
                    tell(v.tensor_tensor(xv[:, :, :, 1], gv[:, :, :, 1], ref, ALU.subtract), s.level_arg)
                    if l >= 2:
                        keep_level(l - 2)
                dve.wait_ge(s.g_exp, c + 1)
                link(v.tensor_copy(egend, qdec[:, :, P - 1]))
                tell(v.tensor_tensor(qdec, qdec, Q[:, :, tok], ALU.mult), s.qg_ready)
                for l in range(NLEV - 2, NLEV + 1):
                    keep_level(l)
                dve.wait_ge(s.kend_turned, c + 1)
                tell(v.tensor_copy(kend, by_h(PS[:, 5, :])), s.kend_tm)
                if c == 0:
                    dve.wait_ge(s.mixer_in, 16 * 6)
                dve.wait_ge(s.i_proj, c + 1)
                tell(v.tensor_tensor(ibuf, by_h(PS[:, 0, :]), by_h(bias[:, 0:512]), ALU.add), s.i_ready)
                dve.wait_ge(s.gt_proj, c + 1)
                tell(v.tensor_tensor(gtb, by_h(PS[:, 1, :]), by_h(bias[:, 512:1024]), ALU.add), s.gt_biased)
                dve.wait_ge(s.gt_exp, c + 1)
                link(v.tensor_scalar(xlev[0], xlev[0], 1.0, None, ALU.add))
                link(v.reciprocal(xlev[0], xlev[0]))
                link(v.tensor_tensor(gtb, gtb, xlev[0], ALU.mult))
                if c == NCH - 1:
                    dve.wait_ge(s.zs2_proj, 1)
                    tell(v.tensor_tensor(zs[:, 8:16], PS[:, 6, 0:64].rearrange("p (e b) -> p e b", e=8),
                                         b_cm[:, 24:32].unsqueeze(2).to_broadcast([P, 8, NS]), ALU.add), s.zs_read)
                dve.wait_ge(s.o_num, c + 1)
                tell(v.tensor_copy(hmix, by_h(PS[:, 4, :])), s.o_copied)
                dve.wait_ge(s.s_upd, c + 1)
                for h in range(H):
                    ps = PS[:, 5, h * P:(h + 1) * P]
                    if c == 0:
                        i = v.tensor_copy(Sst[:, h], ps)
                    else:
                        i = v.scalar_tensor_tensor(Sst[:, h], Sst[:, h], egend[:, h:h + 1], ps, ALU.mult, ALU.add)
                tell(i, s.hgs_ready)
                dve.wait_ge(s.o_sq, c + 1)
                tell(v.tensor_reduce(ssq, xlev[1], X, ALU.add), s.ossq_ready)
                dve.wait_ge(s.orstd_ready, c + 1)
                link(v.tensor_tensor(hmix, hmix, rstd.unsqueeze(2).to_broadcast([P, H, P]), ALU.mult))
                tell(v.tensor_tensor(hmix, hmix, gtb, ALU.mult), s.on_ready)
            if 1 <= c <= NCH:
                residual_norm(c - 1)
            if c >= 2:
                logits(c - 2)

        dve.wait_ge(s.mixer_in, 16 * 6)
        dve.wait_ge(s.zs_read, 2)
        a, dd, dec, nm = T[7], T[8], T[9], T[10]
        hb = by_hb
        li, lf, mb = gs[:, :, 0], gs[:, :, 1], gs[:, :, 2]
        link(v.tensor_tensor(hb(a), li, lf, ALU.subtract))
        link(v.tensor_tensor(hb(T[6]), hb(a), mb, ALU.max))
        link(v.tensor_tensor(dd, a, T[6], ALU.subtract))
        link(v.tensor_tensor(hb(dec), mb, hb(T[6]), ALU.subtract))
        link(v.tensor_tensor(hb(T[21]), hb(T[6]), lf, ALU.add))
        tell(v.tensor_scalar(nm, T[21], -1.0, None, ALU.mult), s.sgates_arg)
        qs, ks = conv_ps[:, 0:HB], conv_ps[:, HB:2 * HB]
        flat = lambda ap: ap.rearrange("p h b -> p (h b)")
        for kind in range(2):
            state = (C0, S0)[kind]
            if kind == 0:
                link(v.tensor_tensor(T[0], qs, ks, ALU.mult))
                tell(v.tensor_tensor(T[1], qs, n0, ALU.mult), s.dots_in)
                dve.wait_ge(s.sgates_exp, 1)
                link(v.tensor_scalar(dd, dd, KSCALE, None, ALU.mult))
                link(v.tensor_tensor(T[3], ks, dd, ALU.mult))
                tell(v.tensor_copy(T[4], flat(zs[:, 0:4])), s.kv_in)
                link(v.tensor_tensor(T[20], n0, dec, ALU.mult))
                link(v.tensor_tensor(T[20], T[20], T[3], ALU.add))
                tell(v.tensor_copy(T[12], flat(zs[:, 4:8])), s.ogate_arg)
                dve.wait_ge(s.dots, 1)
                link(v.tensor_tensor(T[15], PS[:, 0, 0:HB], dd, ALU.mult))
                link(v.tensor_tensor(T[16], PS[:, 0, HB:2 * HB], dec, ALU.mult))
                link(v.tensor_tensor(T[16], T[16], T[15], ALU.add))
                link(v.tensor_scalar(T[17], T[16], -1.0, None, ALU.mult))
                link(v.tensor_tensor(T[16], T[16], T[17], ALU.max))
                link(v.tensor_tensor(T[16], T[16], nm, ALU.max))
                link(v.reciprocal(T[16], T[16]))
                link(v.tensor_tensor(T[17], PS[:, 0, 2 * HB:3 * HB], dec, ALU.mult))
                link(v.tensor_tensor(T[15], T[15], T[4], ALU.mult))
                link(v.tensor_tensor(T[15], T[15], T[17], ALU.add))
                link(v.tensor_tensor(T[15], T[15], T[16], ALU.mult))
                dve.wait_ge(s.ogate_exp, 1)
                link(v.tensor_scalar(T[11], T[11], 1.0, None, ALU.add))
                link(v.reciprocal(T[11], T[11]))
                link(v.tensor_tensor(T[15], T[15], T[11], ALU.mult))
                decay = dec
            else:
                kS, qS = K[:, :, NP_:NT], Q[:, :, NP_:NT]
                dve.wait_ge(s.outer, 8)
                tell(v.tensor_copy(hb(T[14]), G[:, :, NP_:NT]), s.sgates_arg)
                link(v.tensor_tensor(hb(T[0]), qS, kS, ALU.mult))
                dve.wait_ge(s.sgates_exp, 2)
                tell(v.tensor_tensor(hb(T[2]), qS, hb(T[14]), ALU.mult), s.dots_in)
                link(v.tensor_copy(hb(T[3]), kS))
                tell(v.tensor_copy(T[4], flat(zs[:, 8:12])), s.kv_in)
                tell(v.tensor_copy(T[12], flat(zs[:, 12:16])), s.ogate_arg)
                dve.wait_ge(s.dots, 2)
                link(v.tensor_tensor(T[15], PS[:, 0, 0:HB], T[4], ALU.mult))
                link(v.tensor_tensor(T[15], T[15], PS[:, 0, 2 * HB:3 * HB], ALU.add))
                dve.wait_ge(s.ogate_exp, 2)
                link(v.tensor_scalar(T[11], T[11], 1.0, None, ALU.add))
                link(v.reciprocal(T[11], T[11]))
                link(v.tensor_tensor(T[11], T[11], T[12], ALU.mult))
                decay = T[14]
            tell(v.tensor_tensor(T[5], T[15], T[15], ALU.mult), s.sq_in)
            dve.wait_ge(s.kv_turned, kind + 1)
            link(v.tensor_copy(SC[0:HB, 24 * HB:24 * HB + P], PS[0:HB, 1, 0:P]))
            tell(v.tensor_tensor(vdiag, PS[0:HB, 1, P:2 * P].unsqueeze(1).to_broadcast([HB, HB, P]),
                                 ident[0:HB, 0:HB].unsqueeze(2).to_broadcast([HB, HB, P]), ALU.mult), s.vdiag_ready)
            dve.wait_ge(s.srstd, kind + 1)
            mix = flat(mixS[:, 4 * kind:4 * kind + 4])
            i = v.tensor_tensor(mix, T[15], T[13], ALU.mult)
            if kind == 0:
                link(i)
            else:
                link(i)
                tell(v.tensor_tensor(mix, mix, T[11], ALU.mult), s.mixS_ready)
            sample_state(kind, state, decay)
        residual_norm(NCH)
        logits(NCH)
        vector_moe(dve, link, tell)

    def pairs_loop(eng, step):
        for i in range(2):
            step(0, i, True, False)
        with eng.Fori(1, TILES // 2 - 1) as pair:
            for i in range(2):
                step(pair, i, False, False)
        for i in range(2):
            step(TILES // 2 - 1, i, False, True)

    early_outs = []

    def sync_moe(sp):
        early_outs.append(outs[0])
        sp.wait_ge(s.outputs, 16 * early_outs[0])
        sp.wait_ge(s.x1_written, 16 * NTT)
        sp.dma_start(XF[:, 0:8 * D].rearrange("p (c n) -> p c n", c=8),
                     x1_dram[0:NP_].rearrange("(c p) n -> p c n", p=P)).then_inc(s.x1_back, 16)
        sp.dma_start(x1_keep[8][0:NS], x1_dram[NP_:NT]).then_inc(s.x1_back, 16)
        sp.wait_ge(s.mixed, NTT)
        sp.wait_ge(s.tiles_known, 1)
        sp.dma_start(ln2_gb, t["ln2"].partition_broadcast(P)).then_inc(s.ln2_in, 16)
        wg = t["w_gate"].rearrange("e (p k) f -> e p k f", k=KD)
        wu = t["w_up"].rearrange("e (p k) f -> e p k f", k=KD)
        wd = t["w_down"].rearrange("e (p k) n -> e p k n", k=2)

        def load_up(pair, i, expert):
            for n, w in enumerate((wg, wu)):
                sp.dma_start(w_gu[i][:, :, n], w[bass.ds(expert, 1)].rearrange("e p k f -> p (e k) f")).then_inc((s.w_gu_in0, s.w_gu_in1)[i], 16)

        def load_down(pair, i, expert):
            sp.dma_start(w_dn[i], wd[bass.ds(expert, 1)].rearrange("e p k n -> p (e k) n")).then_inc((s.w_dn_in0, s.w_dn_in1)[i], 16)

        def expert_of(pair, i):
            return sp.value_load(tile_expert[0:1, bass.ds(pair * 2 + i, 1)].bitcast(I32), min_val=0, max_val=NE - 1)

        for i in range(2):
            e = expert_of(0, i)
            load_up(0, i, e)
            load_down(0, i, e)

        def step(pair, i, first, last):
            done = pair * 2 + (i + 1)
            if not last:
                e = expert_of(pair + 1, i)
                sp.wait_ge(s.up_done, done)
                load_up(pair + 1, i, e)
                sp.wait_ge(s.down_done, done)
                load_down(pair + 1, i, e)
            sp.wait_ge(s.y_read, done * 2)
            sp.dma_start(y_slots[bass.ds((pair * 2 + i) * P, P)], ysb[i]).then_inc((s.y_out0, s.y_out1)[i], 16)

        pairs_loop(sp, step)
        for c in range(NTT):
            r = x_rows(c)
            sp.wait_ge(s.y_ready, c + 1)
            out_dma(sp, t["out_y"][c * P:c * P + r], x1_keep[c][0:r])
        sp.wait_ge(s.outputs, 16 * outs[0])

    def tensor_moe(pe):
        mm = nc.tensor.matmul
        pe.wait_ge(s.esum_ready, 1)
        pe.wait_ge(s.x1_turned_read, NTT)
        mm(PS[:, 0, 0:NTT * NE], const("before"), esum.rearrange("p i e -> p (i e)"), start=True, stop=True)
        mm(PS[:, 1, 0:NTT * NE], ones, esum.rearrange("p i e -> p (i e)"), start=True, stop=True).then_inc(s.ranked, 1)
        pe.wait_ge(s.onehots, 1)
        for q in range(2 * NTT):
            i = mm(PS[:, 2, 0:64], oh_lo[:, q], oh_hi[:, q].rearrange("p w n -> p (w n)"), start=(q == 0), stop=(q == 2 * NTT - 1))
        i.then_inc(s.slots, 1)

        def turn_x(pair, i):
            pe.wait_ge((s.xg_in0, s.xg_in1)[i], pair * 16 + 16)
            for k in range(KD):
                m = nc.tensor.transpose(PS[:, k // 4, (k % 4) * P:(k % 4 + 1) * P], xg[i][:, k:D:KD], ident)
            m.then_inc(s.xg_turned, 1)

        turn_x(0, 0)

        def step(pair, i, first, last):
            n = pair * 2 + i
            pe.wait_ge(s.xgT_ready, n * 2 + 2)
            pe.wait_ge((s.w_gu_in0, s.w_gu_in1)[i], pair * 32 + 32)
            if first:
                pe.wait_ge(s.tiles_known, 1)
                pe.wait_ge(s.logits_read, NTT)
            else:
                pe.wait_ge(s.hid_ready, n - 1)
            for k in range(KD):
                m = mm(PS[:, 2 + i, :], xgT[i][:, k], w_gu[i][:, k].rearrange("p g f -> p (g f)"), start=(k == 0), stop=(k == KD - 1))
            m.then_inc(s.up_done, 1)
            if not (last and i == 1):
                turn_x(pair + i, 1 - i)
            pe.wait_ge(s.hid_ready, n + 1)
            if not (first and i == 0):
                pe.wait_ge(s.hidT_ready, n)
            for k in range(2):
                m = nc.tensor.transpose(PS[:, 4, k * P:(k + 1) * P], hid[:, k:FF:2], ident)
            m.then_inc(s.hid_turned, 1)
            pe.wait_ge(s.hidT_ready, n + 1)
            pe.wait_ge((s.w_dn_in0, s.w_dn_in1)[i], pair * 16 + 16)
            if first and i == 0:
                pe.wait_ge(s.residual, NTT)
            else:
                pe.wait_ge(s.y_read, n * 2)
            for half in range(2):
                for k in range(2):
                    m = mm(PS[:, 5 + half, :], hidT[:, k], w_dn[i][:, k, half * 512:(half + 1) * 512], start=(k == 0), stop=(k == 1))
            m.then_inc(s.down_done, 1)

        pairs_loop(pe, step)

    def scalar_moe(act, link, tell):
        A = nc.scalar.activation
        act.wait_ge(s.route_arg, 1)
        tell(A(gexp, gexp, ACT.Exp), s.route_exp)
        act.wait_ge(s.route_arg, 2)
        tell(A(e2, e2, ACT.Exp), s.route_exp)

        def x_half(pair, i, first):
            n = pair * 2 + i
            act.wait_ge(s.xg_turned, n + 1)
            if not first:
                act.wait_ge(s.up_done, n - 1)
            A(xgT[i][:, 0:4], PS[:, 0, :].rearrange("p (k t) -> p k t", k=4), ACT.Copy).then_inc(s.xgT_ready, 1)

        x_half(0, 0, True)

        def step(pair, i, first, last):
            n = pair * 2 + i
            act.wait_ge(s.up_done, n + 1)
            if not (first and i == 0):
                act.wait_ge(s.hid_ready, n)
            A(silu, PS[:, 2 + i, 0:FF], ACT.Silu).then_inc(s.silu_ready, 1)
            if not (last and i == 1):
                x_half(pair + i, 1 - i, first and i == 0)
            act.wait_ge(s.down_done, n + 1)
            if not first:
                act.wait_ge((s.y_out0, s.y_out1)[i], pair * 16)
            A(ysb[i][:, 0:512], PS[:, 5, :], ACT.Copy).then_inc(s.y_read, 1)

        pairs_loop(act, step)
        for c in range(NTT):
            r = x_rows(c)
            act.wait_ge(s.moments, NTT + c + 1)
            link(A(fsd[0:r], fmv[0:r, 1:2], ACT.Ln, bias=ln_eps[0:r]))
            tell(A(fsd[0:r], fsd[0:r], ACT.Exp, scale=-0.5), s.lstd_ready)

    def pool_moe(pool, link, tell):
        g = nc.gpsimd
        pool.wait_ge(s.tiles_known, 1)
        pool.wait_ge(s.x1_written, 16 * NTT)

        pool.wait_ge(s.routed, NTT)
        pool.wait_ge(s.outputs, 16 * early_outs[0])
        pool.wait_ge(s.normed, NTT)
        for n in range(TILES):
            if n >= 2:
                pool.wait_ge(s.xg_turned, n - 1)
                pool.wait_ge(s.hid_ready, n - 1)
            off = bass.IndirectOffsetOnAxis(slot_tok[:, n:n + 1].bitcast(U32), 0)
            g.indirect_dma_start(xg[n % 2], None, x1_dram, off).then_inc((s.xg_in0, s.xg_in1)[n % 2], 16)
            g.tensor_copy(gate_c[n % 2], slot_gate[:, n:n + 1]).then_inc(s.gate_ready, 1)
        pool.wait_ge(s.y_out0, 16 * (TILES // 2))
        pool.wait_ge(s.y_out1, 16 * (TILES // 2))
        pool.wait_ge(s.slots, 1)
        pool.wait_ge(s.ln2_in, 16)

        def affine(c):
            r = x_rows(c)
            pool.wait_ge(s.normed, NTT + c + 1)
            link(g.tensor_tensor(x1_keep[c][0:r], x1_keep[c][0:r], ln2_gb[0:r, 0], ALU.mult))
            tell(g.tensor_tensor(x1_keep[c][0:r], x1_keep[c][0:r], ln2_gb[0:r, 1], ALU.add), s.y_ready)

        for c in range(NTT):
            r = x_rows(c)
            if c >= 4:
                pool.wait_ge(s.y_added, c - 3)
            for k, dst in ((0, ya), (1, yb)):
                off = bass.IndirectOffsetOnAxis(pos_i[0:r, k * NTT + c:k * NTT + c + 1].bitcast(U32), 0)
                g.indirect_dma_start(dst[c % 4][0:r], None, y_slots, off).then_inc((s.yg_in0, s.yg_in1, s.yg_in2, s.yg_in3)[c % 4], 16)
            if c >= 2:
                affine(c - 2)
        affine(NTT - 2)
        affine(NTT - 1)

    def vector_moe(dve, link, tell):
        v = nc.vector
        last4 = lambda ap: ap.unsqueeze(2).to_broadcast([P, NTT, 4])
        valid = const("valid")
        dve.wait_ge(s.mixed, NTT)

        def first_hot(out, vals, top):
            link(v.tensor_tensor(scr, vals, last4(top), ALU.is_ge))
            link(v.tensor_tensor(scr, scr, const("first").unsqueeze(1).to_broadcast([P, NTT, 4]), ALU.mult))
            link(v.tensor_reduce(s2, scr, X, ALU.max))
            link(v.tensor_tensor(out, scr, last4(s2), ALU.is_equal))

        lg = LG[:, :, 0:NG]
        link(v.tensor_reduce(gmax, lg, X, ALU.max))
        tell(v.tensor_tensor(gexp, lg, last4(gmax), ALU.subtract), s.route_arg)
        first_hot(ghot, lg, gmax)
        dve.wait_ge(s.route_exp, 1)
        link(v.tensor_reduce(gden, gexp, X, ALU.add))
        link(v.reciprocal(gden, gden))
        le = LG[:, :, NG:].rearrange("p i (g j) -> p i g j", g=NG)
        link(v.tensor_tensor(le_m, le, ghot.unsqueeze(3).to_broadcast([P, NTT, NG, NJ]), ALU.mult))
        link(v.tensor_reduce(leg, le_m.rearrange("p i g j -> p i j g"), X, ALU.add))
        link(v.tensor_reduce(v1, leg, X, ALU.max))
        first_hot(hot[0], leg, v1)
        link(v.scalar_tensor_tensor(leg2, hot[0], -BIG, leg, ALU.mult, ALU.add))
        link(v.tensor_reduce(v2, leg2, X, ALU.max))
        first_hot(hot[1], leg2, v2)
        tell(v.tensor_tensor(e2, v2, v1, ALU.subtract), s.route_arg)
        for k in range(2):
            e4 = ex[k].rearrange("p i (g j) -> p i g j", g=NG)
            link(v.tensor_tensor(e4, ghot.unsqueeze(3).to_broadcast([P, NTT, NG, NJ]),
                                 hot[k].unsqueeze(2).to_broadcast([P, NTT, NG, NJ]), ALU.mult))
            link(v.tensor_tensor(ex[k], ex[k], valid.unsqueeze(2).to_broadcast([P, NTT, NE]), ALU.mult))
        tell(v.tensor_tensor(esum, ex[0], ex[1], ALU.add), s.esum_ready)
        dve.wait_ge(s.route_exp, 2)
        link(v.tensor_scalar(s2, e2, 1.0, None, ALU.add))
        link(v.reciprocal(s2, s2))
        link(v.tensor_tensor(s2, s2, gden, ALU.mult))
        link(v.tensor_tensor(wts[:, 0], s2, valid, ALU.mult))
        link(v.tensor_tensor(wts[:, 1], wts[:, 0], e2, ALU.mult))
        dve.wait_ge(s.ranked, 1)
        link(v.tensor_copy(tot, PS[:, 1, 0:NTT * NE].rearrange("p (i e) -> p i e", e=NE)))
        link(v.memset(cnt[:, 0], 0.0))
        for c in range(1, NTT):
            link(v.tensor_tensor(cnt[:, c], cnt[:, c - 1], tot[:, c - 1], ALU.add))
        link(v.tensor_tensor(n_e, cnt[:, NTT - 1], tot[:, NTT - 1], ALU.add))
        link(v.tensor_tensor(slotp, cnt, PS[:, 0, 0:NTT * NE].rearrange("p (i e) -> p i e", e=NE), ALU.add))
        link(v.tensor_tensor(cmp9, n_e.unsqueeze(2).to_broadcast([P, NE, NTT]),
                             const("full").unsqueeze(1).to_broadcast([P, NE, NTT]), ALU.is_gt))
        link(v.tensor_reduce(nt_e, cmp9, X, ALU.add))
        link(v.tensor_tensor_scan(end_e, ones[:, 0:NE], nt_e, 0.0, ALU.mult, ALU.add))
        link(v.tensor_tensor(base_e, end_e, nt_e, ALU.subtract))
        link(v.tensor_scalar(base_e, base_e, float(P), None, ALU.mult))
        link(v.tensor_tensor(slotp, slotp, base_e.unsqueeze(1).to_broadcast([P, NTT, NE]), ALU.add))
        for k in range(2):
            link(v.tensor_tensor(ex[k], ex[k], slotp, ALU.mult))
            link(v.tensor_reduce(pos[:, k * NTT:(k + 1) * NTT], ex[k], X, ALU.add))
        link(v.tensor_copy(pos_i, pos))
        link(v.tensor_scalar(hi_i, pos_i, 7, None, ALU.arith_shift_right))
        link(v.tensor_scalar(lo_i, pos_i, P - 1, None, ALU.bitwise_and))
        link(v.tensor_copy(hi_f, hi_i))
        link(v.tensor_copy(lo_f, lo_i))
        link(v.tensor_tensor(cmp32, const("lane")[:, 0:TILES].unsqueeze(2).to_broadcast([P, TILES, NE]),
                             end_e.unsqueeze(1).to_broadcast([P, TILES, NE]), ALU.is_ge))
        link(v.tensor_reduce(slot_gate, cmp32, X, ALU.add))
        link(v.tensor_scalar(slot_gate, slot_gate, float(NE - 1), None, ALU.min))
        link(v.tensor_copy(tile_expert.bitcast(I32), slot_gate))
        q18 = 2 * NTT
        link(v.tensor_tensor(oh_lo, const("lane").unsqueeze(1).to_broadcast([P, q18, P]), lo_f.unsqueeze(2).to_broadcast([P, q18, P]), ALU.is_equal))
        link(v.tensor_tensor(oh_hi[:, :, 0], const("lane")[:, 0:TILES].unsqueeze(1).to_broadcast([P, q18, TILES]),
                             hi_f.unsqueeze(2).to_broadcast([P, q18, TILES]), ALU.is_equal))
        link(v.tensor_tensor(oh_hi[:, :, 1], oh_hi[:, :, 0], wts.rearrange("p w i -> p (w i)").unsqueeze(2).to_broadcast([P, q18, TILES]), ALU.mult))
        for k in range(2):
            part = oh_hi[:, k * NTT:(k + 1) * NTT, 0]
            i = v.tensor_tensor(part, part, const("token").unsqueeze(2).to_broadcast([P, NTT, TILES]), ALU.mult)
        tell(i, s.onehots)
        dve.wait_ge(s.slots, 1)
        link(v.tensor_copy(slot_tok, PS[:, 2, 0:32]))
        tell(v.tensor_copy(slot_gate, PS[:, 2, 32:64]), s.tiles_known)

        def x_half(pair, i, first):
            n = pair * 2 + i
            dve.wait_ge(s.xg_turned, n + 1)
            if not first:
                dve.wait_ge(s.up_done, n - 1)
            v.tensor_copy(xgT[i][:, 4:8], PS[:, 1, :].rearrange("p (k t) -> p k t", k=4)).then_inc(s.xgT_ready, 1)

        x_half(0, 0, True)

        def step(pair, i, first, last):
            n = pair * 2 + i
            dve.wait_ge(s.silu_ready, n + 1)
            dve.wait_ge(s.gate_ready, n + 1)
            if not (first and i == 0):
                dve.wait_ge(s.hid_turned, n)
            v.scalar_tensor_tensor(hid, silu, gate_c[i], PS[:, 2 + i, FF:2 * FF], ALU.mult, ALU.mult).then_inc(s.hid_ready, 1)
            if not (last and i == 1):
                x_half(pair + i, 1 - i, first and i == 0)
            dve.wait_ge(s.hid_turned, n + 1)
            if not (first and i == 0):
                dve.wait_ge(s.down_done, n)
            v.tensor_copy(hidT, PS[:, 4, 0:2 * P].rearrange("p (k t) -> p k t", k=2)).then_inc(s.hidT_ready, 1)
            dve.wait_ge(s.down_done, n + 1)
            if not first:
                dve.wait_ge((s.y_out0, s.y_out1)[i], pair * 16)
            v.tensor_copy(ysb[i][:, 512:1024], PS[:, 6, :]).then_inc(s.y_read, 1)

        pairs_loop(dve, step)

        dve.wait_ge(s.x1_back, 32)
        for c in range(NTT):
            r = x_rows(c)
            x = x1_keep[c][0:r]
            dve.wait_ge((s.yg_in0, s.yg_in1, s.yg_in2, s.yg_in3)[c % 4], 32 * (c // 4 + 1))
            link(v.scalar_tensor_tensor(x, x, ALPHA, ya[c % 4][0:r], ALU.mult, ALU.add))
            tell(v.tensor_tensor(x, x, yb[c % 4][0:r], ALU.add), s.y_added)
            st = fst.rearrange("p (g n) -> p g n", g=2)
            for n in range(2):
                i = v.bn_stats(st[0:r, n], x[:, n * 512:(n + 1) * 512])
            link(i)
            tell(v.bn_aggr(fmv[0:r], st[0:r]), s.moments)
            dve.wait_ge(s.lstd_ready, NTT + c + 1)
            tell(v.tensor_scalar(x, x, fmv[0:r, 0:1], fsd[0:r], ALU.subtract, ALU.mult), s.normed)

    block = ctx.enter_context(nc.Block())

    @block.sync
    def _(sp):
        sp.dma_start(wgt, t["wg"]).then_inc(s.params_in, 16)
        sp.dma_start(xT[:, 0:4], t["xT"][:, 0:4]).then_inc(s.xT_in, 16)
        sp.dma_start(xT[:, 4:8], t["xT"][:, 4:8]).then_inc(s.xT_in2, 16)
        sp.dma_start(bias, t["b_row"][:, 0:1024].partition_broadcast(P).rearrange("p a n -> p (a n)")).then_inc(s.bias_in, 16)
        for g in range(7):
            if g == 3:
                sp.wait_ge(s.projected, last_piece(3))
            if g == 4:
                sp.wait_ge(s.projected, last_piece(7))
            if g == 5:
                sp.wait_ge(s.projected, last_piece(11))
            if g == 6:
                sp.wait_ge(s.projected, last_piece(15))
            c0 = GROUPS[g][0]
            sp.dma_start(w_slot(g), w_cols[:, :, c0:c0 + 512]).then_inc(w_sem[g], 16)
        sp.wait_ge(s.conv_done, 9)
        out_dma(sp, t["out_conv_p"], raw_p3)
        out_dma(sp, t["out_conv_s"][:, :, 0:2], sconv[:, :, 1:3])
        out_dma(sp, t["out_conv_s"][:, :, 2], raw_s)
        out_dma(sp, t["out_m_p"], mend[0:H, NCH:])
        sp.wait_ge(s.c_ready, NCH)
        out_dma(sp, t["out_C_p"], Cst)
        sync_rest(sp)

    @block.tensor
    def _(pe):
        mm = nc.tensor.matmul

        def project(idx, lhs_of, m):
            if idx >= 4:
                pe.wait_ge(s.proj_read, idx - 3)
            for k in range(KD):
                if idx == 0 and k in (0, 4):
                    pe.wait_ge(s.xT_in2 if k else s.xT_in, 16)
                n = idx % 3
                i = mm(PS[0:m, idx % 4, 0:PIECE], lhs_of(k), xT[:, k, n * PIECE:(n + 1) * PIECE],
                       start=(k == 0), stop=(k == KD - 1))
            i.then_inc(s.projected, 1)

        pe.wait_ge(s.consts_in, 32)
        pe.wait_ge(s.params_in, 16 * N_PARAMS)
        for n in range(3):
            project(n, lambda k: wgt[:, k, :], 64)
        for u in range(16):
            g, j = u // 4, u % 4
            if j == 0:
                pe.wait_ge(w_sem[g], 16)
            if u == 3:
                pe.wait_ge(s.gate_rows, 2)
                for c in range(NCH):
                    i = nc.tensor.transpose(PS[:, 4 + c // 4, (c % 4) * 96:(c % 4 + 1) * 96],
                                            g3[0:96, c * P:(c + 1) * P], ident[0:96, 0:96])
                for h in range(H):
                    mm(PS[:, 6, h * 9:h * 9 + 9], sel[0:H, h, :], mend[0:H, :], start=True, stop=True)
                for h in range(H):
                    i = mm(PS[:, 6, 64 + h * 24:64 + (h + 1) * 24], sel[0:H, h, :], gs_rows[0:H, :], start=True, stop=True)
                i.then_inc(s.gates_spread, 1)
            for n in range(3):
                project(3 + 3 * u + n, lambda k: w_slot(g)[:, k, j * P:(j + 1) * P], P)

        def tokens_product(bank, g, c, sem):
            for k in range(KD):
                i = mm(PS[:, bank, :], xT[:, k, c * P:(c + 1) * P], w_slot(g)[:, k, :], start=(k == 0), stop=(k == KD - 1))
            i.then_inc(sem, 1)

        for c in range(NCH + 1):
            tok = slice(c * P, (c + 1) * P)
            if c < NCH:
                if c == 0:
                    pe.wait_ge(s.proj_read, PIECES)
                    pe.wait_ge(s.gates_read, 1)
                    pe.wait_ge(s.qk_silu, 8)
                else:
                    pe.wait_ge(s.h_turned_read, c - 1)
                    pe.wait_ge(s.s_ready, c)
                    pe.wait_ge(s.c_ready, c)
                for h in range(H):
                    i = mm(PS[:, 2, h * P:(h + 1) * P], sel[0:H, h, :], negM[:, tok], start=True, stop=True)
                i.then_inc(s.decay_b, 1)
                for h in range(H):
                    i = mm(PS[:, 3, h * P:(h + 1) * P], CC[:, 4 + h, tok], CC[:, h, tok], start=True, stop=True)
                i.then_inc(s.scores, 1)
                for h in range(H):
                    i = nc.tensor.transpose(PS[:, 6, h * P:(h + 1) * P], CC[:, 4 + h, tok], ident)
                i.then_inc(s.k_turned, 1)
                if c == 0:
                    pe.wait_ge(s.w_in4, 16)
                    pe.wait_ge(s.w_in5, 16)
                else:
                    pe.wait_ge(s.v_ready, c)
                    pe.wait_ge(s.o_biased, c)
                tokens_product(0, 4, c, s.v_proj)
                tokens_product(1, 5, c, s.o_proj)
            if c >= 1:
                pe.wait_ge(s.hn_ready, c)
                if c < NCH:
                    pe.wait_ge(s.q_arg, c + 1)
                for h in range(H):
                    i = nc.tensor.transpose(PS[:, 2, h * P:(h + 1) * P], hbuf[:, h], ident)
                i.then_inc(s.h_turned, 1)
            if c < NCH:
                pe.wait_ge(s.s_ready, c + 1)
                pe.wait_ge(s.qd_ready, c + 1)
                pe.wait_ge(s.v_ready, c + 1)
                if c >= 1:
                    pe.wait_ge(s.h_ready, c)
                for h in range(H):
                    out = PS[:, 4 + h // 2, (h % 2) * DV1:(h % 2 + 1) * DV1]
                    i = mm(out, dmat[:, h], vext[c % 2][:, h], start=True, stop=(c == 0))
                    if c >= 1:
                        i = mm(out, qd[:, h], Cst[:, h], start=False, stop=True)
                i.then_inc(s.num, 1)
                pe.wait_ge(s.kw_ready, c + 1)
                for h in range(H):
                    i = mm(PS[:, 6 + h // 2, (h % 2) * DV1:(h % 2 + 1) * DV1], kw[:, h], vext[c % 2][:, h], start=True, stop=True)
                i.then_inc(s.cupd, 1)
        for e in range(8):
            for k in range(KD):
                i = mm(PS[:, 0, e * NS:(e + 1) * NS], w_slot(4 + e // 4)[:, k, (e % 4) * P:(e % 4 + 1) * P],
                       xT[:, k, NP_:NT], start=(k == 0), stop=(k == KD - 1))
        i.then_inc(s.zs_proj, 1)
        tensor_rest(pe, tokens_product)

    @block.scalar
    def _(act):
        link, tell = chain(act, s.act_step), teller(act)
        A = nc.scalar.activation
        act.dma_start(cst[:, :], t["consts"]).then_inc(s.consts_in, 16)
        act.dma_start(SC[:, 7680:9216], t["masks"]).then_inc(s.consts_in, 16)
        for dst, src in ((bg[0:64], t["bg"]), (b_cm, t["b_cm"]), (cw, t["cw"]), (cb, t["cb"]), (sconv, t["sconv"]), (m0[0:H], t["m0"]), (g_mix, t["g_mix"])):
            act.dma_start(dst, src).then_inc(s.params_in, 16)
        act.wait_ge(s.params_in, 16 * N_PARAMS)
        act.wait_ge(s.consts_in, 32)

        for idx in range(3):
            act.wait_ge(s.projected, idx + 1)
            tell(A(grow[0:64, idx * PIECE:(idx + 1) * PIECE], PS[0:64, idx % 4, 0:PIECE], ACT.Identity,
              bias=bg[0:64]), s.proj_read)
        act.wait_ge(s.proj_read, 3)
        link(A(fr, grow[32:32 + H], ACT.Copy))
        link(A(lnr, fr, ACT.Abs))
        link(A(lnr, lnr, ACT.Exp, scale=-1.0))
        tell(A(lnr, lnr, ACT.Ln, bias=one_col[0:H]), s.forget_ln)

        def read_unit(u, dst):
            e = [20, 21, 22, 23, 16, 17, 18, 19, 0, 1, 2, 3, 4, 5, 6, 7][u]
            for n in range(3):
                idx = 3 + 3 * u + n
                act.wait_ge(s.projected, idx + 1)
                tell(A(dst[:, n * PIECE:(n + 1) * PIECE], PS[:, idx % 4, 0:PIECE], ACT.Identity,
                  bias=b_cm[:, e:e + 1]), s.proj_read)

        for j in range(H):
            read_unit(j, K[:, j])
            act.wait_ge(s.proj_read, last_piece(j))
            link(A(G[:, j], K[:, j], ACT.Abs))
            link(A(G[:, j], G[:, j], ACT.Exp, scale=-1.0))
            tell(A(G[:, j], G[:, j], ACT.Ln, bias=one_col), s.hf_ln)
            if j == 1:
                act.wait_ge(s.gates_z, 1)
                tell(A(g3[32:32 + H], cmx, ACT.Exp), s.gate_rows)
                tell(A(g3[64:64 + H], lnr[:, 0:NP_], ACT.Exp), s.gate_rows)
            if j >= 1:
                act.wait_ge(s.k_arg, j)
                tell(A(K[:, j - 1], K[:, j - 1], ACT.Exp), s.hg_k_ready)
        act.wait_ge(s.k_arg, H)
        tell(A(K[:, 3], K[:, 3], ACT.Exp), s.hg_k_ready)
        for j in range(H):
            read_unit(4 + j, Q[:, j])
            act.wait_ge(s.proj_read, last_piece(4 + j))
            tell(A(Q[:, j], Q[:, j], ACT.Silu), s.hq_silu)
        for ct in range(9):
            if ct < 8:
                if ct >= 2:
                    act.wait_ge(s.conv_done, ct - 1)
                read_unit(8 + ct, raw[ct % 2][:, 3:])
            if ct >= 1:
                act.wait_ge(s.conv_done, ct)
                tell(A(CC[:, ct - 1], CC[:, ct - 1], ACT.Silu), s.qk_silu)
        act.wait_ge(s.conv_done, 9)
        tell(A(conv_ps, conv_ps, ACT.Silu), s.qk_silu)

        for c in range(NCH + 1):
            if c < NCH:
                act.wait_ge(s.d_arg, c + 1)
                tell(A(dmat, dmat, ACT.Exp), s.d_exp)
                act.wait_ge(s.q_arg, c + 1)
                tell(A(qd, qd, ACT.Exp), s.q_exp)
            if c >= 1:
                act.wait_ge(s.h_turned, c)
                tell(A(CC[:, 0:H, (c - 1) * P:c * P], PS[:, 2, :].rearrange("p (h t) -> p h t", h=H), ACT.Copy), s.h_turned_read)
            if c < NCH:
                act.wait_ge(s.o_biased, c + 1)
                tell(A(ogate, ogate, ACT.Exp, scale=-1.0), s.o_exp)
                act.wait_ge(s.ssq_ready, c + 1)
                link(A(rstd, ssq, ACT.Ln, scale=1.0 / P, bias=rms_eps))
                tell(A(rstd, rstd, ACT.Exp, scale=-0.5), s.rstd_ready)
        scalar_rest(act, link, tell)

    @block.gpsimd
    def _(pool):
        link, tell = chain(pool, s.pool_step), teller(pool)
        pool.wait_ge(s.consts_in, 32)
        tell(nc.gpsimd.tensor_copy(msk[:, :, :].rearrange("p l t -> p (l t)"), mask_words), s.masks_made)
        causal = const("causal").unsqueeze(1).to_broadcast([P, H, P])
        for c in range(NCH):
            pool.wait_ge(s.d_exp, c + 1)
            tell(nc.gpsimd.tensor_tensor(dmat, dmat, causal, ALU.mult), s.d_masked)
            pool.wait_ge(s.h_ready, c + 1)
            tell(nc.gpsimd.tensor_tensor(sq, hbuf, hbuf, ALU.mult), s.h_sq)
        pool_rest(pool, link, tell)

    @block.vector
    def _(dve):
        link, tell = chain(dve, s.dve_step), teller(dve)
        v = nc.vector
        link(v.memset(raw[0][:, 0:3], 0.0))
        link(v.memset(raw[1][:, 0:3], 0.0))
        link(v.memset(g3[0:96], 0.0))
        link(v.memset(keep, 1.0))
        link(v.memset(keep[:, 0:NP_:P], 0.0))
        link(v.memset(drop, 0.0))
        link(v.memset(drop[:, 0:NP_:P], -BIG))
        link(v.memset(mend[0:H], 0.0))
        dve.wait_ge(s.params_in, 16 * N_PARAMS)
        dve.wait_ge(s.forget_ln, 1)
        link(v.scalar_tensor_tensor(fr, fr, 0.0, lnr, ALU.min, ALU.subtract))
        link(v.tensor_tensor_scan(Frow, keep, fr[:, 0:NP_], 0.0, ALU.mult, ALU.add))
        link(v.tensor_tensor(g3[0:H], grow[0:H, 0:NP_], Frow, ALU.subtract))
        link(v.tensor_tensor_scan(cmx, drop, g3[0:H], 0.0, ALU.add, ALU.max))
        link(v.tensor_tensor_scan(mend[0:H, 1:], cmx[:, P - 1:NP_:P], Frow[:, P - 1:NP_:P], 0.0, ALU.max, ALU.add))
        by_chunk = lambda r: r.rearrange("p (c t) -> p c t", c=NCH)
        link(v.tensor_tensor(by_chunk(keep), by_chunk(cmx), mend[0:H, 0:NCH].unsqueeze(2).to_broadcast([H, NCH, P]), ALU.max))
        link(v.tensor_scalar(negM, keep, -1.0, None, ALU.mult))
        link(v.scalar_tensor_tensor(lnr[:, 0:NP_], Frow, -1.0, keep, ALU.mult, ALU.subtract))
        link(v.tensor_copy(drop[:, 0:NCH], keep[:, P - 1:NP_:P]))
        link(v.tensor_tensor(by_chunk(cmx), by_chunk(g3[0:H]), drop[:, 0:NCH].unsqueeze(2).to_broadcast([H, NCH, P]), ALU.subtract))
        link(v.tensor_copy(gs_rows[0:H, 0:NS], grow[0:H, NP_:NT]))
        link(v.tensor_copy(gs_rows[0:H, NS:2 * NS], fr[:, NP_:NT]))
        tell(v.tensor_copy(gs_rows[0:H, 2 * NS:], m0[0:H]), s.gates_z)

        for j in range(H):
            dve.wait_ge(s.hf_ln, j + 1)
            link(v.scalar_tensor_tensor(G[:, j], K[:, j], 0.0, G[:, j], ALU.min, ALU.subtract))
            tell(v.tensor_tensor(K[:, j], G[:, j], K[:, j], ALU.subtract), s.k_arg)
        dve.wait_ge(s.gates_spread, 1)
        for n in range(2):
            i = v.tensor_copy(gcol[:, 4 * n:4 * n + 4], PS[:, 4 + n, 0:384].rearrange("p (c r) -> p c r", c=4))
        link(i)
        link(v.tensor_copy(mprev, PS[:, 6, 0:36].rearrange("p (h c) -> p h c", h=H)))
        tell(v.tensor_copy(gs, PS[:, 6, 64:64 + 96].rearrange("p (h g b) -> p h g b", h=H, g=3)), s.gates_read)
        chunk_keep = cacc
        link(v.memset(chunk_keep, 1.0))
        link(v.memset(chunk_keep[:, 0:NP_:P], 0.0))
        for j in range(H):
            link(v.tensor_tensor_scan(G[:, j, 0:NP_], chunk_keep, G[:, j, 0:NP_], 0.0, ALU.mult, ALU.add))

        for ct in range(8):
            r = raw[ct % 2]
            dve.wait_ge(s.proj_read, last_piece(8 + ct))
            link(v.tensor_scalar(cacc, r[:, 0:NP_], cw[:, ct, 0:1], cb[:, ct:ct + 1], ALU.mult, ALU.add))
            link(v.scalar_tensor_tensor(cacc, r[:, 1:1 + NP_], cw[:, ct, 1:2], cacc, ALU.mult, ALU.add))
            link(v.scalar_tensor_tensor(cacc, r[:, 2:2 + NP_], cw[:, ct, 2:3], cacc, ALU.mult, ALU.add))
            link(v.tensor_copy(raw_s[:, ct], r[:, 3 + NP_:3 + NT]))
            link(v.tensor_copy(raw_p3[:, ct], r[:, NP_:NP_ + 3]))
            tell(v.scalar_tensor_tensor(CC[:, ct], r[:, 3:3 + NP_], cw[:, ct, 3:4], cacc, ALU.mult, ALU.add), s.conv_done)
        cs = conv_ps.rearrange("p (c b) -> p c b", c=8)
        tmp = cacc[:, 0:64].rearrange("p (c b) -> p c b", c=8)
        tap = lambda j: cw[:, :, j:j + 1].to_broadcast([P, 8, NS])
        link(v.tensor_tensor(cs, sconv[:, :, 0], tap(0), ALU.mult))
        link(v.tensor_tensor(cs, cs, cb.unsqueeze(2).to_broadcast([P, 8, NS]), ALU.add))
        for j in (1, 2, 3):
            link(v.tensor_tensor(tmp, raw_s if j == 3 else sconv[:, :, j], tap(j), ALU.mult))
            i = v.tensor_tensor(cs, cs, tmp, ALU.add)
            if j < 3:
                link(i)
        tell(i, s.conv_done)

        dve.wait_ge(s.conv_done, 9)
        for n in range(2):
            link(v.memset(vext[n][:, :, P:], 1.0))
        heads = lambda ap: ap.rearrange("p (h t) -> p h t", h=H)
        for c in range(NCH):
            tok = slice(c * P, (c + 1) * P)
            dve.wait_ge(s.decay_b, c + 1)
            for h in range(H):
                i = v.tensor_scalar(dmat[:, h], PS[:, 2, h * P:(h + 1) * P], gcol[:, c, h:h + 1], 0.0, ALU.add, ALU.min)
            tell(i, s.d_arg)
            tell(v.tensor_tensor(qd, heads(PS[:, 2, :]), mprev[:, :, c:c + 1].to_broadcast([P, H, P]), ALU.add), s.q_arg)
            dve.wait_ge(s.k_turned, c + 1)
            for h in range(H):
                i = v.tensor_scalar(kw[:, h], PS[:, 6, h * P:(h + 1) * P], gcol[:, c, 32 + h:33 + h], KSCALE, ALU.mult, ALU.mult)
            tell(i, s.kw_ready)
            dve.wait_ge(s.q_exp, c + 1)
            dve.wait_ge(s.qk_silu, 8)
            link(v.tensor_copy(dend, qd[:, :, P - 1]))
            tell(v.tensor_tensor(qd, qd, CC[:, 0:H, tok], ALU.mult), s.qd_ready)
            dve.wait_ge(s.scores, c + 1)
            dve.wait_ge(s.d_masked, c + 1)
            tell(v.scalar_tensor_tensor(dmat, heads(PS[:, 3, :]), KSCALE, dmat, ALU.mult, ALU.mult), s.s_ready)
            dve.wait_ge(s.v_proj, c + 1)
            if c == 0:
                dve.wait_ge(s.bias_in, 16)
            tell(v.tensor_tensor(vext[c % 2][:, :, 0:P], heads(PS[:, 0, :]), heads(bias[:, 0:512]), ALU.add), s.v_ready)
            dve.wait_ge(s.o_proj, c + 1)
            tell(v.tensor_tensor(ogate, heads(PS[:, 1, :]), heads(bias[:, 512:1024]), ALU.add), s.o_biased)
            dve.wait_ge(s.o_exp, c + 1)
            link(v.tensor_scalar(ogate, ogate, 1.0, None, ALU.add))
            link(v.reciprocal(ogate, ogate))
            dve.wait_ge(s.num, c + 1)
            qn = PS[:, 4:6, 0:2 * DV1].rearrange("p b (h v) -> p b h v", h=2)[:, :, :, P]
            two = lambda ap: ap.rearrange("p (b h) -> p b h", b=2)
            link(v.scalar_tensor_tensor(two(den), qn, -1.0, two(gcol[:, c, 64:68]), ALU.mult, ALU.max))
            link(v.tensor_tensor(two(den), qn, two(den), ALU.max))
            link(v.reciprocal(rec, den))
            for h in range(H):
                i = v.scalar_tensor_tensor(hbuf[:, h], PS[:, 4 + h // 2, (h % 2) * DV1:(h % 2) * DV1 + P], rec[:, h:h + 1],
                                           ogate[:, h], ALU.mult, ALU.mult)
            tell(i, s.h_ready)
            dve.wait_ge(s.cupd, c + 1)
            for h in range(H):
                ps = PS[:, 6 + h // 2, (h % 2) * DV1:(h % 2 + 1) * DV1]
                if c == 0:
                    i = v.tensor_copy(Cst[:, h], ps)
                else:
                    i = v.scalar_tensor_tensor(Cst[:, h], Cst[:, h], dend[:, h:h + 1], ps, ALU.mult, ALU.add)
            tell(i, s.c_ready)
            dve.wait_ge(s.h_sq, c + 1)
            tell(v.tensor_reduce(ssq, sq, X, ALU.add), s.ssq_ready)
            dve.wait_ge(s.rstd_ready, c + 1)
            tell(v.tensor_tensor(hbuf, hbuf, rstd.unsqueeze(2).to_broadcast([P, H, P]), ALU.mult), s.hn_ready)
        dve.wait_ge(s.zs_proj, 1)
        tell(v.tensor_tensor(zs[:, 0:8], PS[:, 0, 0:64].rearrange("p (e b) -> p e b", e=8),
                        b_cm[:, 8:16].unsqueeze(2).to_broadcast([P, 8, NS]), ALU.add), s.zs_read)
        vector_rest(dve, link, tell)


def layouts(i):
    a = {k: np.asarray(v) for k, v in i.items()}
    x = np.concatenate([a["x_prompt"].reshape(NP_, D), a["x_sample"].reshape(NS, D)])
    w, b = a["w_in"][0], a["b_in"][0]
    wg = np.zeros((D, 64), np.float32)
    wg[:, 0:H], wg[:, 32:32 + H] = w[:, 2048:2048 + H], w[:, 2048 + H:COL_HG]
    bg = np.zeros((64, 1), np.float32)
    bg[0:H, 0], bg[32:32 + H, 0] = b[2048:2048 + H], b[2048 + H:COL_HG]
    cols = [COL_Q, COL_K, COL_V, COL_O, COL_HQ, COL_HF, COL_HI, COL_GT]
    cm = lambda v: v.reshape(-1, P).T
    return {
        "consts": CONST_F, "masks": CONST_M,
        "xT": x.T.reshape(P, KD, NT),
        "x": x,
        "w_in": w,
        "wg": wg.reshape(P, KD, 64), "bg": bg,
        "b_cm": np.concatenate([cm(b[c:c + 512]) for c in cols], 1),
        "b_row": np.concatenate([b[c:c + 512] for c in (COL_V, COL_O, COL_HI, COL_GT)])[None],
        "cw": a["conv_w"][0].reshape(4, 8, P).transpose(2, 1, 0),
        "cb": cm(a["conv_b"][0]),
        "sconv": a["state_conv"][0].reshape(NS, 3, 8, P).transpose(3, 2, 1, 0),
        "C0": a["state_ml_C"][0].transpose(2, 1, 0, 3),
        "n0": a["state_ml_n"][0].transpose(2, 1, 0),
        "m0": a["state_ml_m"][0].T,
        "S0": a["state_hg_S"][0].transpose(2, 1, 0, 3),
        "g_mix": np.concatenate([cm(a["ml_norm_g"][0]), cm(a["hg_norm_g"][0])], 1),
        "w_out": a["w_out"][0],
        "ln1": np.concatenate([a["ln1_g"], a["ln1_b"]]),
        "ln2": np.concatenate([a["ln2_g"], a["ln2_b"]]),
        "w_r": np.concatenate([a["w_router_group"][0], a["w_router_expert"][0]], 1).reshape(KD, P, NG + NE).transpose(1, 0, 2),
        "b_r": np.concatenate([a["b_router_group"], a["b_router_expert"]], 1),
        "w_gate": a["w_gate"][0], "w_up": a["w_up"][0], "w_down": a["w_down"][0],
    }


_OUTS = {
    "y": (NT, D), "conv_p": (P, 8, 3), "C_p": (P, H, DV1), "m_p": (H, 1), "S_p": (P, H, P),
    "conv_s": (P, 8, 3, NS), "C_s": (P, H, NS, P), "n_s": (P, H, NS), "m_s": (H, NS), "S_s": (P, H, NS, P),
}


def kernel(**inputs):
    import concourse.bacc as _bacc
    from concourse.bass_utils import run_bass_kernel_spmd as _run

    nc = _bacc.Bacc("TRN2", target_bir_lowering=False, num_devices=1)
    arrays, args = {}, {}
    for name, a in layouts(inputs).items():
        a = np.ascontiguousarray(a)
        arrays[f"in_{name}"] = a
        args[name] = nc.dram_tensor(f"in_{name}", a.shape, mybir.dt.from_np(a.dtype), kind="ExternalInput").ap()
    for name, shape in _OUTS.items():
        args["out_" + name] = nc.dram_tensor(f"out_{name}", shape, F32, kind="ExternalOutput").ap()
    program(nc, args)
    r = _run(nc, [arrays], core_ids=[0]).results[0]
    o = {name: r[f"out_{name}"] for name in _OUTS}
    return (
        o["y"][:NP_].reshape(1, NP_, D), o["y"][NP_:].reshape(NS, 1, D),
        o["conv_p"].transpose(2, 1, 0).reshape(1, 1, 3, D),
        o["C_p"][:, :, :P].transpose(1, 0, 2)[None, None], o["C_p"][:, :, P].T[None, None], o["m_p"].T[None], o["S_p"].transpose(1, 0, 2)[None, None],
        o["conv_s"].transpose(3, 2, 1, 0).reshape(1, NS, 3, D),
        o["C_s"].transpose(2, 1, 0, 3)[None], o["n_s"].transpose(2, 1, 0)[None], o["m_s"].T[None],
        o["S_s"].transpose(2, 1, 0, 3)[None],
    )
```

```python
from contextlib import ExitStack

import numpy as np

import concourse.bass as bass
from concourse import mybir

F32 = mybir.dt.float32
I32 = mybir.dt.int32
U32 = mybir.dt.uint32
U8 = mybir.dt.uint8
ALU = mybir.AluOpType
ACT = mybir.ActivationFunctionType
X = mybir.AxisListType.X

P = 128
D = 1024
NP_, NS = 1024, 8
NT = NP_ + NS
KD = D // P
NCH = NP_ // P
H = 4
DV1 = P + 1
PIECE = NT // 3
HB = H * NS
LEVELS = [64, 32, 16, 8, 4, 2, 1]
NLEV = len(LEVELS)
NTT = NCH + 1
NG, NJ = 4, 4
NE = NG * NJ
FF = 256
TILES = (2 * NT + NE * (P - 1)) // P
ALPHA = 2 ** 0.25
LN_EPS, RMS_EPS = 1e-5, 1e-6
KSCALE = P ** -0.5
N_PARAMS = 8
BIG = 1e30
SMALL = 904

COL_Q, COL_K, COL_V, COL_O = 0, 512, 1024, 1536
COL_HG = 4 * 512 + 2 * H
COL_HQ, COL_HF, COL_HI, COL_GT = COL_HG, COL_HG + 512, COL_HG + 1024, COL_HG + 1536

CONST = {}


def constants():
    i = np.arange(P)
    c = {
        "ident": np.eye(P),
        "ones": np.ones((P, P)),
        "causal": (i[:, None] <= i[None, :]),
        "before": (i[:, None] < i[None, :]),
        "lane": np.broadcast_to(i[None, :], (P, P)),
        "token": np.where(i[:, None] + P * np.arange(NTT)[None] < NT, i[:, None] + P * np.arange(NTT)[None], 0),
        "valid": (i[:, None] + P * np.arange(NTT)[None] < NT),
        "first": np.broadcast_to(np.array([4, 3, 2, 1]), (P, 4)),
        "full": np.broadcast_to(P * np.arange(NTT), (P, NTT)),
        "eps": np.broadcast_to(np.array([1.0, RMS_EPS, LN_EPS, 0.0]), (P, 4)),
    }
    cols, at = [], 0
    for name, a in c.items():
        a = np.asarray(a, np.float32).reshape(P, -1)
        CONST[name] = (at, at + a.shape[1])
        at += a.shape[1]
        cols.append(a)
    masks = []
    for b in LEVELS:
        blk, first = i // (2 * b), (i // b) % 2 == 0
        masks.append((blk[:, None] == blk[None, :]) & first[:, None] & ~first[None, :])
    masks.append(np.eye(P, dtype=bool))
    masks = np.stack(masks, 1).astype(np.float32).reshape(P, -1)
    sel = ((i[:, None, None] == np.arange(H)[None, :, None]) * np.ones((P, H, P), np.float32)).reshape(P, -1)
    return np.ascontiguousarray(np.concatenate(cols, 1)), np.concatenate([masks, sel], 1)


CONST_F, CONST_M = constants()


def program(nc, t):
    with ExitStack() as ctx:
        _program(nc, t, ctx)


def _program(nc, t, ctx):
    def sb(name, shape, dt=F32):
        return ctx.enter_context(nc.sbuf_tensor(name, shape, dt))

    cst = sb("constants", [P, CONST_F.shape[1]])
    msk = sb("level_masks", [P, NLEV + 1, P], U8)
    xT = sb("x_cm", [P, KD, NT])
    W = sb("weight_slots", [P, 3, KD, 512])
    CC = sb("conv_qk", [P, 8, NP_])
    G = sb("hg_decay", [P, H, NT])
    Q = sb("hg_q", [P, H, NT])
    K = sb("hg_k", [P, H, NT])
    SC = sb("scratch", [P, 9728])
    R = sb("router", [P, 384])
    SM = sb("small", [P, SMALL])
    PS = ctx.enter_context(nc.psum_tensor("psum", [P, 8, 512], F32))

    def const(name):
        a, b = CONST[name]
        return cst[:, a:b]

    ident, ones = const("ident"), const("ones")
    one_col, rms_eps, ln_eps = (cst[:, CONST["eps"][0] + n:CONST["eps"][0] + n + 1] for n in range(3))

    at = [0]

    def small(n):
        at[0] += n
        assert at[0] <= SMALL
        return SM[:, at[0] - n:at[0]]

    cw = small(32).rearrange("p (c j) -> p c j", c=8)
    cb = small(8)
    b_cm = small(32)
    bg = small(1)
    g_mix = small(8)
    sconv = small(8 * 3 * NS).rearrange("p (c j b) -> p c j b", c=8, j=3)
    raw_s = small(8 * NS).rearrange("p (c b) -> p c b", c=8)
    raw_p3 = small(24).rearrange("p (c j) -> p c j", c=8)
    conv_ps = small(64)
    mend = small(NCH + 1)
    mprev = small(H * (NCH + 1)).rearrange("p (h c) -> p h c", h=H)
    m0 = small(NS)
    gs_rows = small(3 * NS)
    gs = small(H * 3 * NS).rearrange("p (h g b) -> p h g b", h=H, g=3)
    zs = small(16 * NS).rearrange("p (e b) -> p e b", e=16)
    den, rec, ssq, rstd, dend = (small(H) for _ in range(5))
    ms_row = small(NS)

    raw = [SC[:, 0:3 + NT], SC[:, 1036:1036 + 3 + NT]]
    cacc = SC[:, 2072:2072 + NP_]
    g3 = SC[:, 3100:3100 + NP_]
    CF = CC[:, :, :].rearrange("p a b -> p (a b)")
    grow = CF[:, 0:NT]
    fr, lnr = CF[0:H, NT:2 * NT], CF[0:H, 2 * NT:3 * NT]
    keep, drop, Frow, cmx = (CF[0:H, 3100 + n * NP_:3100 + (n + 1) * NP_] for n in range(4))
    buf = lambda n: SC[:, n * 512:(n + 1) * 512].rearrange("p (h t) -> p h t", h=H)
    dmat, qd, kw, hbuf, sq = (buf(n) for n in range(5))
    vext = [SC[:, 2560 + n * 516:2560 + (n + 1) * 516].rearrange("p (h v) -> p h v", h=H) for n in range(2)]
    ogate = SC[:, 3592:4104].rearrange("p (h t) -> p h t", h=H)
    Cst = SC[:, 4104:4620].rearrange("p (h v) -> p h v", h=H)
    negM = SC[0:H, 4620:5644]
    gcol = SC[:, 5644:6412].rearrange("p (c r) -> p c r", c=NCH)
    bias = SC[:, 6656:7680]

    xlev = [buf(0), buf(1)]
    amat, hmix, qdec, kend, ibuf, gtb = (buf(n) for n in (2, 3, 4, 5, 6, 7))
    Sst = buf(8)
    zrow = SC[0:NS, 5632:6656], SC[0:NS, 0:1024]
    xrow = SC[:, 4608:5632]
    xTt = SC[:, 5632:6656].rearrange("p (k t) -> p k t", k=KD)
    ln_gb = SC[:, 7680:9728].rearrange("p (g n) -> p g n", g=2)
    w_out = W[:, 1:3].rearrange("p s a b -> p (s a b)").rearrange("p (e n) -> p e n", e=8)
    w_r = R[:, 0:160].rearrange("p (k e) -> p k e", k=KD)
    b_r = R[:, 160:180]
    LG = R[:, 180:360].rearrange("p (i e) -> p i e", i=NTT)
    stats = R[:, 360:372].rearrange("p (g n) -> p g n", g=2)
    mv = R[:, 372:374]
    lstd = R[:, 374:375]
    egend = R[:, 376:380]
    mixS = small(8 * NS).rearrange("p (e b) -> p e b", e=8)
    XF = xT[:, :, :].rearrange("p k t -> p (k t)")
    C0 = XF[:, 0:4096].rearrange("p (e v) -> p e v", e=HB)
    vdiag = XF[0:HB, 4096:8192].rearrange("p (e v) -> p e v", e=HB)
    S0 = W[:, 0].rearrange("p k n -> p (k n)").rearrange("p (e v) -> p e v", e=HB)
    n0 = small(HB)
    T = [SC[:, n * HB:(n + 1) * HB] for n in range(32)]
    by_hb = lambda ap: ap.rearrange("p (h b) -> p h b", h=H)
    x1_dram = nc.dram_tensor("x1_rows", (NT, D), F32).ap()
    flatf = lambda tile: tile[:, :, :].rearrange("p a b -> p (a b)")
    KF, GF, QF = flatf(K), flatf(G), flatf(Q)
    wslots = [flatf(CC), W[:, 1:3].rearrange("p s a b -> p (s a b)")]
    w_gu = [w[:, 0:4096].rearrange("p (k g f) -> p k g f", k=KD, g=2) for w in wslots]
    w_dn = [w[:, 4096:6144].rearrange("p (k n) -> p k n", k=2) for w in wslots]
    xg = [SC[:, n * D:(n + 1) * D] for n in range(2)]
    xgT = [SC[:, (2 + n) * D:(3 + n) * D].rearrange("p (k t) -> p k t", k=KD) for n in range(2)]
    ysb = [SC[:, (4 + n) * D:(5 + n) * D] for n in range(2)]
    silu, hid = SC[:, 6144:6400], SC[:, 6400:6656]
    hidT = SC[:, 6656:6912].rearrange("p (k t) -> p k t", k=2)
    gate_c = [SC[:, 6914 + n:6915 + n] for n in range(2)]
    y_slots = nc.dram_tensor("y_slots", (TILES * P, D), F32).ap()
    oh_lo = KF[:, 0:18 * P].rearrange("p (q n) -> p q n", q=18)
    oh_hi = QF[:, 0:18 * 64].rearrange("p (q w n) -> p q w n", q=18, w=2)
    kat = [18 * P]

    def route_tile(n):
        kat[0] += n
        assert kat[0] <= 4128
        return KF[:, kat[0] - n:kat[0]]

    slot_tok = route_tile(TILES).bitcast(I32)
    slot_gate = route_tile(TILES)
    tile_expert = route_tile(TILES)
    pos = route_tile(2 * NTT)
    pos_i = route_tile(2 * NTT).bitcast(I32)
    hi_i, lo_i = (route_tile(2 * NTT).bitcast(I32) for _ in range(2))
    hi_f, lo_f = (route_tile(2 * NTT) for _ in range(2))
    wts = route_tile(2 * NTT).rearrange("p (w i) -> p w i", w=2)
    gat = [0]

    def work(*shape):
        n = int(np.prod(shape))
        gat[0] += n
        assert gat[0] <= 4128
        ap = GF[:, gat[0] - n:gat[0]]
        if len(shape) == 2:
            return ap.rearrange("p (a b) -> p a b", b=shape[1])
        if len(shape) == 3:
            return ap.rearrange("p (a b c) -> p a b c", b=shape[1], c=shape[2])
        return ap

    gmax, gden, v1, v2, e2, s2 = (work(NTT) for _ in range(6))
    gexp, ghot, scr, leg, leg2 = (work(NTT, 4) for _ in range(5))
    hot = [work(NTT, 4) for _ in range(2)]
    ex = [work(NTT, NE) for _ in range(2)]
    esum, tot, slotp = (work(NTT, NE) for _ in range(3))
    le_m = work(NTT, 4, 4)
    cnt = work(NTT, NE)
    n_e, nt_e, end_e, base_e = (work(NE) for _ in range(4))
    cmp9 = work(NE, NTT)
    cmp32 = work(TILES, NE)
    x1_keep = [XF[:, c * D:(c + 1) * D] for c in range(8)] + [SC[:, 8 * D:9 * D]]
    ya = [GF[:, n * D:(n + 1) * D] for n in range(4)]
    yb = [QF[:, n * D:(n + 1) * D] for n in range(4)]
    ln2_gb = wslots[0][:, 6144:8192].rearrange("p (g n) -> p g n", g=2)
    fst, fmv, fsd = (small(n) for n in (12, 2, 1))
    class Semaphores:
        pass

    s = Semaphores()

    def sem(name):
        return ctx.enter_context(nc.semaphore(name))

    s.consts_in = sem("consts_in")
    s.params_in = sem("params_in")
    s.xT_in = sem("xT_in")
    s.xT_in2 = sem("xT_in2")
    s.bias_in = sem("bias_in")
    s.w_in0 = sem("w_in0")
    s.w_in1 = sem("w_in1")
    s.w_in2 = sem("w_in2")
    s.w_in3 = sem("w_in3")
    s.w_in4 = sem("w_in4")
    s.w_in5 = sem("w_in5")
    s.w_in6 = sem("w_in6")
    s.w_in7 = sem("w_in7")
    s.dve_step = sem("dve_step")
    s.act_step = sem("act_step")
    s.pool_step = sem("pool_step")
    s.projected = sem("projected")
    s.proj_read = sem("proj_read")
    s.gates_z = sem("gates_z")
    s.forget_ln = sem("forget_ln")
    s.gate_rows = sem("gate_rows")
    s.gates_spread = sem("gates_spread")
    s.gates_read = sem("gates_read")
    s.hf_ln = sem("hf_ln")
    s.k_arg = sem("k_arg")
    s.hg_k_ready = sem("hg_k_ready")
    s.conv_done = sem("conv_done")
    s.qk_silu = sem("qk_silu")
    s.hq_silu = sem("hq_silu")
    s.decay_b = sem("decay_b")
    s.scores = sem("scores")
    s.k_turned = sem("k_turned")
    s.num = sem("num")
    s.cupd = sem("cupd")
    s.h_turned = sem("h_turned")
    s.h_turned_read = sem("h_turned_read")
    s.d_arg = sem("d_arg")
    s.q_arg = sem("q_arg")
    s.d_exp = sem("d_exp")
    s.q_exp = sem("q_exp")
    s.d_masked = sem("d_masked")
    s.kw_ready = sem("kw_ready")
    s.s_ready = sem("s_ready")
    s.qd_ready = sem("qd_ready")
    s.v_proj = sem("v_proj")
    s.o_proj = sem("o_proj")
    s.v_ready = sem("v_ready")
    s.o_biased = sem("o_biased")
    s.o_exp = sem("o_exp")
    s.h_ready = sem("h_ready")
    s.h_sq = sem("h_sq")
    s.ssq_ready = sem("ssq_ready")
    s.rstd_ready = sem("rstd_ready")
    s.hn_ready = sem("hn_ready")
    s.c_ready = sem("c_ready")
    s.zs_proj = sem("zs_proj")
    s.zs_read = sem("zs_read")
    s.outputs = sem("outputs")
    s.masks_made = sem("masks_made")
    s.dots = sem("dots")
    s.dots_in = sem("dots_in")
    s.down_done = sem("down_done")
    s.esum_ready = sem("esum_ready")
    s.g_exp = sem("g_exp")
    s.gate_ready = sem("gate_ready")
    s.gt_biased = sem("gt_biased")
    s.gt_exp = sem("gt_exp")
    s.gt_proj = sem("gt_proj")
    s.hgs_ready = sem("hgs_ready")
    s.hidT_ready = sem("hidT_ready")
    s.hid_ready = sem("hid_ready")
    s.hid_turned = sem("hid_turned")
    s.i_proj = sem("i_proj")
    s.i_ready = sem("i_ready")
    s.kend_arg = sem("kend_arg")
    s.kend_exp = sem("kend_exp")
    s.kend_ready = sem("kend_ready")
    s.kend_tm = sem("kend_tm")
    s.kend_turned = sem("kend_turned")
    s.kv_in = sem("kv_in")
    s.kv_turned = sem("kv_turned")
    s.level_arg = sem("level_arg")
    s.level_exp = sem("level_exp")
    s.level_kept = sem("level_kept")
    s.level_scaled = sem("level_scaled")
    s.levels = sem("levels")
    s.ln2_in = sem("ln2_in")
    s.logits_read = sem("logits_read")
    s.lstd_ready = sem("lstd_ready")
    s.mixS_ready = sem("mixS_ready")
    s.mixed = sem("mixed")
    s.mixer_in = sem("mixer_in")
    s.moments = sem("moments")
    s.normed = sem("normed")
    s.o_scaled = sem("o_scaled")
    s.o_num = sem("o_num")
    s.o_turned = sem("o_turned")
    s.o_turned_read = sem("o_turned_read")
    s.ogate_arg = sem("ogate_arg")
    s.ogate_exp = sem("ogate_exp")
    s.on_ready = sem("on_ready")
    s.onehots = sem("onehots")
    s.gt_gated = sem("gt_gated")
    s.outer = sem("outer")
    s.qg_ready = sem("qg_ready")
    s.ranked = sem("ranked")
    s.residual = sem("residual")
    s.route_arg = sem("route_arg")
    s.route_exp = sem("route_exp")
    s.routed = sem("routed")
    s.s_upd = sem("s_upd")
    s.sgates_arg = sem("sgates_arg")
    s.sgates_exp = sem("sgates_exp")
    s.silu_ready = sem("silu_ready")
    s.slots = sem("slots")
    s.sq_in = sem("sq_in")
    s.sq_sum = sem("sq_sum")
    s.srstd = sem("srstd")
    s.state_in = sem("state_in")
    s.state_read = sem("state_read")
    s.tiles_known = sem("tiles_known")
    s.up_done = sem("up_done")
    s.vdiag_ready = sem("vdiag_ready")
    s.w_dn_in0 = sem("w_dn_in0")
    s.w_dn_in1 = sem("w_dn_in1")
    s.w_gu_in0 = sem("w_gu_in0")
    s.w_gu_in1 = sem("w_gu_in1")
    s.x1_back = sem("x1_back")
    s.x1_ready = sem("x1_ready")
    s.x1_turned = sem("x1_turned")
    s.x1_turned_read = sem("x1_turned_read")
    s.x1_written = sem("x1_written")
    s.x_in = sem("x_in")
    s.xgT_ready = sem("xgT_ready")
    s.xg_in0 = sem("xg_in0")
    s.xg_in1 = sem("xg_in1")
    s.xg_turned = sem("xg_turned")
    s.y_added = sem("y_added")
    s.y_out0 = sem("y_out0")
    s.y_out1 = sem("y_out1")
    s.y_read = sem("y_read")
    s.y_ready = sem("y_ready")
    s.yg_in0 = sem("yg_in0")
    s.yg_in1 = sem("yg_in1")
    s.yg_in2 = sem("yg_in2")
    s.yg_in3 = sem("yg_in3")
    s.zs_row = sem("zs_row")
    s.zs_turned = sem("zs_turned")
    outs = [0]

    def out_dma(eng, dst, src):
        eng.dma_start(dst, src).then_inc(s.outputs, 16)
        outs[0] += 1

    def chain(eng, sem):
        n = [0]

        def link(ins):
            n[0] += 1
            ins.then_inc(sem, 1)
            eng.wait_ge(sem, n[0])
        return link

    def teller(eng):
        told = {}

        def tell(ins, sem):
            told[sem] = told.get(sem, 0) + 1
            ins.then_inc(sem, 1)
            eng.wait_ge(sem, told[sem])
        return tell

    w_cols = t["w_in"].rearrange("(p k) e -> p k e", k=KD)
    GROUPS = [(COL_HF, 0), (COL_HQ, 1), (COL_Q, 2), (COL_K, 0), (COL_V, 1), (COL_O, 2), (COL_GT, 0), (COL_HI, 3)]
    slot3 = CC[:, 4:8, :].rearrange("p a (b e) -> p (a b) e", b=2)
    w_slot = lambda g: slot3 if GROUPS[g][1] == 3 else W[:, GROUPS[g][1]]
    w_sem = [s.w_in0, s.w_in1, s.w_in2, s.w_in3, s.w_in4, s.w_in5, s.w_in6, s.w_in7]
    PIECES = 3 * 17
    last_piece = lambda unit: 3 * (unit + 2)
    mask_words = SC[:, 7680:7680 + (NLEV + 1) * P]
    sel = SC[:, 8704:8704 + H * P].rearrange("p (h m) -> p h m", h=H)
    wgt = SC[:, 4200:4200 + KD * 64].rearrange("p (k e) -> p k e", k=KD)

    def x_rows(c):
        return P if c < NCH else NS

    def sync_rest(sp):
        sp.wait_ge(s.qk_silu, 9)
        sp.wait_ge(s.cupd, NCH)
        sp.wait_ge(s.h_turned_read, NCH)
        sp.wait_ge(s.zs_proj, 1)
        sp.wait_ge(s.masks_made, 1)
        sp.dma_start(w_slot(7), w_cols[:, :, COL_HI:COL_HI + 512]).then_inc(s.w_in7, 16)
        sp.wait_ge(s.o_biased, NCH)
        sp.dma_start(bias, t["b_row"][:, 1024:2048].partition_broadcast(P).rearrange("p a n -> p (a n)")).then_inc(s.mixer_in, 16)
        sp.dma_start(w_out, t["w_out"].rearrange("(e p) n -> p e n", p=P)).then_inc(s.mixer_in, 16)
        sp.dma_start(ln_gb, t["ln1"].partition_broadcast(P)).then_inc(s.mixer_in, 16)
        sp.dma_start(w_r, t["w_r"]).then_inc(s.mixer_in, 16)
        sp.dma_start(b_r, t["b_r"].partition_broadcast(P).rearrange("p a n -> p (a n)")).then_inc(s.mixer_in, 16)
        sp.dma_start(by_hb(n0), t["n0"]).then_inc(s.mixer_in, 16)
        for c in range(NTT):
            if c == 0:
                sp.wait_ge(s.c_ready, NCH)
                sp.wait_ge(s.outputs, 16 * outs[0])
            else:
                sp.wait_ge(s.x1_turned, c)
                sp.wait_ge(s.x1_written, 16 * c)
            r = x_rows(c)
            sp.dma_start(xrow[0:r], t["x"][c * P:c * P + r]).then_inc(s.x_in, 16)
            if c == NCH - 1:
                sp.wait_ge(s.hgs_ready, NCH)
                out_dma(sp, t["out_S_p"], Sst)
            if c == NCH:
                sp.wait_ge(s.state_read, 8)
                out_dma(sp, t["out_C_s"].rearrange("p h b v -> p (h b) v"), C0)
                out_dma(sp, t["out_n_s"].rearrange("p h b -> p (h b)"), T[20])
                out_dma(sp, t["out_m_s"].rearrange("h b -> (h b)").unsqueeze(0), T[21][0:1])
                sp.wait_ge(s.state_read, 16)
                out_dma(sp, t["out_S_s"].rearrange("p h b v -> p (h b) v"), S0)
            sp.wait_ge(s.x1_ready, c + 1)
            sp.dma_start(x1_dram[c * P:c * P + r], xrow[0:r]).then_inc(s.x1_written, 16)
        sync_moe(sp)

    def samples_product(pe, banks, groups):
        for bank, g in zip(banks, groups):
            for k in range(KD):
                i = nc.tensor.matmul(PS[0:NS, bank, :], xT[:, k, NP_:NT], w_slot(g)[:, k, :], start=(k == 0), stop=(k == KD - 1))
        i.then_inc(s.zs_proj, 1)

    def samples_turn(pe, count, row, bank):
        pe.wait_ge(s.zs_row, count)
        for e in range(8):
            i = nc.tensor.transpose(PS[:, bank, e * NS:(e + 1) * NS], row[:, e * P:(e + 1) * P], ident[0:NS, 0:NS])
        i.then_inc(s.zs_turned, 1)

    def samples_rows(dve, tell, count, banks, row):
        dve.wait_ge(s.zs_proj, count)
        for n in range(2):
            i = nc.vector.tensor_copy(row[:, n * 512:(n + 1) * 512], PS[0:NS, banks[n], :])
        tell(i, s.zs_row)

    def samples_bias(dve, tell, count, bank):
        dve.wait_ge(s.zs_turned, count)
        e = 8 * (count - 1)
        tell(nc.vector.tensor_tensor(zs[:, e:e + 8], PS[:, bank, 0:64].rearrange("p (e b) -> p e b", e=8),
                                     b_cm[:, 8 + 2 * e:16 + 2 * e].unsqueeze(2).to_broadcast([P, 8, NS]), ALU.add), s.zs_read)

    def tensor_rest(pe, tokens_product):
        mm = nc.tensor.matmul
        hp = lambda bank, h: PS[:, bank, h * P:(h + 1) * P]
        pe.wait_ge(s.hg_k_ready, H)
        pe.wait_ge(s.hq_silu, H)

        def out_project(c, lhs_of):
            r = x_rows(c)
            for n in range(2):
                for e in range(8):
                    i = mm(PS[0:r, 6 + n, :], lhs_of(e), w_out[:, e, n * 512:(n + 1) * 512], start=(e == 0), stop=(e == 7))
            i.then_inc(s.mixed, 1)

        def turn_x1(c):
            r = x_rows(c)
            pe.wait_ge(s.x1_ready, c + 1)
            for k in range(KD):
                i = nc.tensor.transpose(PS[:, 4 + k // 4, (k % 4) * P:(k % 4) * P + r], xrow[0:r, k * P:(k + 1) * P], ident[0:r, 0:r])
            i.then_inc(s.x1_turned, 1)

        def route(c):
            r = x_rows(c)
            pe.wait_ge(s.x1_turned_read, c + 1)
            pe.wait_ge(s.mixer_in, 16 * 6)
            for k in range(KD):
                i = mm(PS[0:r, 5, 0:NG + NE], xTt[:, k, 0:r], w_r[:, k, :], start=(k == 0), stop=(k == KD - 1))
            i.then_inc(s.routed, 1)

        def turn_outputs(c):
            pe.wait_ge(s.on_ready, c + 1)
            for h in range(H):
                i = nc.tensor.transpose(hp(4, h), hmix[:, h], ident)
            i.then_inc(s.o_turned, 1)

        def project_in(c, part):
            if part == 0:
                if c == 0:
                    pe.wait_ge(s.w_in6, 16)
                    pe.wait_ge(s.zs_read, 1)
                else:
                    pe.wait_ge(s.gt_gated, c)
            if part == 2:
                if c == 0:
                    pe.wait_ge(s.w_in7, 16)
                else:
                    pe.wait_ge(s.kend_tm, c)
            bank, g = 1 - part // 2, 6 + part // 2
            for k in range(4 * (part % 2), 4 * (part % 2) + 4):
                i = mm(PS[:, bank, :], xT[:, k, c * P:(c + 1) * P], w_slot(g)[:, k, :], start=(k == 0), stop=(k == KD - 1))
            if part % 2:
                i.then_inc((s.gt_proj, s.i_proj)[part // 2], 1)

        def project_out(c, part):
            if part == 0:
                if c == 0:
                    pe.wait_ge(s.mixer_in, 16 * 6)
                    pe.wait_ge(s.c_ready, NCH)
                else:
                    pe.wait_ge(s.residual, c)
                pe.wait_ge(s.o_turned_read, c + 1)
            tok = slice(c * P, (c + 1) * P)
            n = part // 2
            for e in range(4 * (part % 2), 4 * (part % 2) + 4):
                lhs = CC[:, e, tok] if e < 4 else Q[:, e - 4, tok]
                i = mm(PS[:, 6 + n, :], lhs, w_out[:, e, n * 512:(n + 1) * 512], start=(e == 0), stop=(e == 7))
            if part == 3:
                i.then_inc(s.mixed, 1)

        for c in range(NCH):
            tok = slice(c * P, (c + 1) * P)
            for l in range(NLEV + 1):
                n = (NLEV + 1) * c + l
                if n == 0:
                    pe.wait_ge(s.h_turned_read, NCH)
                elif n == 1:
                    pe.wait_ge(s.s_ready, NCH)
                else:
                    pe.wait_ge(s.level_kept, n - 1)
                if l < NLEV:
                    xl = xlev[(NLEV * c + l) % 2]
                    pe.wait_ge(s.level_scaled, 2 * (NLEV * c + l + 1))
                for h in range(H):
                    if l < NLEV:
                        i = mm(hp(2 + n % 2, h), xl[:, h], xl[:, h], start=True, stop=True)
                    else:
                        i = mm(hp(2 + n % 2, h), K[:, h, tok], Q[:, h, tok], start=True, stop=True)
                i.then_inc(s.levels, 1)
                if l == 1 and c >= 3:
                    pe.wait_ge(s.hgs_ready, c)
                    route(c - 3)
                if l == 3 and c >= 1:
                    turn_outputs(c - 1)
                if l == 5:
                    pe.wait_ge(s.kend_ready, c + 1)
                    pe.wait_ge(s.i_ready, c + 1)
                    for h in range(H):
                        i = nc.tensor.transpose(hp(0, h), kend[:, h], ident)
                    i.then_inc(s.kend_turned, 1)
                if l == 6 and c >= 2:
                    pe.wait_ge(s.o_turned_read, c)
                    if c >= 3:
                        pe.wait_ge(s.logits_read, c - 2)
                    turn_x1(c - 2)
                if l < 4:
                    project_in(c, l)
                elif c >= 1:
                    project_out(c - 1, l - 4)
            pe.wait_ge(s.level_kept, (NLEV + 1) * (c + 1))
            pe.wait_ge(s.qg_ready, c + 1)
            if c == 0:
                pe.wait_ge(s.h_ready, NCH)
            if c >= 1:
                pe.wait_ge(s.o_turned_read, c)
            if c >= 2:
                pe.wait_ge(s.x1_turned_read, c - 1)
            for h in range(H):
                i = mm(hp(4, h), amat[:, h], ibuf[:, h], start=True, stop=(c == 0))
                if c >= 1:
                    i = mm(hp(4, h), qdec[:, h], Sst[:, h], start=False, stop=True)
            i.then_inc(s.o_num, 1)
            pe.wait_ge(s.kend_tm, c + 1)
            for h in range(H):
                i = mm(hp(5, h), kend[:, h], ibuf[:, h], start=True, stop=True)
            i.then_inc(s.s_upd, 1)
        pe.wait_ge(s.kend_tm, NCH)
        pe.wait_ge(s.gt_gated, NCH)
        samples_product(pe, (0, 1), (7, 6))
        pe.wait_ge(s.hgs_ready, NCH)
        route(NCH - 3)
        turn_outputs(NCH - 1)
        samples_turn(pe, 2, zrow[1], 0)
        for part in range(4):
            project_out(NCH - 1, part)
        pe.wait_ge(s.logits_read, NCH - 2)
        turn_x1(NCH - 2)
        route(NCH - 2)

        for kind in range(2):
            state = (C0, S0)[kind]
            if kind == 0:
                pe.wait_ge(s.zs_read, 2)
                pe.wait_ge(s.level_kept, (NLEV + 1) * NCH)
                pe.wait_ge(s.logits_read, NCH - 1)
            else:
                pe.wait_ge(s.srstd, 1)
            pe.wait_ge(s.state_in, 32)
            pe.wait_ge(s.dots_in, kind + 1)
            n = 2 - kind
            mm(PS[:, 0, 0:n * HB], ones, SC[:, 0:n * HB], start=True, stop=True)
            for e in range(HB):
                q = conv_ps[:, e:e + 1] if kind == 0 else T[2][:, e:e + 1]
                i = mm(PS[:, 0, 2 * HB + e:2 * HB + e + 1], state[:, e, :], q, start=True, stop=True)
            i.then_inc(s.dots, 1)
            pe.wait_ge(s.kv_in, kind + 1)
            nc.tensor.transpose(PS[0:HB, 1, 0:P], T[3], ident)
            i = nc.tensor.transpose(PS[0:HB, 1, P:2 * P], T[4], ident)
            i.then_inc(s.kv_turned, 1)
            pe.wait_ge(s.sq_in, kind + 1)
            mm(PS[:, 0, 96:128], ones, T[5], start=True, stop=True).then_inc(s.sq_sum, 1)
            pe.wait_ge(s.vdiag_ready, kind + 1)
            for n in range(8):
                bank = 2 + n % 4
                if n >= 4:
                    pe.wait_ge(s.state_read, 8 * kind + n - 3)
                i = mm(PS[:, bank, :], SC[0:HB, 24 * HB:24 * HB + P], vdiag[:, 4 * n:4 * n + 4, :].rearrange("p a v -> p (a v)"),
                       start=True, stop=True)
                i.then_inc(s.outer, 1)
            if kind == 0:
                pe.wait_ge(s.state_read, 8)
                turn_x1(NCH - 1)
                route(NCH - 1)
        pe.wait_ge(s.mixS_ready, 2)
        pe.wait_ge(s.residual, NCH)
        out_project(NCH, lambda e: mixS[:, e, :])
        turn_x1(NCH)
        route(NCH)
        tensor_moe(pe)

    def scalar_rest(act, link, tell):
        A = nc.scalar.activation
        by_h = lambda ap: ap.rearrange("p (h t) -> p h t", h=H)

        def ln_scale(c):
            r = x_rows(c)
            act.wait_ge(s.moments, c + 1)
            link(A(lstd[0:r], mv[0:r, 1:2], ACT.Ln, bias=ln_eps[0:r]))
            tell(A(lstd[0:r], lstd[0:r], ACT.Exp, scale=-0.5), s.lstd_ready)

        def x1_evacuate(c):
            r = x_rows(c)
            act.wait_ge(s.x1_turned, c + 1)
            if c >= 1:
                act.wait_ge(s.routed, c)
            for n in range(2):
                i = A(xTt[:, 4 * n:4 * n + 4, 0:r], by_h(PS[:, 4 + n, :])[:, :, 0:r], ACT.Copy)
                if n == 0:
                    link(i)
            tell(i, s.x1_turned_read)

        def turned_outputs(c):
            act.wait_ge(s.o_turned, c + 1)
            for h in range(H):
                i = A(Q[:, h, c * P:(c + 1) * P], PS[:, 4, h * P:(h + 1) * P], ACT.Copy, scale=g_mix[:, H + h:H + h + 1])
            tell(i, s.o_turned_read)

        def level_exp(n):
            if n < NLEV * NCH:
                act.wait_ge(s.level_arg, n + 1)
                tell(A(xlev[n % 2], xlev[n % 2], ACT.Exp), s.level_exp)

        def outputs_scale(c):
            act.wait_ge(s.o_num, c + 1)
            for h in range(H):
                i = A(hmix[:, h], PS[:, 4, h * P:(h + 1) * P], ACT.Square, accum_out=ssq[:, h:h + 1])
            link(i)
            link(A(rstd, ssq, ACT.Ln, scale=1.0 / P, bias=rms_eps))
            link(A(rstd, rstd, ACT.Exp, scale=-0.5))
            for h in range(H):
                i = A(hmix[:, h], PS[:, 4, h * P:(h + 1) * P], ACT.Copy, scale=rstd[:, h:h + 1])
            tell(i, s.o_scaled)

        level_exp(0)
        level_exp(1)
        for c in range(NCH):
            if c >= 1:
                outputs_scale(c - 1)
            act.wait_ge(s.kend_arg, c + 1)
            tell(A(kend, kend, ACT.Exp), s.kend_exp)
            for l in range(2, NLEV + 2):
                level_exp(NLEV * c + l)
                if l == 2 and c >= 2:
                    ln_scale(c - 2)
                if l == 3:
                    tell(A(qdec, G[:, :, c * P:(c + 1) * P], ACT.Exp), s.g_exp)
                if l == 4 and c >= 1:
                    turned_outputs(c - 1)
                if l == 5:
                    act.wait_ge(s.gt_biased, c + 1)
                    tell(A(PS[:, 1, :], gtb.rearrange("p h v -> p (h v)"), ACT.Exp, scale=-1.0), s.gt_exp)
                if l == 8 and c >= 2:
                    x1_evacuate(c - 2)
        outputs_scale(NCH - 1)
        act.wait_ge(s.zs_proj, 2)
        act.dma_start(C0, t["C0"].rearrange("p h b v -> p (h b) v")).then_inc(s.state_in, 16)
        act.dma_start(S0, t["S0"].rearrange("p h b v -> p (h b) v")).then_inc(s.state_in, 16)
        ln_scale(NCH - 2)
        turned_outputs(NCH - 1)
        x1_evacuate(NCH - 2)
        act.wait_ge(s.sgates_arg, 1)
        tell(A(SC[:, 8 * HB:11 * HB], SC[:, 8 * HB:11 * HB], ACT.Exp), s.sgates_exp)
        for kind in range(2):
            act.wait_ge(s.ogate_arg, kind + 1)
            tell(A(T[11], T[12], ACT.Exp, scale=-1.0), s.ogate_exp)
            if kind == 0:
                ln_scale(NCH - 1)
            act.wait_ge(s.sq_sum, kind + 1)
            link(A(T[13], PS[:, 0, 96:128], ACT.Ln, scale=1.0 / P, bias=rms_eps))
            tell(A(T[13], T[13], ACT.Exp, scale=-0.5), s.srstd)
            if kind == 0:
                x1_evacuate(NCH - 1)
                act.wait_ge(s.sgates_arg, 2)
                tell(A(T[14], T[14], ACT.Exp), s.sgates_exp)
        ln_scale(NCH)
        x1_evacuate(NCH)
        scalar_moe(act, link, tell)

    def pool_rest(pool, link, tell):
        g = nc.gpsimd

        def ln_gain(c):
            r = x_rows(c)
            pool.wait_ge(s.normed, c + 1)
            if c == 0:
                pool.wait_ge(s.mixer_in, 16 * 6)
            link(g.tensor_tensor(xrow[0:r], xrow[0:r], ln_gb[0:r, 0], ALU.mult))

        def ln_shift(c):
            r = x_rows(c)
            tell(g.tensor_tensor(xrow[0:r], xrow[0:r], ln_gb[0:r, 1], ALU.add), s.x1_ready)

        def level_scale(n):
            c, l = divmod(n, NLEV)
            if c == NCH:
                return
            b = LEVELS[l]
            pool.wait_ge(s.level_exp, n + 1)
            for half, src in ((0, K), (1, Q)):
                x = xlev[n % 2].rearrange("p h (n w b) -> p h n w b", w=2, b=b)[:, :, :, half]
                y = src[:, :, c * P:(c + 1) * P].rearrange("p h (n w b) -> p h n w b", w=2, b=b)[:, :, :, half]
                tell(g.tensor_tensor(x, x, y, ALU.mult), s.level_scaled)

        level_scale(0)
        level_scale(1)
        for c in range(NCH):
            pool.wait_ge(s.kend_exp, c + 1)
            tell(g.tensor_tensor(kend, kend, K[:, :, c * P:(c + 1) * P], ALU.mult), s.kend_ready)
            for l in range(2, NLEV + 2):
                level_scale(NLEV * c + l)
                if l == 4 and c >= 2:
                    ln_gain(c - 2)
                if l == 5 and c >= 2:
                    ln_shift(c - 2)
        for c in range(NCH - 2, NTT):
            ln_gain(c)
            ln_shift(c)
        pool_moe(pool, link, tell)

    def vector_rest(dve, link, tell):
        v = nc.vector
        by_h = lambda ap: ap.rearrange("p (h t) -> p h t", h=H)
        link(v.memset(R[:, 180:360], 0.0))
        dve.wait_ge(s.h_turned, NCH)
        dve.wait_ge(s.masks_made, 1)

        def residual_sum(c):
            r = x_rows(c)
            dve.wait_ge(s.mixed, c + 1)
            dve.wait_ge(s.x_in, 16 * (c + 1))
            for n in range(2):
                half = xrow[0:r, n * 512:(n + 1) * 512]
                i = v.scalar_tensor_tensor(half, half, ALPHA, PS[0:r, 6 + n, :], ALU.mult, ALU.add)
            tell(i, s.residual)
            for n in range(2):
                i = v.bn_stats(stats[0:r, n], xrow[0:r, n * 512:(n + 1) * 512])
            link(i)
            tell(v.bn_aggr(mv[0:r], stats[0:r]), s.moments)

        def residual_norm(c):
            r = x_rows(c)
            dve.wait_ge(s.lstd_ready, c + 1)
            tell(v.tensor_scalar(xrow[0:r], xrow[0:r], mv[0:r, 0:1], lstd[0:r], ALU.subtract, ALU.mult), s.normed)

        def logits(c):
            r = x_rows(c)
            dve.wait_ge(s.routed, c + 1)
            dve.wait_ge(s.mixer_in, 16 * 6)
            tell(v.tensor_tensor(LG[0:r, c], PS[0:r, 5, 0:NG + NE], b_r[0:r], ALU.add), s.logits_read)

        def sample_state(kind, state, decay):
            link(v.tensor_tensor(state, state, decay.unsqueeze(2).to_broadcast([P, HB, P]), ALU.mult))
            for n in range(8):
                dve.wait_ge(s.outer, 8 * kind + n + 1)
                part = state[:, 4 * n:4 * n + 4, :]
                tell(v.tensor_tensor(part, part, by_h(PS[:, 2 + n % 4, :]), ALU.add), s.state_read)

        def outputs_gate(c):
            dve.wait_ge(s.o_scaled, c + 1)
            tell(v.tensor_tensor(hmix, hmix, gtb, ALU.mult), s.on_ready)

        def level_arg(n):
            c, l = divmod(n, NLEV)
            if c == NCH:
                return
            b = LEVELS[l]
            if n >= 2:
                dve.wait_ge(s.levels, (NLEV + 1) * ((n - 2) // NLEV) + (n - 2) % NLEV + 1)
            gv = G[:, :, c * P:(c + 1) * P].rearrange("p h (n w b) -> p h n w b", w=2, b=b)
            xv = xlev[n % 2].rearrange("p h (n w b) -> p h n w b", w=2, b=b)
            ref = gv[:, :, :, 0, b - 1:b].to_broadcast([P, H, P // (2 * b), b])
            v.tensor_tensor(xv[:, :, :, 0], ref, gv[:, :, :, 0], ALU.subtract)
            tell(v.tensor_tensor(xv[:, :, :, 1], gv[:, :, :, 1], ref, ALU.subtract), s.level_arg)

        def keep_level(c, l):
            n = (NLEV + 1) * c + l
            dve.wait_ge(s.levels, n + 1)
            tell(v.copy_predicated(amat, msk[:, l:l + 1, :].to_broadcast([P, H, P]), by_h(PS[:, 2 + n % 2, :])), s.level_kept)

        def state_update(c):
            dve.wait_ge(s.s_upd, c + 1)
            for h in range(H):
                ps = PS[:, 5, h * P:(h + 1) * P]
                if c == 0:
                    i = v.tensor_copy(Sst[:, h], ps)
                else:
                    i = v.scalar_tensor_tensor(Sst[:, h], Sst[:, h], egend[:, h:h + 1], ps, ALU.mult, ALU.add)
            tell(i, s.hgs_ready)

        level_arg(0)
        level_arg(1)
        samples_rows(dve, tell, 1, (0, 1), zrow[0])
        samples_bias(dve, tell, 1, 0)
        for c in range(NCH):
            tok = slice(c * P, (c + 1) * P)
            if c >= 1:
                state_update(c - 1)
            tell(v.tensor_tensor(kend, G[:, :, c * P + P - 1:(c + 1) * P].to_broadcast([P, H, P]), G[:, :, tok], ALU.subtract), s.kend_arg)
            link(v.memset(amat, 0.0))
            for l in range(2, NLEV + 2):
                level_arg(NLEV * c + l)
                keep_level(c, l - 2)
                if l == 2 and c >= 2:
                    residual_sum(c - 2)
                if l == 3:
                    if c >= 1:
                        outputs_gate(c - 1)
                    if c >= 3:
                        logits(c - 3)
                if l == 4 and c >= 2:
                    residual_norm(c - 2)
                if l == 5:
                    if c == 0:
                        dve.wait_ge(s.mixer_in, 16 * 6)
                    dve.wait_ge(s.i_proj, c + 1)
                    tell(v.tensor_tensor(ibuf, by_h(PS[:, 0, :]), by_h(bias[:, 0:512]), ALU.add), s.i_ready)
                    dve.wait_ge(s.gt_proj, c + 1)
                    tell(v.tensor_tensor(gtb, by_h(PS[:, 1, :]), by_h(bias[:, 512:1024]), ALU.add), s.gt_biased)
                if l == 6:
                    dve.wait_ge(s.g_exp, c + 1)
                    link(v.tensor_copy(egend, qdec[:, :, P - 1]))
                    tell(v.tensor_tensor(qdec, qdec, Q[:, :, tok], ALU.mult), s.qg_ready)
                    dve.wait_ge(s.kend_turned, c + 1)
                    tell(v.tensor_copy(kend, by_h(PS[:, 0, :])), s.kend_tm)
                if l == 7:
                    dve.wait_ge(s.gt_exp, c + 1)
                    link(v.tensor_scalar(PS[:, 1, :], PS[:, 1, :], 1.0, None, ALU.add))
                    link(v.reciprocal(PS[:, 1, :], PS[:, 1, :]))
                    tell(v.tensor_tensor(gtb, gtb, by_h(PS[:, 1, :]), ALU.mult), s.gt_gated)
            keep_level(c, NLEV)
        samples_rows(dve, tell, 2, (0, 1), zrow[1])
        state_update(NCH - 1)
        residual_sum(NCH - 2)
        outputs_gate(NCH - 1)
        logits(NCH - 3)
        residual_norm(NCH - 2)
        samples_bias(dve, tell, 2, 0)
        logits(NCH - 2)

        dve.wait_ge(s.mixer_in, 16 * 6)
        dve.wait_ge(s.zs_read, 2)
        a, dd, dec, nm = T[7], T[8], T[9], T[10]
        hb = by_hb
        li, lf, mb = gs[:, :, 0], gs[:, :, 1], gs[:, :, 2]
        link(v.tensor_tensor(hb(a), li, lf, ALU.subtract))
        link(v.tensor_tensor(hb(T[6]), hb(a), mb, ALU.max))
        link(v.tensor_tensor(dd, a, T[6], ALU.subtract))
        link(v.tensor_tensor(hb(dec), mb, hb(T[6]), ALU.subtract))
        link(v.tensor_tensor(hb(T[21]), hb(T[6]), lf, ALU.add))
        tell(v.tensor_scalar(nm, T[21], -1.0, None, ALU.mult), s.sgates_arg)
        qs, ks = conv_ps[:, 0:HB], conv_ps[:, HB:2 * HB]
        flat = lambda ap: ap.rearrange("p h b -> p (h b)")
        for kind in range(2):
            state = (C0, S0)[kind]
            if kind == 0:
                link(v.tensor_tensor(T[0], qs, ks, ALU.mult))
                tell(v.tensor_tensor(T[1], qs, n0, ALU.mult), s.dots_in)
                dve.wait_ge(s.sgates_exp, 1)
                link(v.tensor_scalar(dd, dd, KSCALE, None, ALU.mult))
                link(v.tensor_tensor(T[3], ks, dd, ALU.mult))
                tell(v.tensor_copy(T[4], flat(zs[:, 0:4])), s.kv_in)
                link(v.tensor_tensor(T[20], n0, dec, ALU.mult))
                link(v.tensor_tensor(T[20], T[20], T[3], ALU.add))
                tell(v.tensor_copy(T[12], flat(zs[:, 4:8])), s.ogate_arg)
                residual_sum(NCH - 1)
                residual_norm(NCH - 1)
                dve.wait_ge(s.dots, 1)
                link(v.tensor_tensor(T[15], PS[:, 0, 0:HB], dd, ALU.mult))
                link(v.tensor_tensor(T[16], PS[:, 0, HB:2 * HB], dec, ALU.mult))
                link(v.tensor_tensor(T[16], T[16], T[15], ALU.add))
                link(v.tensor_scalar(T[17], T[16], -1.0, None, ALU.mult))
                link(v.tensor_tensor(T[16], T[16], T[17], ALU.max))
                link(v.tensor_tensor(T[16], T[16], nm, ALU.max))
                link(v.reciprocal(T[16], T[16]))
                link(v.tensor_tensor(T[17], PS[:, 0, 2 * HB:3 * HB], dec, ALU.mult))
                link(v.tensor_tensor(T[15], T[15], T[4], ALU.mult))
                link(v.tensor_tensor(T[15], T[15], T[17], ALU.add))
                link(v.tensor_tensor(T[15], T[15], T[16], ALU.mult))
                dve.wait_ge(s.ogate_exp, 1)
                link(v.tensor_scalar(T[11], T[11], 1.0, None, ALU.add))
                link(v.reciprocal(T[11], T[11]))
                link(v.tensor_tensor(T[15], T[15], T[11], ALU.mult))
                decay = dec
            else:
                kS, qS = K[:, :, NP_:NT], Q[:, :, NP_:NT]
                dve.wait_ge(s.outer, 8)
                tell(v.tensor_copy(hb(T[14]), G[:, :, NP_:NT]), s.sgates_arg)
                link(v.tensor_tensor(hb(T[0]), qS, kS, ALU.mult))
                dve.wait_ge(s.sgates_exp, 2)
                tell(v.tensor_tensor(hb(T[2]), qS, hb(T[14]), ALU.mult), s.dots_in)
                link(v.tensor_copy(hb(T[3]), kS))
                tell(v.tensor_copy(T[4], flat(zs[:, 8:12])), s.kv_in)
                tell(v.tensor_copy(T[12], flat(zs[:, 12:16])), s.ogate_arg)
                dve.wait_ge(s.dots, 2)
                link(v.tensor_tensor(T[15], PS[:, 0, 0:HB], T[4], ALU.mult))
                link(v.tensor_tensor(T[15], T[15], PS[:, 0, 2 * HB:3 * HB], ALU.add))
                dve.wait_ge(s.ogate_exp, 2)
                link(v.tensor_scalar(T[11], T[11], 1.0, None, ALU.add))
                link(v.reciprocal(T[11], T[11]))
                link(v.tensor_tensor(T[11], T[11], T[12], ALU.mult))
                decay = T[14]
            tell(v.tensor_tensor(T[5], T[15], T[15], ALU.mult), s.sq_in)
            dve.wait_ge(s.kv_turned, kind + 1)
            link(v.tensor_copy(SC[0:HB, 24 * HB:24 * HB + P], PS[0:HB, 1, 0:P]))
            tell(v.tensor_tensor(vdiag, PS[0:HB, 1, P:2 * P].unsqueeze(1).to_broadcast([HB, HB, P]),
                                 ident[0:HB, 0:HB].unsqueeze(2).to_broadcast([HB, HB, P]), ALU.mult), s.vdiag_ready)
            dve.wait_ge(s.srstd, kind + 1)
            mix = flat(mixS[:, 4 * kind:4 * kind + 4])
            link(v.tensor_tensor(mix, T[15], T[13], ALU.mult))
            if kind == 1:
                link(v.tensor_tensor(mix, mix, T[11], ALU.mult))
            gain = g_mix[:, 4 * kind:4 * kind + 4].unsqueeze(2).to_broadcast([P, H, NS])
            tell(v.tensor_tensor(mixS[:, 4 * kind:4 * kind + 4], mixS[:, 4 * kind:4 * kind + 4], gain, ALU.mult), s.mixS_ready)
            sample_state(kind, state, decay)
            if kind == 0:
                logits(NCH - 1)
        residual_sum(NCH)
        residual_norm(NCH)
        logits(NCH)
        vector_moe(dve, link, tell)

    def pairs_loop(eng, step):
        for i in range(2):
            step(0, i, True, False)
        with eng.Fori(1, TILES // 2 - 1) as pair:
            for i in range(2):
                step(pair, i, False, False)
        for i in range(2):
            step(TILES // 2 - 1, i, False, True)

    early_outs = []

    def sync_moe(sp):
        early_outs.append(outs[0])
        sp.wait_ge(s.outputs, 16 * early_outs[0])
        sp.wait_ge(s.x1_written, 16 * NTT)
        sp.dma_start(XF[:, 0:8 * D].rearrange("p (c n) -> p c n", c=8),
                     x1_dram[0:NP_].rearrange("(c p) n -> p c n", p=P)).then_inc(s.x1_back, 16)
        sp.dma_start(x1_keep[8][0:NS], x1_dram[NP_:NT]).then_inc(s.x1_back, 16)
        sp.wait_ge(s.mixed, NTT)
        sp.wait_ge(s.tiles_known, 1)
        sp.dma_start(ln2_gb, t["ln2"].partition_broadcast(P)).then_inc(s.ln2_in, 16)
        wg = t["w_gate"].rearrange("e (p k) f -> e p k f", k=KD)
        wu = t["w_up"].rearrange("e (p k) f -> e p k f", k=KD)
        wd = t["w_down"].rearrange("e (p k) n -> e p k n", k=2)

        def load_up(pair, i, expert):
            for n, w in enumerate((wg, wu)):
                sp.dma_start(w_gu[i][:, :, n], w[bass.ds(expert, 1)].rearrange("e p k f -> p (e k) f")).then_inc((s.w_gu_in0, s.w_gu_in1)[i], 16)

        def load_down(pair, i, expert):
            sp.dma_start(w_dn[i], wd[bass.ds(expert, 1)].rearrange("e p k n -> p (e k) n")).then_inc((s.w_dn_in0, s.w_dn_in1)[i], 16)

        def expert_of(pair, i):
            return sp.value_load(tile_expert[0:1, bass.ds(pair * 2 + i, 1)].bitcast(I32), min_val=0, max_val=NE - 1)

        for i in range(2):
            e = expert_of(0, i)
            load_up(0, i, e)
            load_down(0, i, e)

        def step(pair, i, first, last):
            done = pair * 2 + (i + 1)
            if not last:
                e = expert_of(pair + 1, i)
                sp.wait_ge(s.up_done, done)
                load_up(pair + 1, i, e)
                sp.wait_ge(s.down_done, done)
                load_down(pair + 1, i, e)
            sp.wait_ge(s.y_read, done * 2)
            sp.dma_start(y_slots[bass.ds((pair * 2 + i) * P, P)], ysb[i]).then_inc((s.y_out0, s.y_out1)[i], 16)

        pairs_loop(sp, step)
        for c in range(NTT):
            r = x_rows(c)
            sp.wait_ge(s.y_ready, c + 1)
            out_dma(sp, t["out_y"][c * P:c * P + r], x1_keep[c][0:r])
        sp.wait_ge(s.outputs, 16 * outs[0])

    def tensor_moe(pe):
        mm = nc.tensor.matmul
        pe.wait_ge(s.esum_ready, 1)
        pe.wait_ge(s.x1_turned_read, NTT)
        mm(PS[:, 0, 0:NTT * NE], const("before"), esum.rearrange("p i e -> p (i e)"), start=True, stop=True)
        mm(PS[:, 1, 0:NTT * NE], ones, esum.rearrange("p i e -> p (i e)"), start=True, stop=True).then_inc(s.ranked, 1)
        pe.wait_ge(s.onehots, 1)
        for q in range(2 * NTT):
            i = mm(PS[:, 2, 0:64], oh_lo[:, q], oh_hi[:, q].rearrange("p w n -> p (w n)"), start=(q == 0), stop=(q == 2 * NTT - 1))
        i.then_inc(s.slots, 1)

        def turn_x(pair, i):
            pe.wait_ge((s.xg_in0, s.xg_in1)[i], pair * 16 + 16)
            for k in range(KD):
                m = nc.tensor.transpose(PS[:, k // 4, (k % 4) * P:(k % 4 + 1) * P], xg[i][:, k:D:KD], ident)
            m.then_inc(s.xg_turned, 1)

        turn_x(0, 0)

        def step(pair, i, first, last):
            n = pair * 2 + i
            pe.wait_ge(s.xgT_ready, n * 2 + 2)
            pe.wait_ge((s.w_gu_in0, s.w_gu_in1)[i], pair * 32 + 32)
            if first:
                pe.wait_ge(s.tiles_known, 1)
                pe.wait_ge(s.logits_read, NTT)
            else:
                pe.wait_ge(s.hid_ready, n - 1)
            for k in range(KD):
                m = mm(PS[:, 2 + i, :], xgT[i][:, k], w_gu[i][:, k].rearrange("p g f -> p (g f)"), start=(k == 0), stop=(k == KD - 1))
            m.then_inc(s.up_done, 1)
            if not (last and i == 1):
                turn_x(pair + i, 1 - i)
            pe.wait_ge(s.hid_ready, n + 1)
            if not (first and i == 0):
                pe.wait_ge(s.hidT_ready, n)
            for k in range(2):
                m = nc.tensor.transpose(PS[:, 4, k * P:(k + 1) * P], hid[:, k:FF:2], ident)
            m.then_inc(s.hid_turned, 1)
            pe.wait_ge(s.hidT_ready, n + 1)
            pe.wait_ge((s.w_dn_in0, s.w_dn_in1)[i], pair * 16 + 16)
            if first and i == 0:
                pe.wait_ge(s.residual, NTT)
            else:
                pe.wait_ge(s.y_read, n * 2)
            for half in range(2):
                for k in range(2):
                    m = mm(PS[:, 5 + half, :], hidT[:, k], w_dn[i][:, k, half * 512:(half + 1) * 512], start=(k == 0), stop=(k == 1))
            m.then_inc(s.down_done, 1)

        pairs_loop(pe, step)

    def scalar_moe(act, link, tell):
        A = nc.scalar.activation
        act.wait_ge(s.route_arg, 1)
        tell(A(gexp, gexp, ACT.Exp), s.route_exp)
        act.wait_ge(s.route_arg, 2)
        tell(A(e2, e2, ACT.Exp), s.route_exp)

        def x_half(pair, i, first):
            n = pair * 2 + i
            act.wait_ge(s.xg_turned, n + 1)
            if not first:
                act.wait_ge(s.up_done, n - 1)
            A(xgT[i][:, 0:4], PS[:, 0, :].rearrange("p (k t) -> p k t", k=4), ACT.Copy).then_inc(s.xgT_ready, 1)

        x_half(0, 0, True)

        def step(pair, i, first, last):
            n = pair * 2 + i
            act.wait_ge(s.up_done, n + 1)
            if not (first and i == 0):
                act.wait_ge(s.hid_ready, n)
            A(silu, PS[:, 2 + i, 0:FF], ACT.Silu).then_inc(s.silu_ready, 1)
            if not (last and i == 1):
                x_half(pair + i, 1 - i, first and i == 0)
            act.wait_ge(s.down_done, n + 1)
            if not first:
                act.wait_ge((s.y_out0, s.y_out1)[i], pair * 16)
            A(ysb[i][:, 0:512], PS[:, 5, :], ACT.Copy).then_inc(s.y_read, 1)

        pairs_loop(act, step)
        nc.scalar.preload_act_table_set("natural_log_exp_and_others")
        for c in range(NTT):
            r = x_rows(c)
            act.wait_ge(s.moments, NTT + c + 1)
            link(A(fsd[0:r], fmv[0:r, 1:2], ACT.Ln, bias=ln_eps[0:r]))
            tell(A(fsd[0:r], fsd[0:r], ACT.Exp, scale=-0.5), s.lstd_ready)

    def pool_moe(pool, link, tell):
        g = nc.gpsimd
        pool.wait_ge(s.tiles_known, 1)
        pool.wait_ge(s.x1_written, 16 * NTT)

        pool.wait_ge(s.routed, NTT)
        pool.wait_ge(s.outputs, 16 * early_outs[0])
        pool.wait_ge(s.normed, NTT)
        for n in range(TILES):
            if n >= 2:
                pool.wait_ge(s.xg_turned, n - 1)
                pool.wait_ge(s.hid_ready, n - 1)
            off = bass.IndirectOffsetOnAxis(slot_tok[:, n:n + 1].bitcast(U32), 0)
            g.indirect_dma_start(xg[n % 2], None, x1_dram, off).then_inc((s.xg_in0, s.xg_in1)[n % 2], 16)
            g.tensor_copy(gate_c[n % 2], slot_gate[:, n:n + 1]).then_inc(s.gate_ready, 1)
        pool.wait_ge(s.y_out0, 16 * (TILES // 2))
        pool.wait_ge(s.y_out1, 16 * (TILES // 2))
        pool.wait_ge(s.slots, 1)
        pool.wait_ge(s.ln2_in, 16)

        def affine(c):
            r = x_rows(c)
            pool.wait_ge(s.normed, NTT + c + 1)
            link(g.tensor_tensor(x1_keep[c][0:r], x1_keep[c][0:r], ln2_gb[0:r, 0], ALU.mult))
            tell(g.tensor_tensor(x1_keep[c][0:r], x1_keep[c][0:r], ln2_gb[0:r, 1], ALU.add), s.y_ready)

        for c in range(NTT):
            r = x_rows(c)
            if c >= 4:
                pool.wait_ge(s.y_added, c - 3)
            for k, dst in ((0, ya), (1, yb)):
                off = bass.IndirectOffsetOnAxis(pos_i[0:r, k * NTT + c:k * NTT + c + 1].bitcast(U32), 0)
                g.indirect_dma_start(dst[c % 4][0:r], None, y_slots, off).then_inc((s.yg_in0, s.yg_in1, s.yg_in2, s.yg_in3)[c % 4], 16)
            if c >= 2:
                affine(c - 2)
        affine(NTT - 2)
        affine(NTT - 1)

    def vector_moe(dve, link, tell):
        v = nc.vector
        last4 = lambda ap: ap.unsqueeze(2).to_broadcast([P, NTT, 4])
        valid = const("valid")
        dve.wait_ge(s.mixed, NTT)

        def first_hot(out, vals, top):
            link(v.tensor_tensor(scr, vals, last4(top), ALU.is_ge))
            link(v.tensor_tensor(scr, scr, const("first").unsqueeze(1).to_broadcast([P, NTT, 4]), ALU.mult))
            link(v.tensor_reduce(s2, scr, X, ALU.max))
            link(v.tensor_tensor(out, scr, last4(s2), ALU.is_equal))

        lg = LG[:, :, 0:NG]
        link(v.tensor_reduce(gmax, lg, X, ALU.max))
        tell(v.tensor_tensor(gexp, lg, last4(gmax), ALU.subtract), s.route_arg)
        first_hot(ghot, lg, gmax)
        dve.wait_ge(s.route_exp, 1)
        link(v.tensor_reduce(gden, gexp, X, ALU.add))
        link(v.reciprocal(gden, gden))
        le = LG[:, :, NG:].rearrange("p i (g j) -> p i g j", g=NG)
        link(v.tensor_tensor(le_m, le, ghot.unsqueeze(3).to_broadcast([P, NTT, NG, NJ]), ALU.mult))
        link(v.tensor_reduce(leg, le_m.rearrange("p i g j -> p i j g"), X, ALU.add))
        link(v.tensor_reduce(v1, leg, X, ALU.max))
        first_hot(hot[0], leg, v1)
        link(v.scalar_tensor_tensor(leg2, hot[0], -BIG, leg, ALU.mult, ALU.add))
        link(v.tensor_reduce(v2, leg2, X, ALU.max))
        first_hot(hot[1], leg2, v2)
        tell(v.tensor_tensor(e2, v2, v1, ALU.subtract), s.route_arg)
        for k in range(2):
            e4 = ex[k].rearrange("p i (g j) -> p i g j", g=NG)
            link(v.tensor_tensor(e4, ghot.unsqueeze(3).to_broadcast([P, NTT, NG, NJ]),
                                 hot[k].unsqueeze(2).to_broadcast([P, NTT, NG, NJ]), ALU.mult))
            link(v.tensor_tensor(ex[k], ex[k], valid.unsqueeze(2).to_broadcast([P, NTT, NE]), ALU.mult))
        tell(v.tensor_tensor(esum, ex[0], ex[1], ALU.add), s.esum_ready)
        dve.wait_ge(s.route_exp, 2)
        link(v.tensor_scalar(s2, e2, 1.0, None, ALU.add))
        link(v.reciprocal(s2, s2))
        link(v.tensor_tensor(s2, s2, gden, ALU.mult))
        link(v.tensor_tensor(wts[:, 0], s2, valid, ALU.mult))
        link(v.tensor_tensor(wts[:, 1], wts[:, 0], e2, ALU.mult))
        dve.wait_ge(s.ranked, 1)
        link(v.tensor_copy(tot, PS[:, 1, 0:NTT * NE].rearrange("p (i e) -> p i e", e=NE)))
        link(v.memset(cnt[:, 0], 0.0))
        for c in range(1, NTT):
            link(v.tensor_tensor(cnt[:, c], cnt[:, c - 1], tot[:, c - 1], ALU.add))
        link(v.tensor_tensor(n_e, cnt[:, NTT - 1], tot[:, NTT - 1], ALU.add))
        link(v.tensor_tensor(slotp, cnt, PS[:, 0, 0:NTT * NE].rearrange("p (i e) -> p i e", e=NE), ALU.add))
        link(v.tensor_tensor(cmp9, n_e.unsqueeze(2).to_broadcast([P, NE, NTT]),
                             const("full").unsqueeze(1).to_broadcast([P, NE, NTT]), ALU.is_gt))
        link(v.tensor_reduce(nt_e, cmp9, X, ALU.add))
        link(v.tensor_tensor_scan(end_e, ones[:, 0:NE], nt_e, 0.0, ALU.mult, ALU.add))
        link(v.tensor_tensor(base_e, end_e, nt_e, ALU.subtract))
        link(v.tensor_scalar(base_e, base_e, float(P), None, ALU.mult))
        link(v.tensor_tensor(slotp, slotp, base_e.unsqueeze(1).to_broadcast([P, NTT, NE]), ALU.add))
        for k in range(2):
            link(v.tensor_tensor(ex[k], ex[k], slotp, ALU.mult))
            link(v.tensor_reduce(pos[:, k * NTT:(k + 1) * NTT], ex[k], X, ALU.add))
        link(v.tensor_copy(pos_i, pos))
        link(v.tensor_scalar(hi_i, pos_i, 7, None, ALU.arith_shift_right))
        link(v.tensor_scalar(lo_i, pos_i, P - 1, None, ALU.bitwise_and))
        link(v.tensor_copy(hi_f, hi_i))
        link(v.tensor_copy(lo_f, lo_i))
        link(v.tensor_tensor(cmp32, const("lane")[:, 0:TILES].unsqueeze(2).to_broadcast([P, TILES, NE]),
                             end_e.unsqueeze(1).to_broadcast([P, TILES, NE]), ALU.is_ge))
        link(v.tensor_reduce(slot_gate, cmp32, X, ALU.add))
        link(v.tensor_scalar(slot_gate, slot_gate, float(NE - 1), None, ALU.min))
        link(v.tensor_copy(tile_expert.bitcast(I32), slot_gate))
        q18 = 2 * NTT
        link(v.tensor_tensor(oh_lo, const("lane").unsqueeze(1).to_broadcast([P, q18, P]), lo_f.unsqueeze(2).to_broadcast([P, q18, P]), ALU.is_equal))
        link(v.tensor_tensor(oh_hi[:, :, 0], const("lane")[:, 0:TILES].unsqueeze(1).to_broadcast([P, q18, TILES]),
                             hi_f.unsqueeze(2).to_broadcast([P, q18, TILES]), ALU.is_equal))
        link(v.tensor_tensor(oh_hi[:, :, 1], oh_hi[:, :, 0], wts.rearrange("p w i -> p (w i)").unsqueeze(2).to_broadcast([P, q18, TILES]), ALU.mult))
        for k in range(2):
            part = oh_hi[:, k * NTT:(k + 1) * NTT, 0]
            i = v.tensor_tensor(part, part, const("token").unsqueeze(2).to_broadcast([P, NTT, TILES]), ALU.mult)
        tell(i, s.onehots)
        dve.wait_ge(s.slots, 1)
        link(v.tensor_copy(slot_tok, PS[:, 2, 0:32]))
        tell(v.tensor_copy(slot_gate, PS[:, 2, 32:64]), s.tiles_known)

        def x_half(pair, i, first):
            n = pair * 2 + i
            dve.wait_ge(s.xg_turned, n + 1)
            if not first:
                dve.wait_ge(s.up_done, n - 1)
            v.tensor_copy(xgT[i][:, 4:8], PS[:, 1, :].rearrange("p (k t) -> p k t", k=4)).then_inc(s.xgT_ready, 1)

        x_half(0, 0, True)

        def step(pair, i, first, last):
            n = pair * 2 + i
            dve.wait_ge(s.silu_ready, n + 1)
            dve.wait_ge(s.gate_ready, n + 1)
            if not (first and i == 0):
                dve.wait_ge(s.hid_turned, n)
            v.scalar_tensor_tensor(hid, silu, gate_c[i], PS[:, 2 + i, FF:2 * FF], ALU.mult, ALU.mult).then_inc(s.hid_ready, 1)
            if not (last and i == 1):
                x_half(pair + i, 1 - i, first and i == 0)
            dve.wait_ge(s.hid_turned, n + 1)
            if not (first and i == 0):
                dve.wait_ge(s.down_done, n)
            v.tensor_copy(hidT, PS[:, 4, 0:2 * P].rearrange("p (k t) -> p k t", k=2)).then_inc(s.hidT_ready, 1)
            dve.wait_ge(s.down_done, n + 1)
            if not first:
                dve.wait_ge((s.y_out0, s.y_out1)[i], pair * 16)
            v.tensor_copy(ysb[i][:, 512:1024], PS[:, 6, :]).then_inc(s.y_read, 1)

        pairs_loop(dve, step)

        dve.wait_ge(s.x1_back, 32)
        for c in range(NTT):
            r = x_rows(c)
            x = x1_keep[c][0:r]
            dve.wait_ge((s.yg_in0, s.yg_in1, s.yg_in2, s.yg_in3)[c % 4], 32 * (c // 4 + 1))
            link(v.scalar_tensor_tensor(x, x, ALPHA, ya[c % 4][0:r], ALU.mult, ALU.add))
            tell(v.tensor_tensor(x, x, yb[c % 4][0:r], ALU.add), s.y_added)
            st = fst.rearrange("p (g n) -> p g n", g=2)
            for n in range(2):
                i = v.bn_stats(st[0:r, n], x[:, n * 512:(n + 1) * 512])
            link(i)
            tell(v.bn_aggr(fmv[0:r], st[0:r]), s.moments)
            dve.wait_ge(s.lstd_ready, NTT + c + 1)
            tell(v.tensor_scalar(x, x, fmv[0:r, 0:1], fsd[0:r], ALU.subtract, ALU.mult), s.normed)

    block = ctx.enter_context(nc.Block())

    @block.sync
    def _(sp):
        sp.dma_start(wgt, t["wg"]).then_inc(s.params_in, 16)
        sp.dma_start(xT[:, 0:4], t["xT"][:, 0:4]).then_inc(s.xT_in, 16)
        sp.dma_start(xT[:, 4:8], t["xT"][:, 4:8]).then_inc(s.xT_in2, 16)
        sp.dma_start(bias, t["b_row"][:, 0:1024].partition_broadcast(P).rearrange("p a n -> p (a n)")).then_inc(s.bias_in, 16)
        for g in range(7):
            if g == 3:
                sp.wait_ge(s.projected, last_piece(3))
            if g == 4:
                sp.wait_ge(s.projected, last_piece(7))
            if g == 5:
                sp.wait_ge(s.projected, last_piece(11))
            if g == 6:
                sp.wait_ge(s.projected, last_piece(15))
            c0 = GROUPS[g][0]
            sp.dma_start(w_slot(g), w_cols[:, :, c0:c0 + 512]).then_inc(w_sem[g], 16)
        sp.wait_ge(s.conv_done, 9)
        out_dma(sp, t["out_conv_p"], raw_p3)
        out_dma(sp, t["out_conv_s"][:, :, 0:2], sconv[:, :, 1:3])
        out_dma(sp, t["out_conv_s"][:, :, 2], raw_s)
        out_dma(sp, t["out_m_p"], mend[0:H, NCH:])
        sp.wait_ge(s.c_ready, NCH)
        out_dma(sp, t["out_C_p"], Cst)
        sync_rest(sp)

    @block.tensor
    def _(pe):
        mm = nc.tensor.matmul

        def project(idx, lhs_of, m):
            if idx >= 4:
                pe.wait_ge(s.proj_read, idx - 3)
            for k in range(KD):
                if idx == 0 and k in (0, 4):
                    pe.wait_ge(s.xT_in2 if k else s.xT_in, 16)
                n = idx % 3
                i = mm(PS[0:m, idx % 4, 0:PIECE], lhs_of(k), xT[:, k, n * PIECE:(n + 1) * PIECE],
                       start=(k == 0), stop=(k == KD - 1))
            i.then_inc(s.projected, 1)

        pe.wait_ge(s.consts_in, 32)
        pe.wait_ge(s.params_in, 16 * N_PARAMS)
        for n in range(3):
            project(n, lambda k: wgt[:, k, :], 64)
        for u in range(16):
            g, j = u // 4, u % 4
            if j == 0:
                pe.wait_ge(w_sem[g], 16)
            if u == 3:
                pe.wait_ge(s.gate_rows, 2)
                for c in range(NCH):
                    i = nc.tensor.transpose(PS[:, 4 + c // 4, (c % 4) * 96:(c % 4 + 1) * 96],
                                            g3[0:96, c * P:(c + 1) * P], ident[0:96, 0:96])
                for h in range(H):
                    mm(PS[:, 6, h * 9:h * 9 + 9], sel[0:H, h, :], mend[0:H, :], start=True, stop=True)
                for h in range(H):
                    i = mm(PS[:, 6, 64 + h * 24:64 + (h + 1) * 24], sel[0:H, h, :], gs_rows[0:H, :], start=True, stop=True)
                i.then_inc(s.gates_spread, 1)
            for n in range(3):
                project(3 + 3 * u + n, lambda k: w_slot(g)[:, k, j * P:(j + 1) * P], P)

        def tokens_product(bank, g, c, sem):
            for k in range(KD):
                i = mm(PS[:, bank, :], xT[:, k, c * P:(c + 1) * P], w_slot(g)[:, k, :], start=(k == 0), stop=(k == KD - 1))
            i.then_inc(sem, 1)

        for c in range(NCH + 1):
            tok = slice(c * P, (c + 1) * P)
            if c < NCH:
                if c == 0:
                    pe.wait_ge(s.proj_read, PIECES)
                    pe.wait_ge(s.gates_read, 1)
                    pe.wait_ge(s.qk_silu, 8)
                else:
                    pe.wait_ge(s.h_turned_read, c - 1)
                    pe.wait_ge(s.s_ready, c)
                for h in range(H):
                    i = mm(PS[:, 2, h * P:(h + 1) * P], sel[0:H, h, :], negM[:, tok], start=True, stop=True)
                i.then_inc(s.decay_b, 1)
                for h in range(H):
                    i = mm(PS[:, 3, h * P:(h + 1) * P], CC[:, 4 + h, tok], CC[:, h, tok], start=True, stop=True)
                i.then_inc(s.scores, 1)
                if c == 0:
                    pe.wait_ge(s.w_in4, 16)
                else:
                    pe.wait_ge(s.v_ready, c)
                tokens_product(0, 4, c, s.v_proj)
                if c >= 1:
                    pe.wait_ge(s.c_ready, c)
                for h in range(H):
                    i = nc.tensor.transpose(PS[:, 6, h * P:(h + 1) * P], CC[:, 4 + h, tok], ident)
                i.then_inc(s.k_turned, 1)
                if c == 0:
                    pe.wait_ge(s.w_in5, 16)
                else:
                    pe.wait_ge(s.o_biased, c)
                tokens_product(1, 5, c, s.o_proj)
            if c >= 1:
                pe.wait_ge(s.hn_ready, c)
                if c < NCH:
                    pe.wait_ge(s.q_arg, c + 1)
                for h in range(H):
                    i = nc.tensor.transpose(PS[:, 2, h * P:(h + 1) * P], hbuf[:, h], ident)
                i.then_inc(s.h_turned, 1)
            if c < NCH:
                pe.wait_ge(s.s_ready, c + 1)
                pe.wait_ge(s.qd_ready, c + 1)
                pe.wait_ge(s.v_ready, c + 1)
                if c >= 1:
                    pe.wait_ge(s.h_ready, c)
                for h in range(H):
                    out = PS[:, 4 + h // 2, (h % 2) * DV1:(h % 2 + 1) * DV1]
                    i = mm(out, dmat[:, h], vext[c % 2][:, h], start=True, stop=(c == 0))
                    if c >= 1:
                        i = mm(out, qd[:, h], Cst[:, h], start=False, stop=True)
                i.then_inc(s.num, 1)
                pe.wait_ge(s.kw_ready, c + 1)
                for h in range(H):
                    i = mm(PS[:, 6 + h // 2, (h % 2) * DV1:(h % 2 + 1) * DV1], kw[:, h], vext[c % 2][:, h], start=True, stop=True)
                i.then_inc(s.cupd, 1)
        pe.wait_ge(s.v_ready, NCH)
        pe.wait_ge(s.o_biased, NCH)
        samples_product(pe, (0, 1), (4, 5))
        samples_turn(pe, 1, zrow[0], 0)
        tensor_rest(pe, tokens_product)

    @block.scalar
    def _(act):
        link, tell = chain(act, s.act_step), teller(act)
        A = nc.scalar.activation
        act.dma_start(cst[:, :], t["consts"]).then_inc(s.consts_in, 16)
        act.dma_start(SC[:, 7680:9216], t["masks"]).then_inc(s.consts_in, 16)
        for dst, src in ((bg[0:64], t["bg"]), (b_cm, t["b_cm"]), (cw, t["cw"]), (cb, t["cb"]), (sconv, t["sconv"]), (m0[0:H], t["m0"]), (g_mix, t["g_mix"])):
            act.dma_start(dst, src).then_inc(s.params_in, 16)
        act.wait_ge(s.params_in, 16 * N_PARAMS)
        act.wait_ge(s.consts_in, 32)

        nc.scalar.preload_act_table_set("natural_log_exp_and_others")
        for idx in range(3):
            act.wait_ge(s.projected, idx + 1)
            tell(A(grow[0:64, idx * PIECE:(idx + 1) * PIECE], PS[0:64, idx % 4, 0:PIECE], ACT.Identity,
              bias=bg[0:64]), s.proj_read)
        act.wait_ge(s.proj_read, 3)
        link(A(fr, grow[32:32 + H], ACT.Copy))
        link(A(lnr, fr, ACT.Abs))
        link(A(lnr, lnr, ACT.Exp, scale=-1.0))
        tell(A(lnr, lnr, ACT.Ln, bias=one_col[0:H]), s.forget_ln)

        def read_unit(u, dst):
            e = [20, 21, 22, 23, 16, 17, 18, 19, 0, 1, 2, 3, 4, 5, 6, 7][u]
            for n in range(3):
                idx = 3 + 3 * u + n
                act.wait_ge(s.projected, idx + 1)
                tell(A(dst[:, n * PIECE:(n + 1) * PIECE], PS[:, idx % 4, 0:PIECE], ACT.Identity,
                  bias=b_cm[:, e:e + 1]), s.proj_read)

        for j in range(H):
            read_unit(j, K[:, j])
            act.wait_ge(s.proj_read, last_piece(j))
            link(A(G[:, j], K[:, j], ACT.Abs))
            link(A(G[:, j], G[:, j], ACT.Exp, scale=-1.0))
            tell(A(G[:, j], G[:, j], ACT.Ln, bias=one_col), s.hf_ln)
            if j == 1:
                act.wait_ge(s.gates_z, 1)
                tell(A(g3[32:32 + H], cmx, ACT.Exp), s.gate_rows)
                tell(A(g3[64:64 + H], lnr[:, 0:NP_], ACT.Exp), s.gate_rows)
            if j >= 1:
                act.wait_ge(s.k_arg, j)
                tell(A(K[:, j - 1], K[:, j - 1], ACT.Exp), s.hg_k_ready)
        act.wait_ge(s.k_arg, H)
        tell(A(K[:, 3], K[:, 3], ACT.Exp), s.hg_k_ready)
        for j in range(H):
            read_unit(4 + j, Q[:, j])
            act.wait_ge(s.proj_read, last_piece(4 + j))
            tell(A(Q[:, j], Q[:, j], ACT.Silu), s.hq_silu)
        for ct in range(9):
            if ct < 8:
                if ct >= 2:
                    act.wait_ge(s.conv_done, ct - 1)
                read_unit(8 + ct, raw[ct % 2][:, 3:])
            if ct >= 1:
                act.wait_ge(s.conv_done, ct)
                tell(A(CC[:, ct - 1], CC[:, ct - 1], ACT.Silu), s.qk_silu)
        act.wait_ge(s.conv_done, 9)
        tell(A(conv_ps, conv_ps, ACT.Silu), s.qk_silu)

        nc.scalar.preload_act_table_set("natural_log_exp_and_others")
        for c in range(NCH + 1):
            if c < NCH:
                act.wait_ge(s.d_arg, c + 1)
                tell(A(dmat, dmat, ACT.Exp), s.d_exp)
                act.wait_ge(s.q_arg, c + 1)
                tell(A(qd, qd, ACT.Exp), s.q_exp)
            if c >= 1:
                act.wait_ge(s.h_turned, c)
                for h in range(H):
                    i = A(CC[:, h, (c - 1) * P:c * P], PS[:, 2, h * P:(h + 1) * P], ACT.Copy, scale=g_mix[:, h:h + 1])
                tell(i, s.h_turned_read)
            if c < NCH:
                act.wait_ge(s.o_biased, c + 1)
                tell(A(ogate, ogate, ACT.Exp, scale=-1.0), s.o_exp)
                act.wait_ge(s.ssq_ready, c + 1)
                link(A(rstd, ssq, ACT.Ln, scale=1.0 / P, bias=rms_eps))
                tell(A(rstd, rstd, ACT.Exp, scale=-0.5), s.rstd_ready)
        scalar_rest(act, link, tell)

    @block.gpsimd
    def _(pool):
        link, tell = chain(pool, s.pool_step), teller(pool)
        pool.wait_ge(s.consts_in, 32)
        tell(nc.gpsimd.tensor_copy(msk[:, :, :].rearrange("p l t -> p (l t)"), mask_words), s.masks_made)
        causal = const("causal").unsqueeze(1).to_broadcast([P, H, P])
        for c in range(NCH):
            pool.wait_ge(s.d_exp, c + 1)
            tell(nc.gpsimd.tensor_tensor(dmat, dmat, causal, ALU.mult), s.d_masked)
            pool.wait_ge(s.h_ready, c + 1)
            tell(nc.gpsimd.tensor_tensor(sq, hbuf, hbuf, ALU.mult), s.h_sq)
        pool_rest(pool, link, tell)

    @block.vector
    def _(dve):
        link, tell = chain(dve, s.dve_step), teller(dve)
        v = nc.vector
        link(v.memset(raw[0][:, 0:3], 0.0))
        link(v.memset(raw[1][:, 0:3], 0.0))
        link(v.memset(g3[0:96], 0.0))
        link(v.memset(keep, 1.0))
        link(v.memset(keep[:, 0:NP_:P], 0.0))
        link(v.memset(drop, 0.0))
        link(v.memset(drop[:, 0:NP_:P], -BIG))
        link(v.memset(mend[0:H], 0.0))
        dve.wait_ge(s.params_in, 16 * N_PARAMS)
        dve.wait_ge(s.forget_ln, 1)
        link(v.scalar_tensor_tensor(fr, fr, 0.0, lnr, ALU.min, ALU.subtract))
        link(v.tensor_tensor_scan(Frow, keep, fr[:, 0:NP_], 0.0, ALU.mult, ALU.add))
        link(v.tensor_tensor(g3[0:H], grow[0:H, 0:NP_], Frow, ALU.subtract))
        link(v.tensor_tensor_scan(cmx, drop, g3[0:H], 0.0, ALU.add, ALU.max))
        link(v.tensor_tensor_scan(mend[0:H, 1:], cmx[:, P - 1:NP_:P], Frow[:, P - 1:NP_:P], 0.0, ALU.max, ALU.add))
        by_chunk = lambda r: r.rearrange("p (c t) -> p c t", c=NCH)
        link(v.tensor_tensor(by_chunk(keep), by_chunk(cmx), mend[0:H, 0:NCH].unsqueeze(2).to_broadcast([H, NCH, P]), ALU.max))
        link(v.tensor_scalar(negM, keep, -1.0, None, ALU.mult))
        link(v.scalar_tensor_tensor(lnr[:, 0:NP_], Frow, -1.0, keep, ALU.mult, ALU.subtract))
        link(v.tensor_copy(drop[:, 0:NCH], keep[:, P - 1:NP_:P]))
        link(v.tensor_tensor(by_chunk(cmx), by_chunk(g3[0:H]), drop[:, 0:NCH].unsqueeze(2).to_broadcast([H, NCH, P]), ALU.subtract))
        link(v.tensor_copy(gs_rows[0:H, 0:NS], grow[0:H, NP_:NT]))
        link(v.tensor_copy(gs_rows[0:H, NS:2 * NS], fr[:, NP_:NT]))
        tell(v.tensor_copy(gs_rows[0:H, 2 * NS:], m0[0:H]), s.gates_z)

        for j in range(H):
            dve.wait_ge(s.hf_ln, j + 1)
            link(v.scalar_tensor_tensor(G[:, j], K[:, j], 0.0, G[:, j], ALU.min, ALU.subtract))
            tell(v.tensor_tensor(K[:, j], G[:, j], K[:, j], ALU.subtract), s.k_arg)
        dve.wait_ge(s.gates_spread, 1)
        for n in range(2):
            i = v.tensor_copy(gcol[:, 4 * n:4 * n + 4], PS[:, 4 + n, 0:384].rearrange("p (c r) -> p c r", c=4))
        link(i)
        link(v.tensor_copy(mprev, PS[:, 6, 0:36].rearrange("p (h c) -> p h c", h=H)))
        tell(v.tensor_copy(gs, PS[:, 6, 64:64 + 96].rearrange("p (h g b) -> p h g b", h=H, g=3)), s.gates_read)
        chunk_keep = cacc
        link(v.memset(chunk_keep, 1.0))
        link(v.memset(chunk_keep[:, 0:NP_:P], 0.0))
        for j in range(H):
            link(v.tensor_tensor_scan(G[:, j, 0:NP_], chunk_keep, G[:, j, 0:NP_], 0.0, ALU.mult, ALU.add))

        for ct in range(8):
            r = raw[ct % 2]
            dve.wait_ge(s.proj_read, last_piece(8 + ct))
            link(v.tensor_scalar(cacc, r[:, 0:NP_], cw[:, ct, 0:1], cb[:, ct:ct + 1], ALU.mult, ALU.add))
            link(v.scalar_tensor_tensor(cacc, r[:, 1:1 + NP_], cw[:, ct, 1:2], cacc, ALU.mult, ALU.add))
            link(v.scalar_tensor_tensor(cacc, r[:, 2:2 + NP_], cw[:, ct, 2:3], cacc, ALU.mult, ALU.add))
            link(v.tensor_copy(raw_s[:, ct], r[:, 3 + NP_:3 + NT]))
            link(v.tensor_copy(raw_p3[:, ct], r[:, NP_:NP_ + 3]))
            tell(v.scalar_tensor_tensor(CC[:, ct], r[:, 3:3 + NP_], cw[:, ct, 3:4], cacc, ALU.mult, ALU.add), s.conv_done)
        cs = conv_ps.rearrange("p (c b) -> p c b", c=8)
        tmp = cacc[:, 0:64].rearrange("p (c b) -> p c b", c=8)
        tap = lambda j: cw[:, :, j:j + 1].to_broadcast([P, 8, NS])
        link(v.tensor_tensor(cs, sconv[:, :, 0], tap(0), ALU.mult))
        link(v.tensor_tensor(cs, cs, cb.unsqueeze(2).to_broadcast([P, 8, NS]), ALU.add))
        for j in (1, 2, 3):
            link(v.tensor_tensor(tmp, raw_s if j == 3 else sconv[:, :, j], tap(j), ALU.mult))
            i = v.tensor_tensor(cs, cs, tmp, ALU.add)
            if j < 3:
                link(i)
        tell(i, s.conv_done)

        dve.wait_ge(s.conv_done, 9)
        for n in range(2):
            link(v.memset(vext[n][:, :, P:], 1.0))
        heads = lambda ap: ap.rearrange("p (h t) -> p h t", h=H)
        for c in range(NCH):
            tok = slice(c * P, (c + 1) * P)
            dve.wait_ge(s.decay_b, c + 1)
            for h in range(H):
                i = v.tensor_scalar(dmat[:, h], PS[:, 2, h * P:(h + 1) * P], gcol[:, c, h:h + 1], 0.0, ALU.add, ALU.min)
            tell(i, s.d_arg)
            tell(v.tensor_tensor(qd, heads(PS[:, 2, :]), mprev[:, :, c:c + 1].to_broadcast([P, H, P]), ALU.add), s.q_arg)
            dve.wait_ge(s.q_exp, c + 1)
            dve.wait_ge(s.qk_silu, 8)
            link(v.tensor_copy(dend, qd[:, :, P - 1]))
            tell(v.tensor_tensor(qd, qd, CC[:, 0:H, tok], ALU.mult), s.qd_ready)
            dve.wait_ge(s.scores, c + 1)
            dve.wait_ge(s.d_masked, c + 1)
            tell(v.scalar_tensor_tensor(dmat, heads(PS[:, 3, :]), KSCALE, dmat, ALU.mult, ALU.mult), s.s_ready)
            dve.wait_ge(s.v_proj, c + 1)
            if c == 0:
                dve.wait_ge(s.bias_in, 16)
            tell(v.tensor_tensor(vext[c % 2][:, :, 0:P], heads(PS[:, 0, :]), heads(bias[:, 0:512]), ALU.add), s.v_ready)
            dve.wait_ge(s.k_turned, c + 1)
            for h in range(H):
                i = v.tensor_scalar(kw[:, h], PS[:, 6, h * P:(h + 1) * P], gcol[:, c, 32 + h:33 + h], KSCALE, ALU.mult, ALU.mult)
            tell(i, s.kw_ready)
            dve.wait_ge(s.o_proj, c + 1)
            tell(v.tensor_tensor(ogate, heads(PS[:, 1, :]), heads(bias[:, 512:1024]), ALU.add), s.o_biased)
            dve.wait_ge(s.o_exp, c + 1)
            link(v.tensor_scalar(ogate, ogate, 1.0, None, ALU.add))
            link(v.reciprocal(ogate, ogate))
            dve.wait_ge(s.cupd, c + 1)
            for h in range(H):
                ps = PS[:, 6 + h // 2, (h % 2) * DV1:(h % 2 + 1) * DV1]
                if c == 0:
                    i = v.tensor_copy(Cst[:, h], ps)
                else:
                    i = v.scalar_tensor_tensor(Cst[:, h], Cst[:, h], dend[:, h:h + 1], ps, ALU.mult, ALU.add)
            tell(i, s.c_ready)
            dve.wait_ge(s.num, c + 1)
            qn = PS[:, 4:6, 0:2 * DV1].rearrange("p b (h v) -> p b h v", h=2)[:, :, :, P]
            two = lambda ap: ap.rearrange("p (b h) -> p b h", b=2)
            link(v.scalar_tensor_tensor(two(den), qn, -1.0, two(gcol[:, c, 64:68]), ALU.mult, ALU.max))
            link(v.tensor_tensor(two(den), qn, two(den), ALU.max))
            link(v.reciprocal(rec, den))
            for h in range(H):
                i = v.scalar_tensor_tensor(hbuf[:, h], PS[:, 4 + h // 2, (h % 2) * DV1:(h % 2) * DV1 + P], rec[:, h:h + 1],
                                           ogate[:, h], ALU.mult, ALU.mult)
            tell(i, s.h_ready)
            dve.wait_ge(s.h_sq, c + 1)
            tell(v.tensor_reduce(ssq, sq, X, ALU.add), s.ssq_ready)
            dve.wait_ge(s.rstd_ready, c + 1)
            tell(v.tensor_tensor(hbuf, hbuf, rstd.unsqueeze(2).to_broadcast([P, H, P]), ALU.mult), s.hn_ready)
        vector_rest(dve, link, tell)


def layouts(i):
    a = {k: np.asarray(v) for k, v in i.items()}
    x = np.concatenate([a["x_prompt"].reshape(NP_, D), a["x_sample"].reshape(NS, D)])
    w, b = a["w_in"][0], a["b_in"][0]
    wg = np.zeros((D, 64), np.float32)
    wg[:, 0:H], wg[:, 32:32 + H] = w[:, 2048:2048 + H], w[:, 2048 + H:COL_HG]
    bg = np.zeros((64, 1), np.float32)
    bg[0:H, 0], bg[32:32 + H, 0] = b[2048:2048 + H], b[2048 + H:COL_HG]
    cols = [COL_Q, COL_K, COL_V, COL_O, COL_HQ, COL_HF, COL_HI, COL_GT]
    cm = lambda v: v.reshape(-1, P).T
    return {
        "consts": CONST_F, "masks": CONST_M,
        "xT": x.T.reshape(P, KD, NT),
        "x": x,
        "w_in": w,
        "wg": wg.reshape(P, KD, 64), "bg": bg,
        "b_cm": np.concatenate([cm(b[c:c + 512]) for c in cols], 1),
        "b_row": np.concatenate([b[c:c + 512] for c in (COL_V, COL_O, COL_HI, COL_GT)])[None],
        "cw": a["conv_w"][0].reshape(4, 8, P).transpose(2, 1, 0),
        "cb": cm(a["conv_b"][0]),
        "sconv": a["state_conv"][0].reshape(NS, 3, 8, P).transpose(3, 2, 1, 0),
        "C0": a["state_ml_C"][0].transpose(2, 1, 0, 3),
        "n0": a["state_ml_n"][0].transpose(2, 1, 0),
        "m0": a["state_ml_m"][0].T,
        "S0": a["state_hg_S"][0].transpose(2, 1, 0, 3),
        "g_mix": np.concatenate([cm(a["ml_norm_g"][0]), cm(a["hg_norm_g"][0])], 1),
        "w_out": a["w_out"][0],
        "ln1": np.concatenate([a["ln1_g"], a["ln1_b"]]),
        "ln2": np.concatenate([a["ln2_g"], a["ln2_b"]]),
        "w_r": np.concatenate([a["w_router_group"][0], a["w_router_expert"][0]], 1).reshape(KD, P, NG + NE).transpose(1, 0, 2),
        "b_r": np.concatenate([a["b_router_group"], a["b_router_expert"]], 1),
        "w_gate": a["w_gate"][0], "w_up": a["w_up"][0], "w_down": a["w_down"][0],
    }


_OUTS = {
    "y": (NT, D), "conv_p": (P, 8, 3), "C_p": (P, H, DV1), "m_p": (H, 1), "S_p": (P, H, P),
    "conv_s": (P, 8, 3, NS), "C_s": (P, H, NS, P), "n_s": (P, H, NS), "m_s": (H, NS), "S_s": (P, H, NS, P),
}


def kernel(**inputs):
    import concourse.bacc as _bacc
    from concourse.bass_utils import run_bass_kernel_spmd as _run

    nc = _bacc.Bacc("TRN2", target_bir_lowering=False, num_devices=1)
    arrays, args = {}, {}
    for name, a in layouts(inputs).items():
        a = np.ascontiguousarray(a)
        arrays[f"in_{name}"] = a
        args[name] = nc.dram_tensor(f"in_{name}", a.shape, mybir.dt.from_np(a.dtype), kind="ExternalInput").ap()
    for name, shape in _OUTS.items():
        args["out_" + name] = nc.dram_tensor(f"out_{name}", shape, F32, kind="ExternalOutput").ap()
    program(nc, args)
    r = _run(nc, [arrays], core_ids=[0]).results[0]
    o = {name: r[f"out_{name}"] for name in _OUTS}
    return (
        o["y"][:NP_].reshape(1, NP_, D), o["y"][NP_:].reshape(NS, 1, D),
        o["conv_p"].transpose(2, 1, 0).reshape(1, 1, 3, D),
        o["C_p"][:, :, :P].transpose(1, 0, 2)[None, None], o["C_p"][:, :, P].T[None, None], o["m_p"].T[None], o["S_p"].transpose(1, 0, 2)[None, None],
        o["conv_s"].transpose(3, 2, 1, 0).reshape(1, NS, 3, D),
        o["C_s"].transpose(2, 1, 0, 3)[None], o["n_s"].transpose(2, 1, 0)[None], o["m_s"].T[None],
        o["S_s"].transpose(2, 1, 0, 3)[None],
    )
```

```python
from contextlib import ExitStack

import numpy as np

import concourse.bass as bass
from concourse import mybir

F32 = mybir.dt.float32
I32 = mybir.dt.int32
U32 = mybir.dt.uint32
U8 = mybir.dt.uint8
ALU = mybir.AluOpType
ACT = mybir.ActivationFunctionType
X = mybir.AxisListType.X

P = 128
D = 1024
Y_SHIFTED = 3
NP_, NS = 1024, 8
NT = NP_ + NS
KD = D // P
NCH = NP_ // P
H = 4
DV1 = P + 1
PIECE = NT // 3
HB = H * NS
LEVELS = [64, 32, 16, 8, 4, 2, 1]
NLEV = len(LEVELS)
NTT = NCH + 1
NG, NJ = 4, 4
NE = NG * NJ
FF = 256
TILES = (2 * NT + NE * (P - 1)) // P
ALPHA = 2 ** 0.25
LN_EPS, RMS_EPS = 1e-5, 1e-6
KSCALE = P ** -0.5
BIG = 1e30
SMALL = 904

COL_Q, COL_K, COL_V, COL_O = 0, 512, 1024, 1536
COL_HG = 4 * 512 + 2 * H
COL_HQ, COL_HF, COL_HI, COL_GT = COL_HG, COL_HG + 512, COL_HG + 1024, COL_HG + 1536

CONST = {}


def constants():
    i = np.arange(P)
    c = {
        "ident": np.eye(P),
        "ones": np.ones((P, P)),
        "causal": (i[:, None] <= i[None, :]),
        "before": (i[:, None] < i[None, :]),
        "lane": np.broadcast_to(i[None, :], (P, P)),
        "token": np.where(i[:, None] + P * np.arange(NTT)[None] < NT, i[:, None] + P * np.arange(NTT)[None], 0),
        "valid": (i[:, None] + P * np.arange(NTT)[None] < NT),
        "first": np.broadcast_to(np.array([4, 3, 2, 1]), (P, 4)),
        "full": np.broadcast_to(P * np.arange(NTT), (P, NTT)),
        "eps": np.broadcast_to(np.array([1.0, RMS_EPS, LN_EPS, 0.0]), (P, 4)),
    }
    cols, at = [], 0
    for name, a in c.items():
        a = np.asarray(a, np.float32).reshape(P, -1)
        CONST[name] = (at, at + a.shape[1])
        at += a.shape[1]
        cols.append(a)
    masks = []
    for b in LEVELS:
        blk, first = i // (2 * b), (i // b) % 2 == 0
        masks.append((blk[:, None] == blk[None, :]) & first[:, None] & ~first[None, :])
    masks.append(np.eye(P, dtype=bool))
    masks = np.stack(masks, 1).astype(np.float32).reshape(P, -1)
    sel = ((i[:, None, None] == np.arange(H)[None, :, None]) * np.ones((P, H, P), np.float32)).reshape(P, -1)
    return np.ascontiguousarray(np.concatenate(cols, 1)), np.concatenate([masks, sel], 1)


CONST_F, CONST_M = constants()


def program(nc, t):
    with ExitStack() as ctx:
        _program(nc, t, ctx)


def _program(nc, t, ctx):
    def sb(name, shape, dt=F32):
        return ctx.enter_context(nc.sbuf_tensor(name, shape, dt))

    cst = sb("constants", [P, CONST_F.shape[1]])
    msk = sb("level_masks", [P, NLEV + 1, P], U8)
    xT = sb("x_cm", [P, KD, NT])
    W = sb("weight_slots", [P, 3, KD, 512])
    CC = sb("conv_qk", [P, 8, NP_])
    G = sb("hg_decay", [P, H, NT])
    Q = sb("hg_q", [P, H, NT])
    K = sb("hg_k", [P, H, NT])
    SC = sb("scratch", [P, 9728])
    R = sb("router", [P, 384])
    SM = sb("small", [P, SMALL])
    PS = ctx.enter_context(nc.psum_tensor("psum", [P, 8, 512], F32))

    def const(name):
        a, b = CONST[name]
        return cst[:, a:b]

    ident, ones = const("ident"), const("ones")
    one_col, rms_eps, ln_eps = (cst[:, CONST["eps"][0] + n:CONST["eps"][0] + n + 1] for n in range(3))

    at = [0]

    def small(n):
        at[0] += n
        assert at[0] <= SMALL
        return SM[:, at[0] - n:at[0]]

    params = small(32 + 8 + 32 + 1 + 8 + 24 * NS + NS)
    at[0] = 0
    cw = small(32).rearrange("p (c j) -> p c j", c=8)
    cb = small(8)
    b_cm = small(32)
    bg = small(1)
    g_mix = small(8)
    sconv = small(8 * 3 * NS).rearrange("p (c j b) -> p c j b", c=8, j=3)
    m0 = small(NS)
    raw_s = small(8 * NS).rearrange("p (c b) -> p c b", c=8)
    raw_p3 = small(24).rearrange("p (c j) -> p c j", c=8)
    conv_ps = small(64)
    mend = small(NCH + 1)
    mprev = small(H * (NCH + 1)).rearrange("p (h c) -> p h c", h=H)
    gs_rows = small(3 * NS)
    gs = small(H * 3 * NS).rearrange("p (h g b) -> p h g b", h=H, g=3)
    zs = small(16 * NS).rearrange("p (e b) -> p e b", e=16)
    den, rec, ssq, rstd, dend = (small(H) for _ in range(5))

    raw = [SC[:, 0:3 + NT], SC[:, 1036:1036 + 3 + NT]]
    cacc = SC[:, 2072:2072 + NP_]
    g3 = SC[:, 3100:3100 + NP_]
    CF = CC[:, :, :].rearrange("p a b -> p (a b)")
    grow = CF[:, 0:NT]
    fr, lnr = CF[0:H, NT:2 * NT], CF[0:H, 2 * NT:3 * NT]
    keep, drop, Frow, cmx = (CF[0:H, 3100 + n * NP_:3100 + (n + 1) * NP_] for n in range(4))
    buf = lambda n: SC[:, n * 512:(n + 1) * 512].rearrange("p (h t) -> p h t", h=H)
    dmat, qd, kw, hbuf, sq = (buf(n) for n in range(5))
    vext = [SC[:, 2560 + n * 516:2560 + (n + 1) * 516].rearrange("p (h v) -> p h v", h=H) for n in range(2)]
    ogate = SC[:, 3592:4104].rearrange("p (h t) -> p h t", h=H)
    Cst = SC[:, 4104:4620].rearrange("p (h v) -> p h v", h=H)
    negM = SC[0:H, 4620:5644]
    gcol = SC[:, 5644:6412].rearrange("p (c r) -> p c r", c=NCH)
    bias = SC[:, 6656:7680]

    xlev = [buf(0), buf(1)]
    amat, hmix, qdec, kend, ibuf, gtb = (buf(n) for n in (2, 3, 4, 5, 6, 7))
    Sst = buf(8)
    zrow = SC[0:NS, 5632:6656], SC[0:NS, 0:1024]
    xrow = SC[:, 4608:5632]
    xTt = SC[:, 5632:6656].rearrange("p (k t) -> p k t", k=KD)
    ln_gb = SC[:, 7680:9728].rearrange("p (g n) -> p g n", g=2)
    w_out = W[:, 1:3].rearrange("p s a b -> p (s a b)").rearrange("p (e n) -> p e n", e=8)
    w_r = R[:, 0:160].rearrange("p (k e) -> p k e", k=KD)
    b_r = R[:, 160:180]
    LG = R[:, 180:360].rearrange("p (i e) -> p i e", i=NTT)
    stats = R[:, 360:372].rearrange("p (g n) -> p g n", g=2)
    mv = R[:, 372:374]
    lstd = R[:, 374:375]
    egend = R[:, 376:380]
    mixS = small(8 * NS).rearrange("p (e b) -> p e b", e=8)
    XF = xT[:, :, :].rearrange("p k t -> p (k t)")
    C0 = XF[:, 0:4096].rearrange("p (e v) -> p e v", e=HB)
    vdiag = [w.rearrange("p (e v) -> p e v", e=HB) for w in (CF[0:HB, 0:4096], CF[0:HB, 4096:8192])]
    S0 = W[:, 0].rearrange("p k n -> p (k n)").rearrange("p (e v) -> p e v", e=HB)
    n0 = small(HB)
    T, TH = ([SC[:, at + n * HB:at + (n + 1) * HB] for n in range(24)] for at in (0, 1024))
    kv_outer = [SC[:, 2560 + n * 512:3072 + n * 512] for n in range(3)]
    kvT = [SC[0:HB, 1792 + n * 384:2176 + n * 384] for n in range(2)]
    q_apart = [SC[:, 2560:3584], SC[:, 6656:7680]]
    by_hb = lambda ap: ap.rearrange("p (h b) -> p h b", h=H)
    x1_dram = nc.dram_tensor("x1_rows", (NT, D), F32).ap()
    flatf = lambda tile: tile[:, :, :].rearrange("p a b -> p (a b)")
    KF, GF, QF = flatf(K), flatf(G), flatf(Q)
    wslots = [flatf(CC), W[:, 1:3].rearrange("p s a b -> p (s a b)")]
    w_gu = [w[:, 0:4096].rearrange("p (k g f) -> p k g f", k=KD, g=2) for w in wslots]
    w_dn = [w[:, 4096:6144].rearrange("p (k n) -> p k n", k=2) for w in wslots]
    xg = [SC[:, n * D:(n + 1) * D] for n in range(2)]
    xgT = [SC[:, (2 + n) * D:(3 + n) * D].rearrange("p (k t) -> p k t", k=KD) for n in range(2)]
    ysb = [SC[:, (4 + n) * D:(5 + n) * D] for n in range(2)]
    silu, hid = SC[:, 6144:6400], SC[:, 6400:6656]
    hidT = SC[:, 6656:6912].rearrange("p (k t) -> p k t", k=2)
    gate_c = [SC[:, 6914 + n:6915 + n] for n in range(2)]
    y_slots = nc.dram_tensor("y_slots", (TILES * P, D), F32).ap()
    oh_lo = KF[:, 0:18 * P].rearrange("p (q n) -> p q n", q=18)
    oh_hi = QF[:, 0:18 * 64].rearrange("p (q w n) -> p q w n", q=18, w=2)
    kat = [18 * P]

    def route_tile(n):
        kat[0] += n
        assert kat[0] <= 4128
        return KF[:, kat[0] - n:kat[0]]

    slot_tok = route_tile(TILES).bitcast(I32)
    slot_gate = route_tile(TILES)
    tile_expert = route_tile(TILES)
    pos = route_tile(2 * NTT)
    pos_i = route_tile(2 * NTT).bitcast(I32)
    hi_i, lo_i = (route_tile(2 * NTT).bitcast(I32) for _ in range(2))
    hi_f, lo_f = (route_tile(2 * NTT) for _ in range(2))
    wts = route_tile(2 * NTT).rearrange("p (w i) -> p w i", w=2)
    gat = [0]

    def work(*shape):
        n = int(np.prod(shape))
        gat[0] += n
        assert gat[0] <= 4128
        ap = GF[:, gat[0] - n:gat[0]]
        if len(shape) == 2:
            return ap.rearrange("p (a b) -> p a b", b=shape[1])
        if len(shape) == 3:
            return ap.rearrange("p (a b c) -> p a b c", b=shape[1], c=shape[2])
        return ap

    gmax, gden, v1, v2, e2, s2 = (work(NTT) for _ in range(6))
    gexp, ghot, scr, leg, leg2 = (work(NTT, 4) for _ in range(5))
    hot = [work(NTT, 4) for _ in range(2)]
    ex = [work(NTT, NE) for _ in range(2)]
    esum, tot, slotp = (work(NTT, NE) for _ in range(3))
    le_m = work(NTT, 4, 4)
    cnt = work(NTT, NE)
    n_e, nt_e, end_e, base_e = (work(NE) for _ in range(4))
    cmp9 = work(NE, NTT)
    cmp32 = work(TILES, NE)
    x1_keep = [XF[:, (c + 4) % 8 * D:((c + 4) % 8 + 1) * D] for c in range(8)] + [SC[:, 8 * D:9 * D]]
    ln2_gb = wslots[0][:, 6144:8192].rearrange("p (g n) -> p g n", g=2)
    fst = GF[:, 0:NTT * 12].rearrange("p (i g n) -> p i g n", i=NTT, g=2)
    fmv = GF[:, 128:128 + NTT * 2].rearrange("p (i n) -> p i n", n=2)
    fsd, fshift = GF[:, 160:160 + NTT], GF[:, 176:176 + NTT]

    class Semaphores:
        pass

    s = Semaphores()

    def sem(name):
        return ctx.enter_context(nc.semaphore(name))

    s.consts_in = sem("consts_in")
    s.params_in = sem("params_in")
    s.wg_in = sem("wg_in")
    s.x_in0 = sem("x_in0")
    s.x_in1 = sem("x_in1")
    s.x_in2 = sem("x_in2")
    s.bias2_in = sem("bias2_in")
    s.bias_in = sem("bias_in")
    s.w_in0 = sem("w_in0")
    s.w_in1 = sem("w_in1")
    s.w_in2 = sem("w_in2")
    s.w_in3 = sem("w_in3")
    s.w_in4 = sem("w_in4")
    s.w_in5 = sem("w_in5")
    s.w_in6 = sem("w_in6")
    s.w_in7 = sem("w_in7")
    s.dve_step = sem("dve_step")
    s.act_step = sem("act_step")
    s.pool_step = sem("pool_step")
    s.projected = sem("projected")
    s.proj_read = sem("proj_read")
    s.gates_z = sem("gates_z")
    s.forget_ln = sem("forget_ln")
    s.gate_rows = sem("gate_rows")
    s.gates_spread = sem("gates_spread")
    s.gates_read = sem("gates_read")
    s.hf_ln = sem("hf_ln")
    s.k_arg = sem("k_arg")
    s.hg_k_ready = sem("hg_k_ready")
    s.conv_done = sem("conv_done")
    s.qk_silu = sem("qk_silu")
    s.hq_silu = sem("hq_silu")
    s.decay_b = sem("decay_b")
    s.scores = sem("scores")
    s.k_turned = sem("k_turned")
    s.num = sem("num")
    s.cupd = sem("cupd")
    s.h_turned = sem("h_turned")
    s.h_turned_read = sem("h_turned_read")
    s.d_arg = sem("d_arg")
    s.q_arg = sem("q_arg")
    s.d_exp = sem("d_exp")
    s.q_exp = sem("q_exp")
    s.d_masked = sem("d_masked")
    s.kw_ready = sem("kw_ready")
    s.s_ready = sem("s_ready")
    s.qd_ready = sem("qd_ready")
    s.v_proj = sem("v_proj")
    s.o_proj = sem("o_proj")
    s.v_ready = sem("v_ready")
    s.o_biased = sem("o_biased")
    s.o_exp = sem("o_exp")
    s.h_ready = sem("h_ready")
    s.h_sq = sem("h_sq")
    s.ssq_ready = sem("ssq_ready")
    s.rstd_ready = sem("rstd_ready")
    s.hn_ready = sem("hn_ready")
    s.c_ready = sem("c_ready")
    s.zs_proj = sem("zs_proj")
    s.zs_read = sem("zs_read")
    s.outputs = sem("outputs")
    s.masks_made = sem("masks_made")
    s.dots = sem("dots")
    s.dots_in = sem("dots_in")
    s.down_done = sem("down_done")
    s.esum_ready = sem("esum_ready")
    s.g_exp = sem("g_exp")
    s.gate_ready = sem("gate_ready")
    s.gt_biased = sem("gt_biased")
    s.gt_exp = sem("gt_exp")
    s.gt_proj = sem("gt_proj")
    s.hgs_ready = sem("hgs_ready")
    s.hidT_ready = sem("hidT_ready")
    s.hid_ready = sem("hid_ready")
    s.hid_turned = sem("hid_turned")
    s.i_proj = sem("i_proj")
    s.i_ready = sem("i_ready")
    s.kend_arg = sem("kend_arg")
    s.kend_exp = sem("kend_exp")
    s.kend_ready = sem("kend_ready")
    s.kend_tm = sem("kend_tm")
    s.kend_turned = sem("kend_turned")
    s.kv_in = sem("kv_in")
    s.kv_read = sem("kv_read")
    s.kv_turned = sem("kv_turned")
    s.level_arg = sem("level_arg")
    s.level_exp = sem("level_exp")
    s.level_kept = sem("level_kept")
    s.level_scaled = sem("level_scaled")
    s.levels = sem("levels")
    s.ln2_in = sem("ln2_in")
    s.logits_read = sem("logits_read")
    s.lstd_ready = sem("lstd_ready")
    s.mixS_ready = sem("mixS_ready")
    s.mixed = sem("mixed")
    s.mixer_in = sem("mixer_in")
    s.moments = sem("moments")
    s.normed = sem("normed")
    s.o_scaled = sem("o_scaled")
    s.o_num = sem("o_num")
    s.o_turned = sem("o_turned")
    s.o_turned_read = sem("o_turned_read")
    s.ogate_arg = sem("ogate_arg")
    s.ogate_exp = sem("ogate_exp")
    s.on_ready = sem("on_ready")
    s.onehots = sem("onehots")
    s.gt_gated = sem("gt_gated")
    s.outer = sem("outer")
    s.outer_read = sem("outer_read")
    s.qg_ready = sem("qg_ready")
    s.ranked = sem("ranked")
    s.residual = sem("residual")
    s.route_arg = sem("route_arg")
    s.route_exp = sem("route_exp")
    s.routed = sem("routed")
    s.s_upd = sem("s_upd")
    s.sgates_arg = sem("sgates_arg")
    s.sgates_exp = sem("sgates_exp")
    s.silu_ready = sem("silu_ready")
    s.slots = sem("slots")
    s.sq_in = sem("sq_in")
    s.sq_sum = sem("sq_sum")
    s.srstd = sem("srstd")
    s.state_in = sem("state_in")
    s.state_added = sem("state_added")
    s.experts_known = sem("experts_known")
    s.tiles_known = sem("tiles_known")
    s.gate_done = sem("gate_done")
    s.up_done = sem("up_done")
    s.vdiag_ready = sem("vdiag_ready")
    s.w_dn_in0 = sem("w_dn_in0")
    s.w_dn_in1 = sem("w_dn_in1")
    s.w_gu_in0 = sem("w_gu_in0")
    s.w_gu_in1 = sem("w_gu_in1")
    s.x1_back = sem("x1_back")
    s.x1_ready = sem("x1_ready")
    s.x1_turned = sem("x1_turned")
    s.x1_turned_read = sem("x1_turned_read")
    s.x1_written = sem("x1_written")
    s.x_in = sem("x_in")
    s.xgT_ready = sem("xgT_ready")
    s.xg_in0 = sem("xg_in0")
    s.xg_in1 = sem("xg_in1")
    s.xg_turned = sem("xg_turned")
    s.y_scaled = sem("y_scaled")
    s.y_out0 = sem("y_out0")
    s.y_out1 = sem("y_out1")
    s.y_read = sem("y_read")
    s.y_ready = sem("y_ready")
    s.yg_in0 = sem("yg_in0")
    s.yg_in1 = sem("yg_in1")
    s.yg_in2 = sem("yg_in2")
    s.yg_in3 = sem("yg_in3")
    s.yg_in4 = sem("yg_in4")
    s.yg_in5 = sem("yg_in5")
    s.zs_row = sem("zs_row")
    s.zs_turned = sem("zs_turned")
    outs = [0]

    def out_dma(eng, dst, src):
        eng.dma_start(dst, src).then_inc(s.outputs, 16)
        outs[0] += 1

    def chain(eng, sem):
        n = [0]

        def link(ins):
            n[0] += 1
            ins.then_inc(sem, 1)
            eng.wait_ge(sem, n[0])
        return link

    def teller(eng):
        told = {}

        def tell(ins, sem):
            told[sem] = told.get(sem, 0) + 1
            ins.then_inc(sem, 1)
            eng.wait_ge(sem, told[sem])
        return tell

    w_cols = t["w_in"].rearrange("(p k) e -> p k e", k=KD)
    GROUPS = [(COL_HF, 0), (COL_HQ, 1), (COL_Q, 2), (COL_K, 0), (COL_V, 1), (COL_O, 2), (COL_GT, 0), (COL_HI, 3)]
    slot3 = CC[:, 4:8, :].rearrange("p a (b e) -> p (a b) e", b=2)
    w_slot = lambda g: slot3 if GROUPS[g][1] == 3 else W[:, GROUPS[g][1]]
    w_sem = [s.w_in0, s.w_in1, s.w_in2, s.w_in3, s.w_in4, s.w_in5, s.w_in6, s.w_in7]
    PIECES = 3 * 17
    last_piece = lambda unit: 3 * (unit + 2)
    mask_words = SC[:, 7680:7680 + (NLEV + 1) * P]
    sel = SC[:, 8704:8704 + H * P].rearrange("p (h m) -> p h m", h=H)
    wgt = SC[:, 4200:4200 + KD * 64].rearrange("p (k e) -> p k e", k=KD)

    def x_rows(c):
        return P if c < NCH else NS

    def sync_rest(sp):
        sp.wait_ge(s.k_turned, NCH)
        sp.dma_start(w_slot(7), w_cols[:, :, COL_HI:COL_HI + 512]).then_inc(s.w_in7, 16)
        sp.wait_ge(s.o_biased, NCH)
        sp.dma_start(bias, t["b_row"][:, 1024:2048].partition_broadcast(P).rearrange("p a n -> p (a n)")).then_inc(s.bias2_in, 16)
        sp.dma_start(w_r, t["w_r"]).then_inc(s.mixer_in, 16)
        sp.dma_start(b_r, t["b_r"].partition_broadcast(P).rearrange("p a n -> p (a n)")).then_inc(s.mixer_in, 16)
        sp.dma_start(by_hb(n0), t["n0"]).then_inc(s.mixer_in, 16)
        sp.wait_ge(s.zs_proj, 1)
        sp.dma_start(w_out, t["w_out"].rearrange("(e p) n -> p e n", p=P)).then_inc(s.mixer_in, 16)
        sp.wait_ge(s.masks_made, 1)
        sp.wait_ge(s.h_turned_read, NCH)
        sp.dma_start(ln_gb, t["ln1"].partition_broadcast(P)).then_inc(s.mixer_in, 16)

        def keep_x1(c):
            at = (c + 4) % 8 * D
            sp.dma_start(XF[:, at:at + 4 * D].rearrange("p (c n) -> p c n", c=4),
                         x1_dram[c * P:(c + 4) * P].rearrange("(c p) n -> p c n", p=P)).then_inc(s.x1_back, 16)

        for c in range(NTT):
            if c == 0:
                sp.wait_ge(s.c_ready, NCH)
                sp.wait_ge(s.outputs, 16 * outs[0])
            else:
                sp.wait_ge(s.x1_turned, c)
                sp.wait_ge(s.x1_written, 16 * c)
            r = x_rows(c)
            sp.dma_start(xrow[0:r], t["x"][c * P:c * P + r]).then_inc(s.x_in, 16)
            if c == NCH - 1:
                sp.wait_ge(s.hgs_ready, NCH)
                out_dma(sp, t["out_S_p"], Sst)
            sp.wait_ge(s.x1_ready, c + 1)
            sp.dma_start(x1_dram[c * P:c * P + r], xrow[0:r]).then_inc(s.x1_written, 16)
        sp.wait_ge(s.x1_written, 16 * NTT)
        keep_x1(0)
        sp.wait_ge(s.mixS_ready, 2)
        out_dma(sp, t["out_n_s"].rearrange("p h b -> p (h b)"), T[20])
        out_dma(sp, t["out_m_s"].rearrange("h b -> (h b)").unsqueeze(0), T[21][0:1])
        sp.wait_ge(s.state_added, 8)
        out_dma(sp, t["out_C_s"].rearrange("p h b v -> p (h b) v"), C0)
        sync_moe(sp, keep_x1)

    def samples_product(pe, banks, groups):
        for bank, g in zip(banks, groups):
            for k in range(KD):
                i = nc.tensor.matmul(PS[0:NS, bank, :], xT[:, k, NP_:NT], w_slot(g)[:, k, :], start=(k == 0), stop=(k == KD - 1))
        i.then_inc(s.zs_proj, 1)

    def samples_turn(pe, count, row, bank):
        pe.wait_ge(s.zs_row, count)
        for e in range(8):
            i = nc.tensor.transpose(PS[:, bank, e * NS:(e + 1) * NS], row[:, e * P:(e + 1) * P], ident[0:NS, 0:NS])
        i.then_inc(s.zs_turned, 1)

    def samples_rows(dve, tell, count, banks, row):
        dve.wait_ge(s.zs_proj, count)
        for n in range(2):
            i = nc.vector.tensor_copy(row[:, n * 512:(n + 1) * 512], PS[0:NS, banks[n], :])
        tell(i, s.zs_row)

    def samples_bias(dve, tell, count, bank):
        dve.wait_ge(s.zs_turned, count)
        e = 8 * (count - 1)
        tell(nc.vector.tensor_tensor(zs[:, e:e + 8], PS[:, bank, 0:64].rearrange("p (e b) -> p e b", e=8),
                                     b_cm[:, 8 + 2 * e:16 + 2 * e].unsqueeze(2).to_broadcast([P, 8, NS]), ALU.add), s.zs_read)

    def tensor_rest(pe):
        mm = nc.tensor.matmul
        hp = lambda bank, h: PS[:, bank, h * P:(h + 1) * P]
        pe.wait_ge(s.hg_k_ready, H)
        pe.wait_ge(s.hq_silu, H)

        def out_project(c, lhs_of):
            r = x_rows(c)
            for n in range(2):
                for e in range(8):
                    i = mm(PS[0:r, 6 + n, :], lhs_of(e), w_out[:, e, n * 512:(n + 1) * 512], start=(e == 0), stop=(e == 7))
            i.then_inc(s.mixed, 1)

        def turn_x1(c):
            r = x_rows(c)
            pe.wait_ge(s.x1_ready, c + 1)
            for k in range(KD):
                i = nc.tensor.transpose(PS[:, 4 + k // 4, (k % 4) * P:(k % 4) * P + r], xrow[0:r, k * P:(k + 1) * P], ident[0:r, 0:r])
            i.then_inc(s.x1_turned, 1)

        def route(c):
            r = x_rows(c)
            pe.wait_ge(s.x1_turned_read, c + 1)
            pe.wait_ge(s.mixer_in, 16 * 5)
            for k in range(KD):
                i = mm(PS[0:r, 5, 0:NG + NE], xTt[:, k, 0:r], w_r[:, k, :], start=(k == 0), stop=(k == KD - 1))
            i.then_inc(s.routed, 1)

        def turn_outputs(c):
            pe.wait_ge(s.on_ready, c + 1)
            for h in range(H):
                i = nc.tensor.transpose(hp(4, h), hmix[:, h], ident)
            i.then_inc(s.o_turned, 1)

        def project_in(c, part):
            if part == 0:
                if c == 0:
                    pe.wait_ge(s.w_in6, 16)
                    pe.wait_ge(s.zs_read, 1)
                else:
                    pe.wait_ge(s.gt_gated, c)
            if part == 2:
                if c == 0:
                    pe.wait_ge(s.w_in7, 16)
                else:
                    pe.wait_ge(s.kend_tm, c)
            bank, g = 1 - part // 2, 6 + part // 2
            for k in range(4 * (part % 2), 4 * (part % 2) + 4):
                i = mm(PS[:, bank, :], xT[:, k, c * P:(c + 1) * P], w_slot(g)[:, k, :], start=(k == 0), stop=(k == KD - 1))
            if part % 2:
                i.then_inc((s.gt_proj, s.i_proj)[part // 2], 1)

        def project_out(c, part):
            if part == 0:
                if c == 0:
                    pe.wait_ge(s.mixer_in, 16 * 5)
                    pe.wait_ge(s.c_ready, NCH)
                else:
                    pe.wait_ge(s.residual, c)
                pe.wait_ge(s.o_turned_read, c + 1)
            tok = slice(c * P, (c + 1) * P)
            n = part // 2
            for e in range(4 * (part % 2), 4 * (part % 2) + 4):
                lhs = CC[:, e, tok] if e < 4 else Q[:, e - 4, tok]
                i = mm(PS[:, 6 + n, :], lhs, w_out[:, e, n * 512:(n + 1) * 512], start=(e == 0), stop=(e == 7))
            if part == 3:
                i.then_inc(s.mixed, 1)

        for c in range(NCH):
            tok = slice(c * P, (c + 1) * P)
            for l in range(NLEV + 1):
                n = (NLEV + 1) * c + l
                if n == 0:
                    pe.wait_ge(s.h_turned_read, NCH)
                elif n == 1:
                    pe.wait_ge(s.s_ready, NCH)
                else:
                    pe.wait_ge(s.level_kept, n - 1)
                if l < NLEV:
                    xl = xlev[(NLEV * c + l) % 2]
                    pe.wait_ge(s.level_scaled, 2 * (NLEV * c + l + 1))
                for h in range(H):
                    if l < NLEV:
                        i = mm(hp(2 + n % 2, h), xl[:, h], xl[:, h], start=True, stop=True)
                    else:
                        i = mm(hp(2 + n % 2, h), K[:, h, tok], Q[:, h, tok], start=True, stop=True)
                i.then_inc(s.levels, 1)
                if l == 1 and c >= 3:
                    pe.wait_ge(s.hgs_ready, c)
                    route(c - 3)
                if l == 3 and c >= 1:
                    turn_outputs(c - 1)
                if l == 5:
                    pe.wait_ge(s.kend_ready, c + 1)
                    pe.wait_ge(s.i_ready, c + 1)
                    for h in range(H):
                        i = nc.tensor.transpose(hp(0, h), kend[:, h], ident)
                    i.then_inc(s.kend_turned, 1)
                if l == 6 and c >= 2:
                    pe.wait_ge(s.o_turned_read, c)
                    if c >= 3:
                        pe.wait_ge(s.logits_read, c - 2)
                    turn_x1(c - 2)
                if l < 4:
                    project_in(c, l)
                elif c >= 1:
                    project_out(c - 1, l - 4)
            pe.wait_ge(s.level_kept, (NLEV + 1) * (c + 1))
            pe.wait_ge(s.qg_ready, c + 1)
            if c == 0:
                pe.wait_ge(s.h_ready, NCH)
            if c >= 1:
                pe.wait_ge(s.o_turned_read, c)
            if c >= 2:
                pe.wait_ge(s.x1_turned_read, c - 1)
            for h in range(H):
                i = mm(hp(4, h), amat[:, h], ibuf[:, h], start=True, stop=(c == 0))
                if c >= 1:
                    i = mm(hp(4, h), qdec[:, h], Sst[:, h], start=False, stop=True)
            i.then_inc(s.o_num, 1)
            pe.wait_ge(s.kend_tm, c + 1)
            for h in range(H):
                i = mm(hp(5, h), kend[:, h], ibuf[:, h], start=True, stop=True)
            i.then_inc(s.s_upd, 1)
        pe.wait_ge(s.kend_tm, NCH)
        pe.wait_ge(s.gt_gated, NCH)
        samples_product(pe, (0, 1), (7, 6))
        pe.wait_ge(s.hgs_ready, NCH)
        route(NCH - 3)
        turn_outputs(NCH - 1)
        samples_turn(pe, 2, zrow[1], 0)
        for part in range(4):
            project_out(NCH - 1, part)
        pe.wait_ge(s.logits_read, NCH - 2)
        turn_x1(NCH - 2)
        route(NCH - 2)

        pe.wait_ge(s.zs_read, 2)
        pe.wait_ge(s.level_kept, (NLEV + 1) * NCH)
        pe.wait_ge(s.state_in, 32)
        for kind in range(2):
            state, tiles, bank = (C0, S0)[kind], (T, TH)[kind], 2 * kind
            pe.wait_ge(s.dots_in, kind + 1)
            n = 2 - kind
            mm(PS[:, bank, 0:n * HB], ones, SC[:, 1024 * kind:1024 * kind + n * HB], start=True, stop=True)
            for e in range(HB):
                mm(PS[0:HB, bank + 1, 2 * P:3 * P], q_apart[kind][:, e * HB:(e + 1) * HB], state[:, e, :],
                   start=(e == 0), stop=(e == HB - 1))
            pe.wait_ge(s.kv_in, kind + 1)
            nc.tensor.transpose(PS[0:HB, bank + 1, 0:P], tiles[3], ident)
            i = nc.tensor.transpose(PS[0:HB, bank + 1, P:2 * P], tiles[4], ident)
            i.then_inc(s.kv_turned, 1)
        for kind in range(2):
            pe.wait_ge(s.kv_read, kind + 1)
            nc.tensor.transpose(PS[:, 2 * kind, 2 * HB:3 * HB], kvT[kind][:, 2 * P:3 * P], ident[0:HB, 0:HB]).then_inc(s.dots, 1)
        for kind in range(2):
            pe.wait_ge(s.sq_in, kind + 1)
            mm(PS[:, 2 * kind, 96:128], ones, (T, TH)[kind][5], start=True, stop=True).then_inc(s.sq_sum, 1)
            if kind == 0:
                pe.wait_ge(s.o_turned_read, NCH)
                pe.wait_ge(s.logits_read, NCH - 1)
                turn_x1(NCH - 1)
        route(NCH - 1)
        pe.wait_ge(s.mixS_ready, 2)
        pe.wait_ge(s.residual, NCH)
        out_project(NCH, lambda e: mixS[:, e, :])

        def outer_product(m):
            if m >= 4:
                pe.wait_ge(s.outer_read, m - 3)
            rhs = vdiag[m // 8][:, 4 * (m % 8):4 * (m % 8) + 4, :].rearrange("p a v -> p (a v)")
            mm(PS[:, m % 4, :], kvT[m // 8][:, 0:P], rhs, start=True, stop=True).then_inc(s.outer, 1)

        pe.wait_ge(s.vdiag_ready, 2)
        for m in range(4):
            outer_product(m)
        pe.wait_ge(s.logits_read, NCH)
        turn_x1(NCH)
        route(NCH)
        for m in range(4, 7):
            outer_product(m)
        pe.wait_ge(s.esum_ready, 1)
        mm(PS[:, 6, 0:NTT * NE], const("before"), esum.rearrange("p i e -> p (i e)"), start=True, stop=True)
        mm(PS[:, 7, 0:NTT * NE], ones, esum.rearrange("p i e -> p (i e)"), start=True, stop=True).then_inc(s.ranked, 1)
        for m in range(7, 12):
            outer_product(m)
        tensor_moe(pe, outer_product)

    def read_outer(act, which):
        for m in which:
            act.wait_ge(s.outer, m + 1)
            if m >= 3:
                act.wait_ge(s.state_added, m - 2)
            nc.scalar.activation(kv_outer[m % 3], PS[:, m % 4, :], ACT.Copy).then_inc(s.outer_read, 1)

    def scalar_rest(act, link, tell):
        A = nc.scalar.activation
        by_h = lambda ap: ap.rearrange("p (h t) -> p h t", h=H)

        def ln_scale(c):
            r = x_rows(c)
            act.wait_ge(s.moments, c + 1)
            link(A(lstd[0:r], mv[0:r, 1:2], ACT.Ln, bias=ln_eps[0:r]))
            tell(A(lstd[0:r], lstd[0:r], ACT.Exp, scale=-0.5), s.lstd_ready)

        def x1_evacuate(c):
            r = x_rows(c)
            act.wait_ge(s.x1_turned, c + 1)
            if c >= 1:
                act.wait_ge(s.routed, c)
            for n in range(2):
                i = A(xTt[:, 4 * n:4 * n + 4, 0:r], by_h(PS[:, 4 + n, :])[:, :, 0:r], ACT.Copy)
                if n == 0:
                    link(i)
            tell(i, s.x1_turned_read)

        def turned_outputs(c):
            act.wait_ge(s.o_turned, c + 1)
            for h in range(H):
                i = A(Q[:, h, c * P:(c + 1) * P], PS[:, 4, h * P:(h + 1) * P], ACT.Copy, scale=g_mix[:, H + h:H + h + 1])
            tell(i, s.o_turned_read)

        def level_exp(n):
            if n < NLEV * NCH:
                act.wait_ge(s.level_arg, n + 1)
                tell(A(xlev[n % 2], xlev[n % 2], ACT.Exp), s.level_exp)

        def outputs_scale(c):
            act.wait_ge(s.o_num, c + 1)
            for h in range(H):
                i = A(hmix[:, h], PS[:, 4, h * P:(h + 1) * P], ACT.Square, accum_out=ssq[:, h:h + 1])
            link(i)
            link(A(rstd, ssq, ACT.Ln, scale=1.0 / P, bias=rms_eps))
            link(A(rstd, rstd, ACT.Exp, scale=-0.5))
            for h in range(H):
                i = A(hmix[:, h], PS[:, 4, h * P:(h + 1) * P], ACT.Copy, scale=rstd[:, h:h + 1])
            tell(i, s.o_scaled)

        level_exp(0)
        level_exp(1)
        for c in range(NCH):
            if c >= 1:
                outputs_scale(c - 1)
            act.wait_ge(s.kend_arg, c + 1)
            tell(A(kend, kend, ACT.Exp), s.kend_exp)
            for l in range(2, NLEV + 2):
                level_exp(NLEV * c + l)
                if l == 2 and c >= 2:
                    ln_scale(c - 2)
                if l == 3:
                    tell(A(qdec, G[:, :, c * P:(c + 1) * P], ACT.Exp), s.g_exp)
                if l == 4 and c >= 1:
                    turned_outputs(c - 1)
                if l == 5:
                    act.wait_ge(s.gt_biased, c + 1)
                    tell(A(PS[:, 1, :], gtb.rearrange("p h v -> p (h v)"), ACT.Exp, scale=-1.0), s.gt_exp)
                if l == 8 and c >= 2:
                    x1_evacuate(c - 2)
        outputs_scale(NCH - 1)
        act.wait_ge(s.zs_proj, 2)
        act.dma_start(C0, t["C0"].rearrange("p h b v -> p (h b) v")).then_inc(s.state_in, 16)
        act.dma_start(S0, t["S0"].rearrange("p h b v -> p (h b) v")).then_inc(s.state_in, 16)
        ln_scale(NCH - 2)
        turned_outputs(NCH - 1)
        act.wait_ge(s.sgates_arg, 1)
        tell(A(SC[:, 8 * HB:11 * HB], SC[:, 8 * HB:11 * HB], ACT.Exp), s.sgates_exp)
        act.wait_ge(s.ogate_arg, 1)
        tell(A(T[11], T[12], ACT.Exp, scale=-1.0), s.ogate_exp)
        act.wait_ge(s.sgates_arg, 2)
        tell(A(TH[14], TH[14], ACT.Exp), s.sgates_exp)
        act.wait_ge(s.ogate_arg, 2)
        tell(A(TH[11], TH[12], ACT.Exp, scale=-1.0), s.ogate_exp)
        x1_evacuate(NCH - 2)
        ln_scale(NCH - 1)

        def spread_v(kind):
            for e in range(HB):
                i = A(vdiag[kind][:, e], kvT[kind][:, P:2 * P], ACT.Copy, scale=ident[0:HB, e:e + 1])
            tell(i, s.vdiag_ready)

        def norm_scale(kind):
            rs = (T, TH)[kind][13]
            act.wait_ge(s.sq_sum, kind + 1)
            link(A(rs, PS[:, 2 * kind, 96:128], ACT.Ln, scale=1.0 / P, bias=rms_eps))
            tell(A(rs, rs, ACT.Exp, scale=-0.5), s.srstd)

        for kind in range(2):
            act.wait_ge(s.kv_turned, kind + 1)
            tell(A(kvT[kind], PS[0:HB, 2 * kind + 1, 0:3 * P], ACT.Copy), s.kv_read)
            act.wait_ge(s.kv_read, kind + 1)
            if kind == 0:
                act.wait_ge(s.mixed, NCH)
                spread_v(0)
        norm_scale(0)
        x1_evacuate(NCH - 1)
        norm_scale(1)
        spread_v(1)
        ln_scale(NCH)
        read_outer(act, range(3))
        x1_evacuate(NCH)
        scalar_moe(act, link, tell)

    def pool_rest(pool, link, tell):
        g = nc.gpsimd

        def ln_gain(c):
            r = x_rows(c)
            pool.wait_ge(s.normed, c + 1)
            if c == 0:
                pool.wait_ge(s.mixer_in, 16 * 5)
            link(g.tensor_tensor(xrow[0:r], xrow[0:r], ln_gb[0:r, 0], ALU.mult))

        def ln_shift(c):
            r = x_rows(c)
            tell(g.tensor_tensor(xrow[0:r], xrow[0:r], ln_gb[0:r, 1], ALU.add), s.x1_ready)

        def level_scale(n):
            c, l = divmod(n, NLEV)
            if c == NCH:
                return
            b = LEVELS[l]
            pool.wait_ge(s.level_exp, n + 1)
            for half, src in ((0, K), (1, Q)):
                x = xlev[n % 2].rearrange("p h (n w b) -> p h n w b", w=2, b=b)[:, :, :, half]
                y = src[:, :, c * P:(c + 1) * P].rearrange("p h (n w b) -> p h n w b", w=2, b=b)[:, :, :, half]
                tell(g.tensor_tensor(x, x, y, ALU.mult), s.level_scaled)

        level_scale(0)
        level_scale(1)
        for c in range(NCH):
            pool.wait_ge(s.kend_exp, c + 1)
            tell(g.tensor_tensor(kend, kend, K[:, :, c * P:(c + 1) * P], ALU.mult), s.kend_ready)
            for l in range(2, NLEV + 2):
                level_scale(NLEV * c + l)
                if l == 4 and c >= 2:
                    ln_gain(c - 2)
                if l == 5 and c >= 2:
                    ln_shift(c - 2)
        for c in range(NCH - 2, NCH):
            ln_gain(c)
            ln_shift(c)
        for kind in range(2):
            state, decay = ((C0, T[9]), (S0, TH[14]))[kind]
            pool.wait_ge(s.dots, kind + 1)
            pool.wait_ge(s.kv_in, kind + 1)
            link(g.tensor_tensor(state, state, decay.unsqueeze(2).to_broadcast([P, HB, P]), ALU.mult))
        def add_outer(m):
            part = (C0, S0)[m // 8][:, 4 * (m % 8):4 * (m % 8) + 4, :]
            pool.wait_ge(s.outer_read, m + 1)
            tell(g.tensor_tensor(part, part, kv_outer[m % 3].rearrange("p (a v) -> p a v", a=4), ALU.add), s.state_added)

        for m in range(12):
            add_outer(m)
        pool_moe(pool, link, tell, add_outer)

    def vector_rest(dve, link, tell):
        v = nc.vector
        by_h = lambda ap: ap.rearrange("p (h t) -> p h t", h=H)
        link(v.memset(R[:, 180:360], 0.0))
        dve.wait_ge(s.h_turned, NCH)
        dve.wait_ge(s.masks_made, 1)

        def residual_sum(c):
            r = x_rows(c)
            dve.wait_ge(s.mixed, c + 1)
            dve.wait_ge(s.x_in, 16 * (c + 1))
            for n in range(2):
                half = xrow[0:r, n * 512:(n + 1) * 512]
                i = v.scalar_tensor_tensor(half, half, ALPHA, PS[0:r, 6 + n, :], ALU.mult, ALU.add)
            tell(i, s.residual)
            for n in range(2):
                i = v.bn_stats(stats[0:r, n], xrow[0:r, n * 512:(n + 1) * 512])
            link(i)
            tell(v.bn_aggr(mv[0:r], stats[0:r]), s.moments)

        def residual_norm(c):
            r = x_rows(c)
            dve.wait_ge(s.lstd_ready, c + 1)
            tell(v.tensor_scalar(xrow[0:r], xrow[0:r], mv[0:r, 0:1], lstd[0:r], ALU.subtract, ALU.mult), s.normed)

        def logits(c):
            r = x_rows(c)
            dve.wait_ge(s.routed, c + 1)
            dve.wait_ge(s.mixer_in, 16 * 5)
            tell(v.tensor_tensor(LG[0:r, c], PS[0:r, 5, 0:NG + NE], b_r[0:r], ALU.add), s.logits_read)

        def outputs_gate(c):
            dve.wait_ge(s.o_scaled, c + 1)
            tell(v.tensor_tensor(hmix, hmix, gtb, ALU.mult), s.on_ready)

        def level_arg(n):
            c, l = divmod(n, NLEV)
            if c == NCH:
                return
            b = LEVELS[l]
            if n >= 2:
                dve.wait_ge(s.levels, (NLEV + 1) * ((n - 2) // NLEV) + (n - 2) % NLEV + 1)
            gv = G[:, :, c * P:(c + 1) * P].rearrange("p h (n w b) -> p h n w b", w=2, b=b)
            xv = xlev[n % 2].rearrange("p h (n w b) -> p h n w b", w=2, b=b)
            ref = gv[:, :, :, 0, b - 1:b].to_broadcast([P, H, P // (2 * b), b])
            v.tensor_tensor(xv[:, :, :, 0], ref, gv[:, :, :, 0], ALU.subtract)
            tell(v.tensor_tensor(xv[:, :, :, 1], gv[:, :, :, 1], ref, ALU.subtract), s.level_arg)

        def keep_level(c, l):
            n = (NLEV + 1) * c + l
            dve.wait_ge(s.levels, n + 1)
            tell(v.copy_predicated(amat, msk[:, l:l + 1, :].to_broadcast([P, H, P]), by_h(PS[:, 2 + n % 2, :])), s.level_kept)

        def state_update(c):
            dve.wait_ge(s.s_upd, c + 1)
            for h in range(H):
                ps = PS[:, 5, h * P:(h + 1) * P]
                if c == 0:
                    i = v.tensor_copy(Sst[:, h], ps)
                else:
                    i = v.scalar_tensor_tensor(Sst[:, h], Sst[:, h], egend[:, h:h + 1], ps, ALU.mult, ALU.add)
            tell(i, s.hgs_ready)

        level_arg(0)
        level_arg(1)
        samples_rows(dve, tell, 1, (0, 1), zrow[0])
        samples_bias(dve, tell, 1, 0)
        for c in range(NCH):
            tok = slice(c * P, (c + 1) * P)
            if c >= 1:
                state_update(c - 1)
            tell(v.tensor_tensor(kend, G[:, :, c * P + P - 1:(c + 1) * P].to_broadcast([P, H, P]), G[:, :, tok], ALU.subtract), s.kend_arg)
            link(v.memset(amat, 0.0))
            for l in range(2, NLEV + 2):
                level_arg(NLEV * c + l)
                keep_level(c, l - 2)
                if l == 2 and c >= 2:
                    residual_sum(c - 2)
                if l == 3:
                    if c >= 1:
                        outputs_gate(c - 1)
                    if c >= 3:
                        logits(c - 3)
                if l == 4 and c >= 2:
                    residual_norm(c - 2)
                if l == 5:
                    if c == 0:
                        dve.wait_ge(s.bias2_in, 16)
                    dve.wait_ge(s.i_proj, c + 1)
                    tell(v.tensor_tensor(ibuf, by_h(PS[:, 0, :]), by_h(bias[:, 0:512]), ALU.add), s.i_ready)
                    dve.wait_ge(s.gt_proj, c + 1)
                    tell(v.tensor_tensor(gtb, by_h(PS[:, 1, :]), by_h(bias[:, 512:1024]), ALU.add), s.gt_biased)
                if l == 6:
                    dve.wait_ge(s.g_exp, c + 1)
                    link(v.tensor_copy(egend, qdec[:, :, P - 1]))
                    tell(v.tensor_tensor(qdec, qdec, Q[:, :, tok], ALU.mult), s.qg_ready)
                    dve.wait_ge(s.kend_turned, c + 1)
                    tell(v.tensor_copy(kend, by_h(PS[:, 0, :])), s.kend_tm)
                if l == 7:
                    dve.wait_ge(s.gt_exp, c + 1)
                    link(v.tensor_scalar(PS[:, 1, :], PS[:, 1, :], 1.0, None, ALU.add))
                    link(v.reciprocal(PS[:, 1, :], PS[:, 1, :]))
                    tell(v.tensor_tensor(gtb, gtb, by_h(PS[:, 1, :]), ALU.mult), s.gt_gated)
            keep_level(c, NLEV)
        samples_rows(dve, tell, 2, (0, 1), zrow[1])
        state_update(NCH - 1)
        residual_sum(NCH - 2)
        for q in q_apart:
            link(v.memset(q, 0.0))
        outputs_gate(NCH - 1)
        logits(NCH - 3)
        residual_norm(NCH - 2)
        samples_bias(dve, tell, 2, 0)

        dve.wait_ge(s.mixer_in, 16 * 5)
        dve.wait_ge(s.zs_read, 2)
        a, dd, dec, nm = T[7], T[8], T[9], T[10]
        hb = by_hb
        li, lf, mb = gs[:, :, 0], gs[:, :, 1], gs[:, :, 2]
        link(v.tensor_tensor(hb(a), li, lf, ALU.subtract))
        link(v.tensor_tensor(hb(T[6]), hb(a), mb, ALU.max))
        link(v.tensor_tensor(dd, a, T[6], ALU.subtract))
        link(v.tensor_tensor(hb(dec), mb, hb(T[6]), ALU.subtract))
        link(v.tensor_tensor(hb(T[21]), hb(T[6]), lf, ALU.add))
        tell(v.tensor_scalar(nm, T[21], -1.0, None, ALU.mult), s.sgates_arg)
        qs, ks = conv_ps[:, 0:HB], conv_ps[:, HB:2 * HB]
        flat = lambda ap: ap.rearrange("p h b -> p (h b)")
        link(v.tensor_copy(q_apart[0][:, 0:HB * HB:HB + 1], qs))
        link(v.tensor_tensor(T[0], qs, ks, ALU.mult))
        tell(v.tensor_tensor(T[1], qs, n0, ALU.mult), s.dots_in)
        dve.wait_ge(s.sgates_exp, 1)
        link(v.tensor_scalar(dd, dd, KSCALE, None, ALU.mult))
        link(v.tensor_tensor(T[3], ks, dd, ALU.mult))
        tell(v.tensor_copy(T[4], flat(zs[:, 0:4])), s.kv_in)
        tell(v.tensor_copy(T[12], flat(zs[:, 4:8])), s.ogate_arg)
        kS, qS = K[:, :, NP_:NT], Q[:, :, NP_:NT]
        tell(v.tensor_copy(hb(TH[14]), G[:, :, NP_:NT]), s.sgates_arg)
        link(v.tensor_tensor(hb(TH[0]), qS, kS, ALU.mult))
        dve.wait_ge(s.sgates_exp, 2)
        link(v.tensor_tensor(hb(TH[2]), qS, hb(TH[14]), ALU.mult))
        tell(v.tensor_copy(q_apart[1][:, 0:HB * HB:HB + 1], TH[2]), s.dots_in)
        link(v.tensor_copy(hb(TH[3]), kS))
        tell(v.tensor_copy(TH[4], flat(zs[:, 8:12])), s.kv_in)
        tell(v.tensor_copy(TH[12], flat(zs[:, 12:16])), s.ogate_arg)
        link(v.tensor_tensor(T[20], n0, dec, ALU.mult))
        link(v.tensor_tensor(T[20], T[20], T[3], ALU.add))
        logits(NCH - 2)
        residual_sum(NCH - 1)
        residual_norm(NCH - 1)
        for kind in range(2):
            gate = (T, TH)[kind][11]
            dve.wait_ge(s.ogate_exp, kind + 1)
            link(v.tensor_scalar(gate, gate, 1.0, None, ALU.add))
            link(v.reciprocal(gate, gate))
        link(v.tensor_tensor(TH[11], TH[11], TH[12], ALU.mult))
        dve.wait_ge(s.dots, 1)
        link(v.tensor_tensor(T[15], PS[:, 0, 0:HB], dd, ALU.mult))
        link(v.tensor_tensor(T[16], PS[:, 0, HB:2 * HB], dec, ALU.mult))
        link(v.tensor_tensor(T[16], T[16], T[15], ALU.add))
        link(v.tensor_scalar(T[17], T[16], -1.0, None, ALU.mult))
        link(v.tensor_tensor(T[16], T[16], T[17], ALU.max))
        link(v.tensor_tensor(T[16], T[16], nm, ALU.max))
        link(v.reciprocal(T[16], T[16]))
        link(v.tensor_tensor(T[17], PS[:, 0, 2 * HB:3 * HB], dec, ALU.mult))
        link(v.tensor_tensor(T[15], T[15], T[4], ALU.mult))
        link(v.tensor_tensor(T[15], T[15], T[17], ALU.add))
        link(v.tensor_tensor(T[15], T[15], T[16], ALU.mult))
        link(v.tensor_tensor(T[15], T[15], T[11], ALU.mult))
        tell(v.tensor_tensor(T[5], T[15], T[15], ALU.mult), s.sq_in)
        dve.wait_ge(s.dots, 2)
        link(v.tensor_tensor(TH[15], PS[:, 2, 0:HB], TH[4], ALU.mult))
        link(v.tensor_tensor(TH[15], TH[15], PS[:, 2, 2 * HB:3 * HB], ALU.add))
        tell(v.tensor_tensor(TH[5], TH[15], TH[15], ALU.mult), s.sq_in)
        for kind in range(2):
            tiles = (T, TH)[kind]
            mix = mixS[:, 4 * kind:4 * kind + 4]
            dve.wait_ge(s.srstd, kind + 1)
            link(v.tensor_tensor(flat(mix), tiles[15], tiles[13], ALU.mult))
            if kind == 1:
                link(v.tensor_tensor(flat(mix), flat(mix), TH[11], ALU.mult))
            gain = g_mix[:, 4 * kind:4 * kind + 4].unsqueeze(2).to_broadcast([P, H, NS])
            tell(v.tensor_tensor(mix, mix, gain, ALU.mult), s.mixS_ready)
        logits(NCH - 1)
        residual_sum(NCH)
        residual_norm(NCH)
        row = xrow[0:NS]
        dve.wait_ge(s.normed, NTT)
        link(v.tensor_tensor(row, row, ln_gb[0:NS, 0], ALU.mult))
        dve.wait_ge(s.x1_ready, NCH)
        tell(v.tensor_tensor(row, row, ln_gb[0:NS, 1], ALU.add), s.x1_ready)
        logits(NCH)
        vector_moe(dve, link, tell)

    y_sems = (s.yg_in0, s.yg_in1, s.yg_in2, s.yg_in3, s.yg_in4, s.yg_in5)
    def pairs_loop(eng, step):
        for pair in range(2):
            for i in range(2):
                step(pair, i, False)
        with eng.Fori(2, TILES // 2 - 1) as pair:
            for i in range(2):
                step(pair, i, False)
        for i in range(2):
            step(TILES // 2 - 1, i, True)

    def tile_before(pair, i):
        return (pair, 0) if i == 1 else (pair - 1, 1)

    def is_first(pair, i=0):
        return isinstance(pair, int) and pair == 0 and i == 0

    early_outs = []

    def sync_moe(sp, keep_x1):
        wg = t["w_gate"].rearrange("e (p k) f -> e p k f", k=KD)
        wu = t["w_up"].rearrange("e (p k) f -> e p k f", k=KD)
        wd = t["w_down"].rearrange("e (p k) n -> e p k n", k=2)

        def load_up(pair, i, expert):
            for n, w in enumerate((wg, wu)):
                sp.dma_start(w_gu[i][:, :, n], w[bass.ds(expert, 1)].rearrange("e p k f -> p (e k) f")).then_inc((s.w_gu_in0, s.w_gu_in1)[i], 16)

        def load_down(pair, i, expert):
            sp.dma_start(w_dn[i], wd[bass.ds(expert, 1)].rearrange("e p k n -> p (e k) n")).then_inc((s.w_dn_in0, s.w_dn_in1)[i], 16)

        def expert_of(pair, i):
            return sp.value_load(tile_expert[0:1, bass.ds(pair * 2 + i, 1)].bitcast(I32), min_val=0, max_val=NE - 1)

        sp.wait_ge(s.experts_known, 1)
        sp.wait_ge(s.mixed, NTT)
        for i in (1, 0):
            if i == 0:
                sp.wait_ge(s.outer, 8)
            e = expert_of(0, i)
            load_up(0, i, e)
            if i == 0:
                sp.wait_ge(s.outer, 16)
            load_down(0, i, e)
        early_outs.append(outs[0])
        sp.wait_ge(s.outputs, 16 * early_outs[0])
        sp.wait_ge(s.xg_in0, 16)
        sp.wait_ge(s.xg_in1, 16)
        keep_x1(4)
        sp.dma_start(x1_keep[8][0:NS], x1_dram[NP_:NT]).then_inc(s.x1_back, 16)

        def step(pair, i, last):
            done = pair * 2 + (i + 1)
            if last and i == 0:
                sp.dma_start(ln2_gb, t["ln2"].partition_broadcast(P)).then_inc(s.ln2_in, 16)
                sp.wait_ge(s.state_added, 16)
                out_dma(sp, t["out_S_s"].rearrange("p h b v -> p (h b) v"), S0)
            if not last:
                e = expert_of(pair + 1, i)
                sp.wait_ge(s.up_done, done)
                load_up(pair + 1, i, e)
                sp.wait_ge(s.down_done, done)
                load_down(pair + 1, i, e)
            sp.wait_ge(s.y_read, done * 2)
            sp.dma_start(y_slots[bass.ds((pair * 2 + i) * P, P)], ysb[i]).then_inc((s.y_out0, s.y_out1)[i], 16)

        pairs_loop(sp, step)
        for c in range(NTT):
            r = x_rows(c)
            sp.wait_ge(s.y_ready, c + 1)
            out_dma(sp, t["out_y"][c * P:c * P + r], x1_keep[c][0:r])
        sp.wait_ge(s.outputs, 16 * outs[0])

    def tensor_moe(pe, outer_product):
        mm = nc.tensor.matmul
        pe.wait_ge(s.onehots, 1)
        for q in range(2 * NTT):
            i = mm(PS[:, 6, 0:64], oh_lo[:, q], oh_hi[:, q].rearrange("p w n -> p (w n)"), start=(q == 0), stop=(q == 2 * NTT - 1))
        i.then_inc(s.slots, 1)
        for m in range(12, 16):
            outer_product(m)

        def turn_x(pair, i):
            pe.wait_ge((s.xg_in0, s.xg_in1)[i], pair * 16 + 16)
            for k in range(KD):
                m = nc.tensor.transpose(PS[:, k // 4, (k % 4) * P:(k % 4 + 1) * P], xg[i][:, k:D:KD], ident)
            m.then_inc(s.xg_turned, 1)

        def down(pair, i):
            n = pair * 2 + i
            pe.wait_ge(s.hidT_ready, n + 1)
            pe.wait_ge((s.w_dn_in0, s.w_dn_in1)[i], pair * 16 + 16)
            if is_first(pair, i):
                pe.wait_ge(s.residual, NTT)
            else:
                pe.wait_ge(s.y_read, n * 2)
            for half in range(2):
                for k in range(2):
                    m = mm(PS[:, 5 + half, :], hidT[:, k], w_dn[i][:, k, half * 512:(half + 1) * 512], start=(k == 0), stop=(k == 1))
            m.then_inc(s.down_done, 1)

        pe.wait_ge(s.state_added, 16)
        turn_x(0, 0)

        def step(pair, i, last):
            n = pair * 2 + i
            pe.wait_ge(s.xgT_ready, n * 2 + 2)
            pe.wait_ge((s.w_gu_in0, s.w_gu_in1)[i], pair * 32 + 32)
            if is_first(pair, i):
                pe.wait_ge(s.tiles_known, 1)
                pe.wait_ge(s.logits_read, NTT)
            else:
                pe.wait_ge(s.hid_ready, n)
            for g, sem in ((0, s.gate_done), (1, s.up_done)):
                for k in range(KD):
                    m = mm(PS[:, 2 + g, 0:FF], xgT[i][:, k], w_gu[i][:, k, g], start=(k == 0), stop=(k == KD - 1))
                m.then_inc(sem, 1)
            if not (last and i == 1):
                turn_x(pair + i, 1 - i)
            if not is_first(pair, i):
                down(*tile_before(pair, i))
            pe.wait_ge(s.hid_ready, n + 1)
            for k in range(2):
                m = nc.tensor.transpose(PS[:, 4, k * P:(k + 1) * P], hid[:, k:FF:2], ident)
            m.then_inc(s.hid_turned, 1)

        pairs_loop(pe, step)
        down(TILES // 2 - 1, 1)

    def scalar_moe(act, link, tell):
        A = nc.scalar.activation
        act.wait_ge(s.route_arg, 1)
        tell(A(gexp, gexp, ACT.Exp), s.route_exp)
        read_outer(act, range(3, 6))
        act.wait_ge(s.route_arg, 2)
        tell(A(e2, e2, ACT.Exp), s.route_exp)
        read_outer(act, range(6, 16))

        def x_half(pair, i):
            n = pair * 2 + i
            act.wait_ge(s.xg_turned, n + 1)
            if not is_first(pair):
                act.wait_ge(s.up_done, n - 1)
            A(xgT[i][:, 0:4], PS[:, 0, :].rearrange("p (k t) -> p k t", k=4), ACT.Copy).then_inc(s.xgT_ready, 1)

        def y_half(pair, i):
            act.wait_ge(s.down_done, pair * 2 + (i + 1))
            if not is_first(pair):
                act.wait_ge((s.y_out0, s.y_out1)[i], pair * 16)
            A(ysb[i][:, 0:512], PS[:, 5, :], ACT.Copy).then_inc(s.y_read, 1)

        x_half(0, 0)

        def step(pair, i, last):
            n = pair * 2 + i
            act.wait_ge(s.gate_done, n + 1)
            if not is_first(pair, i):
                act.wait_ge(s.hid_ready, n)
            A(silu, PS[:, 2, 0:FF], ACT.Silu).then_inc(s.silu_ready, 1)
            if not (last and i == 1):
                x_half(pair + i, 1 - i)
            if not is_first(pair, i):
                y_half(*tile_before(pair, i))

        pairs_loop(act, step)
        y_half(TILES // 2 - 1, 1)
        nc.scalar.preload_act_table_set("natural_log_exp_and_others")
        for c in range(NTT):
            r = x_rows(c)
            x = x1_keep[c][0:r]
            act.wait_ge(s.moments, NTT + c + 1)
            link(A(fsd[0:r, c:c + 1], fmv[0:r, c, 1:2], ACT.Ln, bias=ln_eps[0:r]))
            link(A(fsd[0:r, c:c + 1], fsd[0:r, c:c + 1], ACT.Exp, scale=-0.5))
            link(A(fshift[0:r, c:c + 1], fshift[0:r, c:c + 1], ACT.Copy, scale=fsd[0:r, c:c + 1]))
            tell(A(x, x, ACT.Identity, bias=fshift[0:r, c:c + 1], scale=fsd[0:r, c:c + 1]), s.lstd_ready)

    def pool_moe(pool, link, tell, add_outer):
        g = nc.gpsimd
        pool.wait_ge(s.tiles_known, 1)
        pool.wait_ge(s.x1_written, 16 * NTT)

        pool.wait_ge(s.routed, NTT)
        pool.wait_ge(s.outputs, 16 * early_outs[0])
        pool.wait_ge(s.normed, NTT)
        for n in range(TILES):
            if n >= 2:
                pool.wait_ge(s.xg_turned, n - 1)
                pool.wait_ge(s.hid_ready, n - 1)
            off = bass.IndirectOffsetOnAxis(slot_tok[:, n:n + 1].bitcast(U32), 0)
            g.indirect_dma_start(xg[n % 2], None, x1_dram, off).then_inc((s.xg_in0, s.xg_in1)[n % 2], 16)
            g.tensor_copy(gate_c[n % 2], slot_gate[:, n:n + 1]).then_inc(s.gate_ready, 1)
            if n == 1:
                for m in range(12, 16):
                    add_outer(m)
            if n == 4:
                pool.wait_ge(s.x1_back, 48)
            if 4 <= n < 4 + NTT:
                x = x1_keep[n - 4][0:x_rows(n - 4)]
                link(g.tensor_scalar(x, x, ALPHA, None, ALU.mult))
        pool.wait_ge(s.y_out0, 16 * (TILES // 2))
        pool.wait_ge(s.y_out1, 16 * (TILES // 2))
        pool.wait_ge(s.slots, 1)

        def add_rows(k, c):
            off = bass.IndirectOffsetOnAxis(pos_i[0:x_rows(c), k * NTT + c:k * NTT + c + 1].bitcast(U32), 0)
            i = g.indirect_dma_start(x1_keep[c][0:x_rows(c)], None, y_slots, off, compute_op=ALU.add)
            i.then_inc(y_sems[c % 6], 16)

        for c in range(NTT + 3):
            if c < NTT:
                if c >= 6:
                    pool.wait_ge(y_sems[c % 6], 32)
                add_rows(0, c)
            if c >= 3:
                pool.wait_ge(y_sems[(c - 3) % 6], 32 * ((c - 3) // 6) + 16)
                add_rows(1, c - 3)
        pool.wait_ge(s.ln2_in, 16)
        for c in range(Y_SHIFTED, NTT):
            r = x_rows(c)
            pool.wait_ge(s.y_scaled, c + 1)
            tell(g.tensor_tensor(x1_keep[c][0:r], x1_keep[c][0:r], ln2_gb[0:r, 1], ALU.add), s.y_ready)

    def vector_moe(dve, link, tell):
        v = nc.vector
        last4 = lambda ap: ap.unsqueeze(2).to_broadcast([P, NTT, 4])
        valid = const("valid")
        dve.wait_ge(s.mixed, NTT)

        def first_hot(out, vals, top):
            link(v.tensor_tensor(scr, vals, last4(top), ALU.is_ge))
            link(v.tensor_tensor(scr, scr, const("first").unsqueeze(1).to_broadcast([P, NTT, 4]), ALU.mult))
            link(v.tensor_reduce(s2, scr, X, ALU.max))
            link(v.tensor_tensor(out, scr, last4(s2), ALU.is_equal))

        lg = LG[:, :, 0:NG]
        link(v.tensor_reduce(gmax, lg, X, ALU.max))
        tell(v.tensor_tensor(gexp, lg, last4(gmax), ALU.subtract), s.route_arg)
        first_hot(ghot, lg, gmax)
        dve.wait_ge(s.route_exp, 1)
        link(v.tensor_reduce(gden, gexp, X, ALU.add))
        link(v.reciprocal(gden, gden))
        le = LG[:, :, NG:].rearrange("p i (g j) -> p i g j", g=NG)
        link(v.tensor_tensor(le_m, le, ghot.unsqueeze(3).to_broadcast([P, NTT, NG, NJ]), ALU.mult))
        link(v.tensor_reduce(leg, le_m.rearrange("p i g j -> p i j g"), X, ALU.add))
        link(v.tensor_reduce(v1, leg, X, ALU.max))
        first_hot(hot[0], leg, v1)
        link(v.scalar_tensor_tensor(leg2, hot[0], -BIG, leg, ALU.mult, ALU.add))
        link(v.tensor_reduce(v2, leg2, X, ALU.max))
        first_hot(hot[1], leg2, v2)
        tell(v.tensor_tensor(e2, v2, v1, ALU.subtract), s.route_arg)
        for k in range(2):
            e4 = ex[k].rearrange("p i (g j) -> p i g j", g=NG)
            link(v.tensor_tensor(e4, ghot.unsqueeze(3).to_broadcast([P, NTT, NG, NJ]),
                                 hot[k].unsqueeze(2).to_broadcast([P, NTT, NG, NJ]), ALU.mult))
            link(v.tensor_tensor(ex[k], ex[k], valid.unsqueeze(2).to_broadcast([P, NTT, NE]), ALU.mult))
        tell(v.tensor_tensor(esum, ex[0], ex[1], ALU.add), s.esum_ready)
        dve.wait_ge(s.route_exp, 2)
        link(v.tensor_scalar(s2, e2, 1.0, None, ALU.add))
        link(v.reciprocal(s2, s2))
        link(v.tensor_tensor(s2, s2, gden, ALU.mult))
        link(v.tensor_tensor(wts[:, 0], s2, valid, ALU.mult))
        link(v.tensor_tensor(wts[:, 1], wts[:, 0], e2, ALU.mult))
        dve.wait_ge(s.ranked, 1)
        link(v.tensor_copy(tot, PS[:, 7, 0:NTT * NE].rearrange("p (i e) -> p i e", e=NE)))
        link(v.memset(cnt[:, 0], 0.0))
        for c in range(1, NTT):
            link(v.tensor_tensor(cnt[:, c], cnt[:, c - 1], tot[:, c - 1], ALU.add))
        link(v.tensor_tensor(n_e, cnt[:, NTT - 1], tot[:, NTT - 1], ALU.add))
        link(v.tensor_tensor(slotp, cnt, PS[:, 6, 0:NTT * NE].rearrange("p (i e) -> p i e", e=NE), ALU.add))
        link(v.tensor_tensor(cmp9, n_e.unsqueeze(2).to_broadcast([P, NE, NTT]),
                             const("full").unsqueeze(1).to_broadcast([P, NE, NTT]), ALU.is_gt))
        link(v.tensor_reduce(nt_e, cmp9, X, ALU.add))
        link(v.tensor_tensor_scan(end_e, ones[:, 0:NE], nt_e, 0.0, ALU.mult, ALU.add))
        link(v.tensor_tensor(base_e, end_e, nt_e, ALU.subtract))
        link(v.tensor_scalar(base_e, base_e, float(P), None, ALU.mult))
        link(v.tensor_tensor(slotp, slotp, base_e.unsqueeze(1).to_broadcast([P, NTT, NE]), ALU.add))
        for k in range(2):
            link(v.tensor_tensor(ex[k], ex[k], slotp, ALU.mult))
            link(v.tensor_reduce(pos[:, k * NTT:(k + 1) * NTT], ex[k], X, ALU.add))
        link(v.tensor_copy(pos_i, pos))
        link(v.tensor_scalar(hi_i, pos_i, 7, None, ALU.arith_shift_right))
        link(v.tensor_scalar(lo_i, pos_i, P - 1, None, ALU.bitwise_and))
        link(v.tensor_copy(hi_f, hi_i))
        link(v.tensor_copy(lo_f, lo_i))
        link(v.tensor_tensor(cmp32, const("lane")[:, 0:TILES].unsqueeze(2).to_broadcast([P, TILES, NE]),
                             end_e.unsqueeze(1).to_broadcast([P, TILES, NE]), ALU.is_ge))
        link(v.tensor_reduce(slot_gate, cmp32, X, ALU.add))
        link(v.tensor_scalar(slot_gate, slot_gate, float(NE - 1), None, ALU.min))
        tell(v.tensor_copy(tile_expert.bitcast(I32), slot_gate), s.experts_known)
        q18 = 2 * NTT
        link(v.tensor_tensor(oh_lo, const("lane").unsqueeze(1).to_broadcast([P, q18, P]), lo_f.unsqueeze(2).to_broadcast([P, q18, P]), ALU.is_equal))
        link(v.tensor_tensor(oh_hi[:, :, 0], const("lane")[:, 0:TILES].unsqueeze(1).to_broadcast([P, q18, TILES]),
                             hi_f.unsqueeze(2).to_broadcast([P, q18, TILES]), ALU.is_equal))
        link(v.tensor_tensor(oh_hi[:, :, 1], oh_hi[:, :, 0], wts.rearrange("p w i -> p (w i)").unsqueeze(2).to_broadcast([P, q18, TILES]), ALU.mult))
        for k in range(2):
            part = oh_hi[:, k * NTT:(k + 1) * NTT, 0]
            i = v.tensor_tensor(part, part, const("token").unsqueeze(2).to_broadcast([P, NTT, TILES]), ALU.mult)
        tell(i, s.onehots)
        dve.wait_ge(s.slots, 1)
        link(v.tensor_copy(slot_tok, PS[:, 6, 0:32]))
        tell(v.tensor_copy(slot_gate, PS[:, 6, 32:64]), s.tiles_known)

        def x_half(pair, i):
            n = pair * 2 + i
            dve.wait_ge(s.xg_turned, n + 1)
            if not is_first(pair):
                dve.wait_ge(s.up_done, n - 1)
            v.tensor_copy(xgT[i][:, 4:8], PS[:, 1, :].rearrange("p (k t) -> p k t", k=4)).then_inc(s.xgT_ready, 1)

        def y_half(pair, i):
            dve.wait_ge(s.down_done, pair * 2 + (i + 1))
            if not is_first(pair):
                dve.wait_ge((s.y_out0, s.y_out1)[i], pair * 16)
            v.tensor_copy(ysb[i][:, 512:1024], PS[:, 6, :]).then_inc(s.y_read, 1)

        x_half(0, 0)

        def step(pair, i, last):
            n = pair * 2 + i
            dve.wait_ge(s.silu_ready, n + 1)
            dve.wait_ge(s.gate_ready, n + 1)
            if not is_first(pair, i):
                dve.wait_ge(s.hid_turned, n)
            dve.wait_ge(s.up_done, n + 1)
            v.scalar_tensor_tensor(hid, silu, gate_c[i], PS[:, 3, 0:FF], ALU.mult, ALU.mult).then_inc(s.hid_ready, 1)
            if not (last and i == 1):
                x_half(pair + i, 1 - i)
            dve.wait_ge(s.hid_turned, n + 1)
            if not is_first(pair, i):
                dve.wait_ge(s.down_done, n)
            v.tensor_copy(hidT, PS[:, 4, 0:2 * P].rearrange("p (k t) -> p k t", k=2)).then_inc(s.hidT_ready, 1)
            if not is_first(pair, i):
                y_half(*tile_before(pair, i))

        pairs_loop(dve, step)
        y_half(TILES // 2 - 1, 1)

        dve.wait_ge(s.ln2_in, 16)
        for c in range(NTT + 1):
            if c < NTT:
                r = x_rows(c)
                dve.wait_ge(y_sems[c % 6], 32 * (c // 6 + 1))
                for n in range(2):
                    i = v.bn_stats(fst[0:r, c, n], x1_keep[c][0:r, n * 512:(n + 1) * 512])
                link(i)
                link(v.bn_aggr(fmv[0:r, c], fst[0:r, c]))
                tell(v.tensor_scalar(fshift[0:r, c:c + 1], fmv[0:r, c, 0:1], -1.0, None, ALU.mult), s.moments)
            if c >= 1:
                x = x1_keep[c - 1][0:x_rows(c - 1)]
                dve.wait_ge(s.lstd_ready, NTT + c)
                tell(v.tensor_tensor(x, x, ln2_gb[0:x_rows(c - 1), 0], ALU.mult), s.y_scaled)
                if c - 1 < Y_SHIFTED:
                    tell(v.tensor_tensor(x, x, ln2_gb[0:x_rows(c - 1), 1], ALU.add), s.y_ready)

    block = ctx.enter_context(nc.Block())

    @block.sync
    def _(sp):
        sp.dma_start(wgt, t["wg"]).then_inc(s.wg_in, 16)
        for n in range(3):
            piece = slice(n * PIECE, (n + 1) * PIECE)
            sp.dma_start(xT[:, :, piece], t["xT"][:, :, piece]).then_inc((s.x_in0, s.x_in1, s.x_in2)[n], 16)
        for g in range(7):
            if g == 3:
                sp.wait_ge(s.projected, last_piece(3))
            if g == 4:
                sp.wait_ge(s.projected, last_piece(7))
            if g == 5:
                sp.wait_ge(s.projected, last_piece(11))
            if g == 6:
                sp.wait_ge(s.projected, last_piece(15))
            c0 = GROUPS[g][0]
            sp.dma_start(w_slot(g), w_cols[:, :, c0:c0 + 512]).then_inc(w_sem[g], 16)
            if g == 2:
                sp.dma_start(bias, t["b_row"][:, 0:1024].partition_broadcast(P).rearrange("p a n -> p (a n)")).then_inc(s.bias_in, 16)
        sp.wait_ge(s.conv_done, 9)
        out_dma(sp, t["out_conv_p"], raw_p3)
        out_dma(sp, t["out_conv_s"][:, :, 0:2], sconv[:, :, 1:3])
        out_dma(sp, t["out_conv_s"][:, :, 2], raw_s)
        out_dma(sp, t["out_m_p"], mend[0:H, NCH:])
        sp.wait_ge(s.c_ready, NCH)
        out_dma(sp, t["out_C_p"], Cst)
        sync_rest(sp)

    @block.tensor
    def _(pe):
        mm = nc.tensor.matmul

        def project(idx, lhs_of, m):
            if idx >= 4:
                pe.wait_ge(s.proj_read, idx - 3)
            n = idx % 3
            if idx < 3:
                pe.wait_ge((s.x_in0, s.x_in1, s.x_in2)[n], 16)
            for k in range(KD):
                i = mm(PS[0:m, idx % 4, 0:PIECE], lhs_of(k), xT[:, k, n * PIECE:(n + 1) * PIECE],
                       start=(k == 0), stop=(k == KD - 1))
            i.then_inc(s.projected, 1)

        pe.wait_ge(s.wg_in, 16)
        for n in range(3):
            project(n, lambda k: wgt[:, k, :], 64)
        for u in range(16):
            g, j = u // 4, u % 4
            if j == 0:
                pe.wait_ge(w_sem[g], 16)
            if u == 3:
                pe.wait_ge(s.consts_in, 32)
                pe.wait_ge(s.gate_rows, 2)
                for c in range(NCH):
                    i = nc.tensor.transpose(PS[:, 4 + c // 4, (c % 4) * 96:(c % 4 + 1) * 96],
                                            g3[0:96, c * P:(c + 1) * P], ident[0:96, 0:96])
                for h in range(H):
                    mm(PS[:, 6, h * 9:h * 9 + 9], sel[0:H, h, :], mend[0:H, :], start=True, stop=True)
                for h in range(H):
                    i = mm(PS[:, 6, 64 + h * 24:64 + (h + 1) * 24], sel[0:H, h, :], gs_rows[0:H, :], start=True, stop=True)
                i.then_inc(s.gates_spread, 1)
            for n in range(3):
                project(3 + 3 * u + n, lambda k: w_slot(g)[:, k, j * P:(j + 1) * P], P)

        def tokens_product(bank, g, c, sem):
            for k in range(KD):
                i = mm(PS[:, bank, :], xT[:, k, c * P:(c + 1) * P], w_slot(g)[:, k, :], start=(k == 0), stop=(k == KD - 1))
            i.then_inc(sem, 1)

        for c in range(NCH + 1):
            tok = slice(c * P, (c + 1) * P)
            if c < NCH:
                if c == 0:
                    pe.wait_ge(s.proj_read, PIECES)
                    pe.wait_ge(s.gates_read, 1)
                    pe.wait_ge(s.qk_silu, 8)
                else:
                    pe.wait_ge(s.h_turned_read, c - 1)
                    pe.wait_ge(s.s_ready, c)
                for h in range(H):
                    i = mm(PS[:, 2, h * P:(h + 1) * P], sel[0:H, h, :], negM[:, tok], start=True, stop=True)
                i.then_inc(s.decay_b, 1)
                for h in range(H):
                    i = mm(PS[:, 3, h * P:(h + 1) * P], CC[:, 4 + h, tok], CC[:, h, tok], start=True, stop=True)
                i.then_inc(s.scores, 1)
                if c == 0:
                    pe.wait_ge(s.w_in4, 16)
                else:
                    pe.wait_ge(s.v_ready, c)
                tokens_product(0, 4, c, s.v_proj)
                if c >= 1:
                    pe.wait_ge(s.c_ready, c)
                for h in range(H):
                    i = nc.tensor.transpose(PS[:, 6, h * P:(h + 1) * P], CC[:, 4 + h, tok], ident)
                i.then_inc(s.k_turned, 1)
                if c == 0:
                    pe.wait_ge(s.w_in5, 16)
                else:
                    pe.wait_ge(s.o_biased, c)
                tokens_product(1, 5, c, s.o_proj)
            if c == NCH:
                pe.wait_ge(s.v_ready, NCH)
                pe.wait_ge(s.o_biased, NCH)
                samples_product(pe, (0, 1), (4, 5))
            if c >= 1:
                pe.wait_ge(s.hn_ready, c)
                if c < NCH:
                    pe.wait_ge(s.q_arg, c + 1)
                for h in range(H):
                    i = nc.tensor.transpose(PS[:, 2, h * P:(h + 1) * P], hbuf[:, h], ident)
                i.then_inc(s.h_turned, 1)
            if c < NCH:
                pe.wait_ge(s.s_ready, c + 1)
                pe.wait_ge(s.qd_ready, c + 1)
                pe.wait_ge(s.v_ready, c + 1)
                if c >= 1:
                    pe.wait_ge(s.h_ready, c)
                for h in range(H):
                    out = PS[:, 4 + h // 2, (h % 2) * DV1:(h % 2 + 1) * DV1]
                    i = mm(out, dmat[:, h], vext[c % 2][:, h], start=True, stop=(c == 0))
                    if c >= 1:
                        i = mm(out, qd[:, h], Cst[:, h], start=False, stop=True)
                i.then_inc(s.num, 1)
                pe.wait_ge(s.kw_ready, c + 1)
                for h in range(H):
                    i = mm(PS[:, 6 + h // 2, (h % 2) * DV1:(h % 2 + 1) * DV1], kw[:, h], vext[c % 2][:, h], start=True, stop=True)
                i.then_inc(s.cupd, 1)
        samples_turn(pe, 1, zrow[0], 0)
        tensor_rest(pe)

    @block.scalar
    def _(act):
        link, tell = chain(act, s.act_step), teller(act)
        A = nc.scalar.activation
        act.dma_start(params, t["params"]).then_inc(s.params_in, 16)
        act.dma_start(cst[:, :], t["consts"]).then_inc(s.consts_in, 16)
        act.dma_start(SC[:, 7680:9216], t["masks"]).then_inc(s.consts_in, 16)
        act.wait_ge(s.params_in, 16)

        nc.scalar.preload_act_table_set("natural_log_exp_and_others")
        for idx in range(3):
            act.wait_ge(s.projected, idx + 1)
            tell(A(grow[0:64, idx * PIECE:(idx + 1) * PIECE], PS[0:64, idx % 4, 0:PIECE], ACT.Identity,
              bias=bg[0:64]), s.proj_read)
        act.wait_ge(s.proj_read, 3)
        act.wait_ge(s.consts_in, 32)
        link(A(fr, grow[32:32 + H], ACT.Copy))
        link(A(lnr, fr, ACT.Abs))
        link(A(lnr, lnr, ACT.Exp, scale=-1.0))
        tell(A(lnr, lnr, ACT.Ln, bias=one_col[0:H]), s.forget_ln)

        def read_unit(u, dst):
            e = [20, 21, 22, 23, 16, 17, 18, 19, 0, 1, 2, 3, 4, 5, 6, 7][u]
            for n in range(3):
                idx = 3 + 3 * u + n
                act.wait_ge(s.projected, idx + 1)
                tell(A(dst[:, n * PIECE:(n + 1) * PIECE], PS[:, idx % 4, 0:PIECE], ACT.Identity,
                  bias=b_cm[:, e:e + 1]), s.proj_read)

        for j in range(H):
            read_unit(j, K[:, j])
            act.wait_ge(s.proj_read, last_piece(j))
            link(A(G[:, j], K[:, j], ACT.Abs))
            link(A(G[:, j], G[:, j], ACT.Exp, scale=-1.0))
            tell(A(G[:, j], G[:, j], ACT.Ln, bias=one_col), s.hf_ln)
            if j == 1:
                act.wait_ge(s.gates_z, 1)
                tell(A(g3[32:32 + H], cmx, ACT.Exp), s.gate_rows)
                tell(A(g3[64:64 + H], lnr[:, 0:NP_], ACT.Exp), s.gate_rows)
            if j >= 1:
                act.wait_ge(s.k_arg, j)
                tell(A(K[:, j - 1], K[:, j - 1], ACT.Exp), s.hg_k_ready)
        act.wait_ge(s.k_arg, H)
        tell(A(K[:, 3], K[:, 3], ACT.Exp), s.hg_k_ready)
        for j in range(H):
            read_unit(4 + j, Q[:, j])
            act.wait_ge(s.proj_read, last_piece(4 + j))
            tell(A(Q[:, j], Q[:, j], ACT.Silu), s.hq_silu)
        for ct in range(9):
            if ct < 8:
                if ct >= 2:
                    act.wait_ge(s.conv_done, ct - 1)
                read_unit(8 + ct, raw[ct % 2][:, 3:])
            if ct >= 1:
                act.wait_ge(s.conv_done, ct)
                tell(A(CC[:, ct - 1], CC[:, ct - 1], ACT.Silu), s.qk_silu)
        act.wait_ge(s.conv_done, 9)
        tell(A(conv_ps, conv_ps, ACT.Silu), s.qk_silu)

        nc.scalar.preload_act_table_set("natural_log_exp_and_others")
        for c in range(NCH + 1):
            if c < NCH:
                act.wait_ge(s.d_arg, c + 1)
                tell(A(dmat, dmat, ACT.Exp), s.d_exp)
                act.wait_ge(s.q_arg, c + 1)
                tell(A(qd, qd, ACT.Exp), s.q_exp)
            if c >= 1:
                act.wait_ge(s.h_turned, c)
                for h in range(H):
                    i = A(CC[:, h, (c - 1) * P:c * P], PS[:, 2, h * P:(h + 1) * P], ACT.Copy, scale=g_mix[:, h:h + 1])
                tell(i, s.h_turned_read)
            if c < NCH:
                act.wait_ge(s.o_biased, c + 1)
                tell(A(ogate, ogate, ACT.Exp, scale=-1.0), s.o_exp)
                act.wait_ge(s.ssq_ready, c + 1)
                link(A(rstd, ssq, ACT.Ln, scale=1.0 / P, bias=rms_eps))
                tell(A(rstd, rstd, ACT.Exp, scale=-0.5), s.rstd_ready)
        scalar_rest(act, link, tell)

    @block.gpsimd
    def _(pool):
        link, tell = chain(pool, s.pool_step), teller(pool)
        pool.wait_ge(s.consts_in, 32)
        tell(nc.gpsimd.tensor_copy(msk[:, :, :].rearrange("p l t -> p (l t)"), mask_words), s.masks_made)
        causal = const("causal").unsqueeze(1).to_broadcast([P, H, P])
        for c in range(NCH):
            pool.wait_ge(s.d_exp, c + 1)
            tell(nc.gpsimd.tensor_tensor(dmat, dmat, causal, ALU.mult), s.d_masked)
            pool.wait_ge(s.h_ready, c + 1)
            tell(nc.gpsimd.tensor_tensor(sq, hbuf, hbuf, ALU.mult), s.h_sq)
        pool_rest(pool, link, tell)

    @block.vector
    def _(dve):
        link, tell = chain(dve, s.dve_step), teller(dve)
        v = nc.vector
        link(v.memset(raw[0][:, 0:3], 0.0))
        link(v.memset(raw[1][:, 0:3], 0.0))
        link(v.memset(g3[0:96], 0.0))
        link(v.memset(keep, 1.0))
        link(v.memset(keep[:, 0:NP_:P], 0.0))
        link(v.memset(drop, 0.0))
        link(v.memset(drop[:, 0:NP_:P], -BIG))
        link(v.memset(mend[0:H], 0.0))
        dve.wait_ge(s.params_in, 16)
        dve.wait_ge(s.forget_ln, 1)
        link(v.scalar_tensor_tensor(fr, fr, 0.0, lnr, ALU.min, ALU.subtract))
        link(v.tensor_tensor_scan(Frow, keep, fr[:, 0:NP_], 0.0, ALU.mult, ALU.add))
        link(v.tensor_tensor(g3[0:H], grow[0:H, 0:NP_], Frow, ALU.subtract))
        link(v.tensor_tensor_scan(cmx, drop, g3[0:H], 0.0, ALU.add, ALU.max))
        link(v.tensor_tensor_scan(mend[0:H, 1:], cmx[:, P - 1:NP_:P], Frow[:, P - 1:NP_:P], 0.0, ALU.max, ALU.add))
        by_chunk = lambda r: r.rearrange("p (c t) -> p c t", c=NCH)
        link(v.tensor_tensor(by_chunk(keep), by_chunk(cmx), mend[0:H, 0:NCH].unsqueeze(2).to_broadcast([H, NCH, P]), ALU.max))
        link(v.tensor_scalar(negM, keep, -1.0, None, ALU.mult))
        link(v.scalar_tensor_tensor(lnr[:, 0:NP_], Frow, -1.0, keep, ALU.mult, ALU.subtract))
        link(v.tensor_copy(drop[:, 0:NCH], keep[:, P - 1:NP_:P]))
        link(v.tensor_tensor(by_chunk(cmx), by_chunk(g3[0:H]), drop[:, 0:NCH].unsqueeze(2).to_broadcast([H, NCH, P]), ALU.subtract))
        link(v.tensor_copy(gs_rows[0:H, 0:NS], grow[0:H, NP_:NT]))
        link(v.tensor_copy(gs_rows[0:H, NS:2 * NS], fr[:, NP_:NT]))
        tell(v.tensor_copy(gs_rows[0:H, 2 * NS:], m0[0:H]), s.gates_z)

        for j in range(H):
            dve.wait_ge(s.hf_ln, j + 1)
            link(v.scalar_tensor_tensor(G[:, j], K[:, j], 0.0, G[:, j], ALU.min, ALU.subtract))
            tell(v.tensor_tensor(K[:, j], G[:, j], K[:, j], ALU.subtract), s.k_arg)
        dve.wait_ge(s.gates_spread, 1)
        for n in range(2):
            i = v.tensor_copy(gcol[:, 4 * n:4 * n + 4], PS[:, 4 + n, 0:384].rearrange("p (c r) -> p c r", c=4))
        link(i)
        link(v.tensor_copy(mprev, PS[:, 6, 0:36].rearrange("p (h c) -> p h c", h=H)))
        tell(v.tensor_copy(gs, PS[:, 6, 64:64 + 96].rearrange("p (h g b) -> p h g b", h=H, g=3)), s.gates_read)
        chunk_keep = cacc
        link(v.memset(chunk_keep, 1.0))
        link(v.memset(chunk_keep[:, 0:NP_:P], 0.0))
        for j in range(H):
            link(v.tensor_tensor_scan(G[:, j, 0:NP_], chunk_keep, G[:, j, 0:NP_], 0.0, ALU.mult, ALU.add))

        for ct in range(8):
            r = raw[ct % 2]
            dve.wait_ge(s.proj_read, last_piece(8 + ct))
            link(v.tensor_scalar(cacc, r[:, 0:NP_], cw[:, ct, 0:1], cb[:, ct:ct + 1], ALU.mult, ALU.add))
            link(v.scalar_tensor_tensor(cacc, r[:, 1:1 + NP_], cw[:, ct, 1:2], cacc, ALU.mult, ALU.add))
            link(v.scalar_tensor_tensor(cacc, r[:, 2:2 + NP_], cw[:, ct, 2:3], cacc, ALU.mult, ALU.add))
            link(v.tensor_copy(raw_s[:, ct], r[:, 3 + NP_:3 + NT]))
            link(v.tensor_copy(raw_p3[:, ct], r[:, NP_:NP_ + 3]))
            tell(v.scalar_tensor_tensor(CC[:, ct], r[:, 3:3 + NP_], cw[:, ct, 3:4], cacc, ALU.mult, ALU.add), s.conv_done)
        cs = conv_ps.rearrange("p (c b) -> p c b", c=8)
        tmp = cacc[:, 0:64].rearrange("p (c b) -> p c b", c=8)
        tap = lambda j: cw[:, :, j:j + 1].to_broadcast([P, 8, NS])
        link(v.tensor_tensor(cs, sconv[:, :, 0], tap(0), ALU.mult))
        link(v.tensor_tensor(cs, cs, cb.unsqueeze(2).to_broadcast([P, 8, NS]), ALU.add))
        for j in (1, 2, 3):
            link(v.tensor_tensor(tmp, raw_s if j == 3 else sconv[:, :, j], tap(j), ALU.mult))
            i = v.tensor_tensor(cs, cs, tmp, ALU.add)
            if j < 3:
                link(i)
        tell(i, s.conv_done)

        dve.wait_ge(s.conv_done, 9)
        for n in range(2):
            link(v.memset(vext[n][:, :, P:], 1.0))
        heads = lambda ap: ap.rearrange("p (h t) -> p h t", h=H)
        for c in range(NCH):
            tok = slice(c * P, (c + 1) * P)
            dve.wait_ge(s.decay_b, c + 1)
            for h in range(H):
                i = v.tensor_scalar(dmat[:, h], PS[:, 2, h * P:(h + 1) * P], gcol[:, c, h:h + 1], 0.0, ALU.add, ALU.min)
            tell(i, s.d_arg)
            tell(v.tensor_tensor(qd, heads(PS[:, 2, :]), mprev[:, :, c:c + 1].to_broadcast([P, H, P]), ALU.add), s.q_arg)
            dve.wait_ge(s.q_exp, c + 1)
            dve.wait_ge(s.qk_silu, 8)
            link(v.tensor_copy(dend, qd[:, :, P - 1]))
            tell(v.tensor_tensor(qd, qd, CC[:, 0:H, tok], ALU.mult), s.qd_ready)
            dve.wait_ge(s.scores, c + 1)
            dve.wait_ge(s.d_masked, c + 1)
            tell(v.scalar_tensor_tensor(dmat, heads(PS[:, 3, :]), KSCALE, dmat, ALU.mult, ALU.mult), s.s_ready)
            dve.wait_ge(s.v_proj, c + 1)
            if c == 0:
                dve.wait_ge(s.bias_in, 16)
            tell(v.tensor_tensor(vext[c % 2][:, :, 0:P], heads(PS[:, 0, :]), heads(bias[:, 0:512]), ALU.add), s.v_ready)
            dve.wait_ge(s.k_turned, c + 1)
            for h in range(H):
                i = v.tensor_scalar(kw[:, h], PS[:, 6, h * P:(h + 1) * P], gcol[:, c, 32 + h:33 + h], KSCALE, ALU.mult, ALU.mult)
            tell(i, s.kw_ready)
            dve.wait_ge(s.o_proj, c + 1)
            tell(v.tensor_tensor(ogate, heads(PS[:, 1, :]), heads(bias[:, 512:1024]), ALU.add), s.o_biased)
            dve.wait_ge(s.o_exp, c + 1)
            link(v.tensor_scalar(ogate, ogate, 1.0, None, ALU.add))
            link(v.reciprocal(ogate, ogate))
            dve.wait_ge(s.cupd, c + 1)
            for h in range(H):
                ps = PS[:, 6 + h // 2, (h % 2) * DV1:(h % 2 + 1) * DV1]
                if c == 0:
                    i = v.tensor_copy(Cst[:, h], ps)
                else:
                    i = v.scalar_tensor_tensor(Cst[:, h], Cst[:, h], dend[:, h:h + 1], ps, ALU.mult, ALU.add)
            tell(i, s.c_ready)
            dve.wait_ge(s.num, c + 1)
            qn = PS[:, 4:6, 0:2 * DV1].rearrange("p b (h v) -> p b h v", h=2)[:, :, :, P]
            two = lambda ap: ap.rearrange("p (b h) -> p b h", b=2)
            link(v.scalar_tensor_tensor(two(den), qn, -1.0, two(gcol[:, c, 64:68]), ALU.mult, ALU.max))
            link(v.tensor_tensor(two(den), qn, two(den), ALU.max))
            link(v.reciprocal(rec, den))
            for h in range(H):
                i = v.scalar_tensor_tensor(hbuf[:, h], PS[:, 4 + h // 2, (h % 2) * DV1:(h % 2) * DV1 + P], rec[:, h:h + 1],
                                           ogate[:, h], ALU.mult, ALU.mult)
            tell(i, s.h_ready)
            dve.wait_ge(s.h_sq, c + 1)
            tell(v.tensor_reduce(ssq, sq, X, ALU.add), s.ssq_ready)
            dve.wait_ge(s.rstd_ready, c + 1)
            tell(v.tensor_tensor(hbuf, hbuf, rstd.unsqueeze(2).to_broadcast([P, H, P]), ALU.mult), s.hn_ready)
        vector_rest(dve, link, tell)


def layouts(i):
    a = {k: np.asarray(v) for k, v in i.items()}
    x = np.concatenate([a["x_prompt"].reshape(NP_, D), a["x_sample"].reshape(NS, D)])
    w, b = a["w_in"][0], a["b_in"][0]
    wg = np.zeros((D, 64), np.float32)
    wg[:, 0:H], wg[:, 32:32 + H] = w[:, 2048:2048 + H], w[:, 2048 + H:COL_HG]
    bg = np.zeros((64, 1), np.float32)
    bg[0:H, 0], bg[32:32 + H, 0] = b[2048:2048 + H], b[2048 + H:COL_HG]
    cols = [COL_Q, COL_K, COL_V, COL_O, COL_HQ, COL_HF, COL_HI, COL_GT]
    cm = lambda v: v.reshape(-1, P).T
    m0 = np.zeros((P, NS), np.float32)
    m0[0:H] = a["state_ml_m"][0].T
    b_gates = np.zeros((P, 1), np.float32)
    b_gates[0:64] = bg
    params = [a["conv_w"][0].reshape(4, 8, P).transpose(2, 1, 0), a["conv_b"][0].reshape(8, P).T,
              np.concatenate([cm(b[c:c + 512]) for c in cols], 1), b_gates,
              np.concatenate([cm(a["ml_norm_g"][0]), cm(a["hg_norm_g"][0])], 1),
              a["state_conv"][0].reshape(NS, 3, 8, P).transpose(3, 2, 1, 0), m0]
    return {
        "consts": CONST_F, "masks": CONST_M,
        "xT": x.T.reshape(P, KD, NT),
        "x": x,
        "w_in": w,
        "wg": wg.reshape(P, KD, 64),
        "params": np.concatenate([v.reshape(P, -1) for v in params], 1),
        "b_row": np.concatenate([b[c:c + 512] for c in (COL_V, COL_O, COL_HI, COL_GT)])[None],
        "C0": a["state_ml_C"][0].transpose(2, 1, 0, 3),
        "n0": a["state_ml_n"][0].transpose(2, 1, 0),
        "S0": a["state_hg_S"][0].transpose(2, 1, 0, 3),
        "w_out": a["w_out"][0],
        "ln1": np.concatenate([a["ln1_g"], a["ln1_b"]]),
        "ln2": np.concatenate([a["ln2_g"], a["ln2_b"]]),
        "w_r": np.concatenate([a["w_router_group"][0], a["w_router_expert"][0]], 1).reshape(KD, P, NG + NE).transpose(1, 0, 2),
        "b_r": np.concatenate([a["b_router_group"], a["b_router_expert"]], 1),
        "w_gate": a["w_gate"][0], "w_up": a["w_up"][0], "w_down": a["w_down"][0],
    }


_OUTS = {
    "y": (NT, D), "conv_p": (P, 8, 3), "C_p": (P, H, DV1), "m_p": (H, 1), "S_p": (P, H, P),
    "conv_s": (P, 8, 3, NS), "C_s": (P, H, NS, P), "n_s": (P, H, NS), "m_s": (H, NS), "S_s": (P, H, NS, P),
}


def kernel(**inputs):
    import concourse.bacc as _bacc
    from concourse.bass_utils import run_bass_kernel_spmd as _run

    nc = _bacc.Bacc("TRN2", target_bir_lowering=False, num_devices=1)
    arrays, args = {}, {}
    for name, a in layouts(inputs).items():
        a = np.ascontiguousarray(a)
        arrays[f"in_{name}"] = a
        args[name] = nc.dram_tensor(f"in_{name}", a.shape, mybir.dt.from_np(a.dtype), kind="ExternalInput").ap()
    for name, shape in _OUTS.items():
        args["out_" + name] = nc.dram_tensor(f"out_{name}", shape, F32, kind="ExternalOutput").ap()
    program(nc, args)
    r = _run(nc, [arrays], core_ids=[0]).results[0]
    o = {name: r[f"out_{name}"] for name in _OUTS}
    return (
        o["y"][:NP_].reshape(1, NP_, D), o["y"][NP_:].reshape(NS, 1, D),
        o["conv_p"].transpose(2, 1, 0).reshape(1, 1, 3, D),
        o["C_p"][:, :, :P].transpose(1, 0, 2)[None, None], o["C_p"][:, :, P].T[None, None], o["m_p"].T[None], o["S_p"].transpose(1, 0, 2)[None, None],
        o["conv_s"].transpose(3, 2, 1, 0).reshape(1, NS, 3, D),
        o["C_s"].transpose(2, 1, 0, 3)[None], o["n_s"].transpose(2, 1, 0)[None], o["m_s"].T[None],
        o["S_s"].transpose(2, 1, 0, 3)[None],
    )
```
